# Optimizing a Trainium2 kernel written in Bass

```python
import jax, jax.numpy as jnp
from jax import lax
import numpy as np

D_MODEL = 1024
BATCH = 1
SEQ = 512
DEPTH = 2

GM_WIDTH = 512
GM_GROUPS = 4
GM_GROUP_DIM = GM_WIDTH // GM_GROUPS
GM_CHUNK = 128
N_Q_HEADS = 8
N_KV_HEADS = 2
HEAD_DIM = 64
ATT_WIDTH = N_Q_HEADS * HEAD_DIM
KV_WIDTH = N_KV_HEADS * HEAD_DIM
WINDOW = 128
ATTN_BLOCK = 128
ROPE_THETA = 10000.0
MAX_POS_OFFSET = 1024
MASK_VALUE = -1e30
HG_HEADS = 4
HG_EXPAND = 128
HG_HEAD_V = 128
HG_KEY_WIDTH = HG_HEADS * HG_EXPAND
HG_WIDTH = HG_HEADS * HG_HEAD_V
HG_CHUNK = 64
HG_MIN_FORGET = 1e-6
N_BRANCH = 3
D_FF = 2816
CONV_W = 3
EPS = 1e-6

IN_SPLITS = (GM_WIDTH, GM_WIDTH, ATT_WIDTH, KV_WIDTH, KV_WIDTH,
             HG_KEY_WIDTH, HG_KEY_WIDTH, HG_WIDTH, HG_WIDTH, N_BRANCH * D_MODEL)
IN_WIDTH = sum(IN_SPLITS)

kernel_name = "hybrid_gated_parallel_mixer_block"

def rms_norm(x, g):
    xf = x.astype(jnp.float32)
    y = xf * lax.rsqrt(jnp.mean(xf * xf, axis=-1, keepdims=True) + EPS)
    return (y * g.astype(jnp.float32)).astype(x.dtype)

def layer_norm(x, g, b):
    xf = x.astype(jnp.float32)
    mu = jnp.mean(xf, axis=-1, keepdims=True)
    var = jnp.mean(jnp.square(xf - mu), axis=-1, keepdims=True)
    y = (xf - mu) * lax.rsqrt(var + EPS)
    return (y * g.astype(jnp.float32) + b.astype(jnp.float32)).astype(x.dtype)

def rope(x, pos):
    half = HEAD_DIM // 2
    inv = ROPE_THETA ** (-jnp.arange(half, dtype=jnp.float32) / half)
    ang = pos.astype(jnp.float32)[..., None] * inv
    cos = jnp.cos(ang)[:, :, None, :]
    sin = jnp.sin(ang)[:, :, None, :]
    xf = x.astype(jnp.float32)
    x1, x2 = xf[..., :half], xf[..., half:]
    return jnp.concatenate([x1 * cos - x2 * sin, x2 * cos + x1 * sin], axis=-1).astype(x.dtype)

def chunked_spatial_gating(u, v, ln_g, ln_b, w_s, b_s):
    B, S, _ = u.shape
    nc = S // GM_CHUNK
    vn = layer_norm(v, ln_g, ln_b).reshape(B, nc, GM_CHUNK, GM_GROUPS, GM_GROUP_DIM)
    causal = jnp.tril(jnp.ones((GM_CHUNK, GM_CHUNK), dtype=bool))
    ws = jnp.where(causal[None], w_s, 0.0).astype(u.dtype)
    s = jnp.einsum('gts,bcsgd->bctgd', ws, vn) + b_s.T.astype(u.dtype)[None, None, :, :, None]
    return u * s.reshape(B, S, GM_WIDTH)

def sliding_window_attention(q, k, v, sinks):
    B, S = q.shape[:2]
    nb = S // ATTN_BLOCK
    G = N_Q_HEADS // N_KV_HEADS
    qb = q.reshape(B, nb, ATTN_BLOCK, N_KV_HEADS, G, HEAD_DIM)

    def with_prev(t):
        tb = t.reshape(B, nb, ATTN_BLOCK, N_KV_HEADS, HEAD_DIM)
        prev = jnp.pad(tb[:, :-1], ((0, 0), (1, 0), (0, 0), (0, 0), (0, 0)))
        return jnp.concatenate([prev, tb], axis=2)

    kk, vv = with_prev(k), with_prev(v)
    scores = jnp.einsum('bnqhgd,bnkhd->bnhgqk', qb, kk).astype(jnp.float32) * (HEAD_DIM ** -0.5)
    qi = jnp.arange(ATTN_BLOCK)[:, None]
    kj = jnp.arange(2 * ATTN_BLOCK)[None, :]
    delta = qi + ATTN_BLOCK - kj
    band = (delta >= 0) & (delta < WINDOW)
    blk = jnp.arange(nb)[:, None, None]
    valid = band[None] & ((blk > 0) | (kj >= ATTN_BLOCK)[None])
    scores = jnp.where(valid[None, :, None, None], scores, MASK_VALUE)
    sink = sinks.astype(jnp.float32).reshape(N_KV_HEADS, G)[None, None, :, :, None, None]
    m = jnp.maximum(jnp.max(scores, axis=-1, keepdims=True), sink)
    p = jnp.exp(scores - m)
    probs = p / (jnp.sum(p, axis=-1, keepdims=True) + jnp.exp(sink - m))
    out = jnp.einsum('bnhgqk,bnkhd->bnqhgd', probs.astype(v.dtype), vv)
    return out.reshape(B, S, ATT_WIDTH)

def hgrn2(q, f_logit, i, g, lb, gnorm):
    B, S, _ = q.shape
    nc = S // HG_CHUNK
    f32 = jnp.float32
    fl = f_logit.astype(f32)
    lbf = lb.astype(f32)
    forget = lbf + (1.0 - lbf) * jax.nn.sigmoid(fl)
    log_f = jnp.log(jnp.maximum(forget, HG_MIN_FORGET))
    k = (1.0 - lbf) * jax.nn.sigmoid(-fl)
    qf = jax.nn.silu(q.astype(f32)) * (HG_EXPAND ** -0.5)
    vf = i.astype(f32)

    def to_chunks(t, d):
        return t.reshape(B, nc, HG_CHUNK, HG_HEADS, d).transpose(1, 0, 2, 3, 4)

    qs, ks, lfs = to_chunks(qf, HG_EXPAND), to_chunks(k, HG_EXPAND), to_chunks(log_f, HG_EXPAND)
    vs = to_chunks(vf, HG_HEAD_V)
    causal = jnp.tril(jnp.ones((HG_CHUNK, HG_CHUNK), dtype=bool))[None, :, :, None, None]

    def step(state, inp):
        qc, kc, vc, lfc = inp
        b = jnp.cumsum(lfc, axis=1)
        o_inter = jnp.einsum('bthk,bhkv->bthv', qc * jnp.exp(b), state)
        diff = jnp.where(causal, b[:, :, None] - b[:, None, :], 0.0)
        decay = jnp.where(causal, jnp.exp(diff), 0.0)
        att = jnp.einsum('bthk,btshk,bshk->bths', qc, decay, kc)
        o = o_inter + jnp.einsum('bths,bshv->bthv', att, vc)
        b_last = b[:, -1]
        new_state = jnp.exp(b_last)[..., None] * state + jnp.einsum(
            'bshk,bshv->bhkv', kc * jnp.exp(b_last[:, None] - b), vc)
        return new_state, o

    s0 = jnp.zeros((B, HG_HEADS, HG_EXPAND, HG_HEAD_V), f32)
    _, o = lax.scan(step, s0, (qs, ks, vs, lfs))
    o = o.transpose(1, 0, 2, 3, 4).reshape(B, S, HG_HEADS, HG_HEAD_V)
    o = rms_norm(o, gnorm) * jax.nn.silu(g.astype(f32)).reshape(B, S, HG_HEADS, HG_HEAD_V)
    return o.reshape(B, S, HG_WIDTH).astype(q.dtype)

def hybrid_mixer(h, pos, lb, w_in, gm_ln_g, gm_ln_b, gm_ws, gm_bs, sinks, hg_gnorm,
                 proj_a, proj_b, proj_c, w_out):
    B, S, _ = h.shape
    proj = h @ w_in
    idx = [int(t) for t in np.cumsum(IN_SPLITS)[:-1]]
    gu, gv, aq, ak, av, hq, hf, hi, hg, gate_logits = jnp.split(proj, idx, axis=-1)
    y_a = chunked_spatial_gating(jax.nn.gelu(gu), jax.nn.gelu(gv), gm_ln_g, gm_ln_b, gm_ws, gm_bs)
    q = rope(aq.reshape(B, S, N_Q_HEADS, HEAD_DIM), pos)
    k = rope(ak.reshape(B, S, N_KV_HEADS, HEAD_DIM), pos)
    v = av.reshape(B, S, N_KV_HEADS, HEAD_DIM)
    y_b = sliding_window_attention(q, k, v, sinks)
    y_c = hgrn2(hq, hf, hi, hg, lb, hg_gnorm)
    gates = jax.nn.sigmoid(gate_logits.astype(jnp.float32)).astype(h.dtype).reshape(B, S, N_BRANCH, D_MODEL)
    merged = (gates[:, :, 0] * (y_a @ proj_a) + gates[:, :, 1] * (y_b @ proj_b)
              + gates[:, :, 2] * (y_c @ proj_c))
    return merged @ w_out

def conv_ffn(h, w1, conv_w, conv_b, w2):
    a = h @ w1
    a = lax.conv_general_dilated(
        a, conv_w[:, None, :].astype(a.dtype), window_strides=(1,), padding=[(CONV_W - 1, 0)],
        dimension_numbers=('NWC', 'WIO', 'NWC'), feature_group_count=2 * D_FF) + conv_b
    gate, val = jnp.split(a, 2, axis=-1)
    return (jax.nn.silu(gate) * val) @ w2

def setup_inputs(seed: int = 0) -> dict:
    key = jax.random.key(seed)
    ks = jax.random.split(key, 32)
    f32 = jnp.float32
    L = DEPTH

    def nrm(k, shape, scale):
        return jax.random.normal(k, shape, f32) * scale

    def gain(k, shape):
        return 1.0 + nrm(k, shape, 0.02)

    offset = jax.random.randint(ks[2], (BATCH, 1), 0, MAX_POS_OFFSET, dtype=jnp.int32)
    return {
        "x": nrm(ks[0], (BATCH, SEQ, D_MODEL), 1.0),
        "c": nrm(ks[1], (BATCH, D_MODEL), 1.0),
        "positions": offset + jnp.arange(SEQ, dtype=jnp.int32)[None, :],
        "ada_w": nrm(ks[3], (L, D_MODEL, 6 * D_MODEL), 0.5 * D_MODEL ** -0.5),
        "ada_b": nrm(ks[4], (L, 6 * D_MODEL), 0.02),
        "norm_mix_pre": gain(ks[5], (L, D_MODEL)),
        "norm_mix_post": gain(ks[6], (L, D_MODEL)),
        "norm_ffn_pre": gain(ks[7], (L, D_MODEL)),
        "norm_ffn_post": gain(ks[8], (L, D_MODEL)),
        "w_in": nrm(ks[9], (L, D_MODEL, IN_WIDTH), D_MODEL ** -0.5),
        "gm_ln_g": gain(ks[10], (L, GM_WIDTH)),
        "gm_ln_b": nrm(ks[11], (L, GM_WIDTH), 0.02),
        "gm_ws": nrm(ks[12], (L, GM_GROUPS, GM_CHUNK, GM_CHUNK), GM_CHUNK ** -0.5),
        "gm_bs": gain(ks[13], (L, GM_GROUPS, GM_CHUNK)),
        "attn_sinks": nrm(ks[14], (L, N_Q_HEADS), 0.5),
        "hg_lb_logits": nrm(ks[15], (L, HG_KEY_WIDTH), 0.5),
        "hg_gnorm": gain(ks[16], (L, HG_HEAD_V)),
        "proj_a": nrm(ks[17], (L, GM_WIDTH, D_MODEL), GM_WIDTH ** -0.5),
        "proj_b": nrm(ks[18], (L, ATT_WIDTH, D_MODEL), ATT_WIDTH ** -0.5),
        "proj_c": nrm(ks[19], (L, HG_WIDTH, D_MODEL), HG_WIDTH ** -0.5),
        "w_out": nrm(ks[20], (L, D_MODEL, D_MODEL), D_MODEL ** -0.5),
        "ffn_w1": nrm(ks[21], (L, D_MODEL, 2 * D_FF), D_MODEL ** -0.5),
        "ffn_conv_w": nrm(ks[22], (L, CONV_W, 2 * D_FF), CONV_W ** -0.5),
        "ffn_conv_b": nrm(ks[23], (L, 2 * D_FF), 0.02),
        "ffn_w2": nrm(ks[24], (L, D_FF, D_MODEL), D_FF ** -0.5),
    }

def reference(x, c, positions, ada_w, ada_b, norm_mix_pre, norm_mix_post, norm_ffn_pre, norm_ffn_post,
              w_in, gm_ln_g, gm_ln_b, gm_ws, gm_bs, attn_sinks, hg_lb_logits, hg_gnorm,
              proj_a, proj_b, proj_c, w_out, ffn_w1, ffn_conv_w, ffn_conv_b, ffn_w2):
    p_lb = jax.nn.softmax(hg_lb_logits.astype(jnp.float32), axis=0)
    lb_all = jnp.cumsum(p_lb, axis=0) - p_lb[0]
    c_act = jax.nn.silu(c)
    for l in range(DEPTH):
        mod = c_act @ ada_w[l] + ada_b[l]
        sh1, sc1, g1, sh2, sc2, g2 = jnp.split(mod, 6, axis=-1)
        h = rms_norm(x, norm_mix_pre[l]) * (1.0 + sc1[:, None]) + sh1[:, None]
        y = hybrid_mixer(h, positions, lb_all[l], w_in[l], gm_ln_g[l], gm_ln_b[l], gm_ws[l], gm_bs[l],
                         attn_sinks[l], hg_gnorm[l], proj_a[l], proj_b[l], proj_c[l], w_out[l])
        x = x + g1[:, None] * rms_norm(y, norm_mix_post[l])
        h = rms_norm(x, norm_ffn_pre[l]) * (1.0 + sc2[:, None]) + sh2[:, None]
        y = conv_ffn(h, ffn_w1[l], ffn_conv_w[l], ffn_conv_b[l], ffn_w2[l])
        x = x + g2[:, None] * rms_norm(y, norm_ffn_post[l])
    return x


_drawn_inputs = setup_inputs


def setup_inputs(seed=0):
    import zlib

    import numpy as np

    out = dict(_drawn_inputs(seed))
    spreads = {}
    factors = {'norm_mix_pre': 5.095,
     'norm_mix_post': 6.255,
     'norm_ffn_pre': 5.022,
     'norm_ffn_post': 7.106,
     'gm_ln_g': 89.958,
     'gm_ln_b': 88.25,
     'gm_bs': 22.13,
     'attn_sinks': 200.0,
     'hg_lb_logits': 21.822,
     'hg_gnorm': 52.405,
     'ffn_conv_b': 5.388}
    for name, (base, spread) in spreads.items():
        noise = np.random.default_rng([zlib.crc32(name.encode()), seed]).standard_normal(out[name].shape)
        drawn = base * np.exp(spread * noise) if base else spread * noise
        out[name] = __import__('jax').numpy.asarray(drawn.astype(out[name].dtype))
    for name, factor in factors.items():
        out[name] = (out[name] * factor).astype(out[name].dtype)
    return out
```

```python
from contextlib import ExitStack

import concourse.bass as bass
from concourse import mybir

ALU = mybir.AluOpType
ACT = mybir.ActivationFunctionType
F32 = mybir.dt.float32
F32R = mybir.dt.float32r
I32 = mybir.dt.int32
U32 = mybir.dt.uint32
AX_X = mybir.AxisListType.X

P = 128
D = 1024
S = 512
L = 2
KD = D // P
NT = S // P
EPS = 1e-6
FF = 2816
NPAIR = FF // P
HEADS = 4
CH = 64
NCH = S // CH
SUB = 8
NSUB = CH // SUB
MID = SUB // 2 - 1
MIN_FORGET = 1e-6
HG_SCALE = 128 ** -0.5
AT_SCALE = 64 ** -0.5
MAGIC = 12582912.0
TWO_PI = 6.283185307179586
TWO_PI_HI = 6.28125
TWO_PI_LO = TWO_PI - TWO_PI_HI
PI_SAFE = 3.1415925

C_ADA, C_NMPRE, C_NMPOST, C_NFPRE, C_NFPOST, C_LB, C_GN, C_CONV = 0, 48, 56, 64, 72, 80, 84, 85
NCOL = C_CONV + NPAIR * 2 * 4
K_ID, K_ONE, K_AM, K_HM, K_INV, K_SGN, K_EPS = 0, 128, 256, 512, 640, 641, 642
NCONST = 643
R_G, R_B, R_BS, R_SINK = 0, 512, 1024, 1536
NROW = 1544

FRONT = ["hf", "hf", "hq", "hq", "hi", "hi", "gv", "gv", "gu", "gu", "kv", "aq", "aq", "hg", "hg"]
NFRONT = len(FRONT)
NMP = 4


def weight_stream():
    out = [("ada", 0, j) for j in range(8)]
    for l in range(L):
        out += [("win", l, b) for b in range(NFRONT)]
        for mp in range(NMP):
            out += [("win", l, NFRONT + 3 * mp + br) for br in range(3)]
            out += [("ada", l, 8 + 3 * mp + j) for j in range(3)]
            out += [("proj", l, 2 * mp), ("proj", l, 2 * mp + 1)]
        out += [("wout", l, m) for m in range(4)]
        out += [("ada", l, j) for j in range(20, 24)]
        out += [("w1", l, p) for p in range(NPAIR)]
        out += [("w2", l, i) for i in range(12)]
        if l + 1 < L:
            out += [("ada", l + 1, j) for j in range(8)]
    return out


TILES = []
for name in ("hf", "hq", "hi", "gv", "gu", "kv", "aq", "hg"):
    TILES += [(name, i) for i in range(2 if name == "kv" else 4)]
for mp in range(NMP):
    TILES += [("gate", 6 * mp + i) for i in range(6)] + [("proj", 6 * mp + i) for i in range(6)]
TILES += [("wout", i) for i in range(8)] + [("w1", i) for i in range(2 * NPAIR)] + [("w2", i) for i in range(8)]
NTILE = len(TILES)
TILE_AT = {t: i for i, t in enumerate(TILES)}

SPLITS = [("h1", k) for k in range(8)] + [("ya", g) for g in range(4)] + [("yc", h) for h in range(4)]
SPLITS += [("mg", m) for m in range(8)] + [("h2", k) for k in range(8)] + [("ff", p) for p in range(NPAIR)]
NSPLIT = len(SPLITS)
SPLIT_AT = {t: i for i, t in enumerate(SPLITS)}


def tile(l, name, i):
    return l * NTILE + TILE_AT[(name, i)]


def split(l, name, i):
    return l * NSPLIT + SPLIT_AT[(name, i)]


def trunk(nc, xT_d, c_d, pos_d, cols_d, rows_d, const_d, ws_d, ada_d, win_d, proj_d, wout_d, w1_d, w2_d, out_d):
    stream = weight_stream()
    at = {b: i for i, b in enumerate(stream)}
    kinds = [b for b in stream if b[0] != "ada"]
    split_no = {b: i for i, b in enumerate(kinds)}
    adas = [b for b in stream if b[0] == "ada"]
    ada_no = {b: i for i, b in enumerate(adas)}

    ctx = ExitStack()
    with ctx:
        def sem(name):
            return ctx.enter_context(nc.semaphore(name))

        KB = 1024
        SLAB = 212832
        start = (nc.sbuf_base + 63) // 64 * 64
        ctx.enter_context(nc.sbuf_tensor("slab", [P, SLAB // 4], F32))

        cursor = [start]

        def place(name, shape, dt, where=None):
            if where is None:
                where = cursor[0]
                n = 4
                for s in shape[1:]:
                    n *= s
                cursor[0] += (n + 31) // 32 * 32
                assert cursor[0] <= start + SLAB, (name, cursor[0] - start)
            return nc.alloc_sbuf_tensor_at(name, shape, dt, offset=where)

        x = place("x", [P, KD, S], F32)
        H0 = cursor[0]
        hh = place("hh", [P, KD, S], F32R)
        hl = place("hl", [P, KD, S], F32R)
        y = place("y", [P, KD, S], F32, H0)
        stage = place("stage", [P, 2, 2048], F32)
        whi = place("whi", [P, 2, 2048], F32R)
        wlo = place("wlo", [P, 2, 2048], F32R)
        R0 = cursor[0]
        cursor[0] += 100 * KB

        def at_kb(name, shape, dt, kb):
            return place(name, shape, dt, R0 + int(kb * KB))

        gut = at_kb("gut", [P, 4, S], F32, 0)
        yah = at_kb("yah", [P, 4, S], F32R, 0)
        gvt = at_kb("gvt", [P, NT, 512], F32, 8)
        yal = at_kb("yal", [P, 4, S], F32R, 8)
        hqs = at_kb("hqs", [P, HEADS, S], F32, 16)
        ych = at_kb("ych", [P, 4, S], F32R, 16)
        hk = at_kb("hk", [P, HEADS, S], F32, 24)
        ycl = at_kb("ycl", [P, 4, S], F32R, 24)
        aqr = at_kb("aqr", [P, 4, S], F32, 32)
        ybh = at_kb("ybh", [P, 4, S], F32R, 32)
        itok = at_kb("itok", [P, NT, 512], F32, 40)
        ybl = at_kb("ybl", [P, 4, S], F32R, 40)
        bb = at_kb("bb", [P, HEADS, S], F32, 48)
        hgs = at_kb("hgs", [P, HEADS, S], F32, 56)
        kd = at_kb("kd", [P, 2, S], F32, 64)
        vt = at_kb("vt", [P, NT, 128], F32, 68)
        khT = at_kb("khT", [P, NT, 128], F32, 70)
        states = at_kb("states", [P, NCH - 1, 128], F32, 72)
        asb = at_kb("asb", [P, S], F32, 75.5)
        mgh = at_kb("mgh", [P, 8, S], F32R, 48)
        mgl = at_kb("mgl", [P, 8, S], F32R, 64)
        kt = at_kb("kt", [P, 4, NCH, CH], F32, 80)
        rows = at_kb("rows", [P, NROW], F32, 80)
        pm = at_kb("pm", [P, 4, 256], F32, 80)
        pts = at_kb("pts", [P, 2, 4, 128], F32, 84)
        gates = at_kb("gates", [P, 6, S], F32, 80)
        tmp = [at_kb(f"tmp{i}", [P, S], F32, 88 + 2 * i) for i in range(4)]
        sq = [at_kb(f"sq{i}", [P, S], F32, 96 + 2 * i) for i in range(2)]
        acth = at_kb("acth", [P, NPAIR, S], F32R, 0)
        actl = at_kb("actl", [P, NPAIR, S], F32R, 44)

        cosb = place("cosb", [P, S], F32)
        sinb = place("sinb", [P, S], F32)
        const = place("const", [P, NCONST], F32)
        cols = place("cols", [P, L, NCOL], F32)
        ws = place("ws", [P, 4, 128], F32)
        mod = place("mod", [P, 48], F32)
        ccol = place("ccol", [P, KD], F32)
        cact = place("cact", [P, KD], F32)
        cA = place("cA", [P, 2, KD], F32)
        cG = place("cG", [P, 2, KD], F32)
        lbs = place("lbs", [P, L, 2, HEADS], F32)
        lbt = place("lbt", [P, 4, HEADS], F32)
        std = place("std", [P, 16], F32)
        rstd = place("rstd", [P, 16], F32)
        bn = place("bn", [P, NT, 6], F32)
        mv = place("mv", [P, NT, 2], F32)
        vstd = place("vstd", [P, 2, NT], F32)
        sink = place("sink", [P, 8], F32)
        amx = place("amx", [P, 3, 4], F32)
        ars = place("ars", [P, 3, 4], F32)
        elast = place("elast", [P, NCH], F32)

        ident = const[:, K_ID:K_ID + P]
        ones = const[:, K_ONE:K_ONE + P]
        eps = const[:, K_EPS:K_EPS + 1]

        acc = [ctx.enter_context(nc.psum_tensor(f"acc{i}", [P, S], F32)) for i in range(4)]
        b4, b5, b6, b7 = [ctx.enter_context(nc.psum_tensor(f"bank{i}", [P, S], F32)) for i in range(4, 8)]
        small = [b4, b5, b6, b7]

        const_in = sem("const_in"); x_in = sem("x_in"); pos_in = sem("pos_in"); rows_in = sem("rows_in")
        ws_in = sem("ws_in"); stored = sem("stored")
        landed = [sem(f"landed{i}") for i in range(2)]
        whi_ready = sem("whi_ready"); wlo_ready = sem("wlo_ready"); third_used = sem("third_used")
        ada_used = sem("ada_used")
        tile_done = sem("tile_done"); acc_free = [sem(f"acc_free{i}") for i in range(4)]
        f_ready = sem("f_ready"); hi_ready = sem("hi_ready"); lo_ready = sem("lo_ready")
        x_ready = sem("x_ready"); sq_ready = sem("sq_ready"); ss_done = sem("ss_done")
        std_ready = sem("std_ready"); diag_ready = sem("diag_ready"); bc_ready = sem("bc_ready")
       
        cact_ready = sem("cact_ready"); mod_read = sem("mod_read")
        ang_ready = sem("ang_ready"); trig_ready = sem("trig_ready"); lb_a = sem("lb_a"); lb_b = sem("lb_b")
        dve_own = sem("dve_own"); act_own = sem("act_own");
       
       
        kd_ready = sem("kd_ready");
        ws_ready = sem("ws_ready"); vvar = sem("vvar"); vsd = sem("vsd"); vn_ready = sem("vn_ready")
        sgu_done = sem("sgu_done");
        forget_ready = sem("forget_ready"); log_ready = sem("log_ready"); diff_ready = sem("diff_ready")
        exp_ready = sem("exp_ready"); kdiff = sem("kdiff"); kexp = sem("kexp"); kt_ready = sem("kt_ready")
        qk_ready = sem("qk_ready"); khT_done = sem("khT_done"); khT_copied = sem("khT_copied")
        ds_done = sem("ds_done"); state_ready = sem("state_ready"); a_done = sem("a_done")
        masked = sem("masked"); o_done = sem("o_done"); o_copied = sem("o_copied");
        osq_ready = sem("osq_ready"); oss_done = sem("oss_done"); ostd = sem("ostd"); odiag = sem("odiag")
        obc = sem("obc");
        qk_done = sem("qk_done"); max_ready = sem("max_ready"); p_exp = sem("p_exp"); p_ready = sem("p_ready")
        pt_done = sem("pt_done"); pt_copied_a = sem("pt_copied_a"); pt_copied_v = sem("pt_copied_v")
        pv_done = sem("pv_done"); ybh_ready = sem("ybh_ready"); yb_ready = sem("yb_ready")
        conv0 = sem("conv0"); silu_done = sem("silu_done")

        last_tile = {}
        for l in range(L):
            for b in range(NFRONT):
                last_tile[("win", l, b)] = tile(l, FRONT[b], 1 if b == 0 or FRONT[b - 1] != FRONT[b] else 3)
            for b in range(3 * NMP):
                last_tile[("win", l, NFRONT + b)] = tile(l, "gate", 2 * b + 1)
            for m in range(8):
                last_tile[("proj", l, m)] = tile(l, "proj", 3 * m + 2)
            for m in range(4):
                last_tile[("wout", l, m)] = tile(l, "wout", 2 * m + 1)
                last_tile[("w2", l, 3 * m + 2)] = tile(l, "w2", 2 * m + 1)
            for p in range(NPAIR):
                last_tile[("w1", l, p)] = tile(l, "w1", 2 * p + 1)

        def block_is_used(eng, b):
            if b in last_tile:
                eng.wait_ge(tile_done, last_tile[b] + 1)
            else:
                eng.wait_ge(third_used, 8 * b[1] + 2 * (b[2] // 3) + b[2] % 3 + 1)

        block = ctx.enter_context(nc.Block())

        def evacuated(eng, t):
            eng.wait_ge(acc_free[t % 4], t // 4 + 1)

        def block_src(kind, l, i):
            if kind == "ada":
                return ada_d[l, i], 2048
            if kind == "win":
                return win_d[l, i], 2048
            if kind == "proj":
                return proj_d[l, i], 1536
            if kind == "wout":
                return wout_d[l, i], 2048
            if kind == "w1":
                return w1_d[l, i], 2048
            k0 = 8 * (i % 3)
            n = min(8, NPAIR - k0) * 256
            return w2_d[l, i // 3, :, k0 * 256:k0 * 256 + n], n

        def block_len(b):
            return block_src(*b)[1]

        def modcols(part):
            return mod[:, 8 * part:8 * part + 8]

        @block.sync
        def _(sp):
            sp.dma_start(const[:, :], const_d).then_inc(const_in, 16)
            sp.dma_start(ccol[:, :], c_d).then_inc(const_in, 16)
            sp.dma_start(cols[:, :, :], cols_d).then_inc(const_in, 16)
            sp.dma_start(x[:, :, :], xT_d).then_inc(x_in, 16)
            for i, b in enumerate(stream):
                if i >= 2:
                    old = stream[i - 2]
                    if old[0] == "ada":
                        sp.wait_ge(ada_used, ada_no[old] + 1)
                    else:
                        sp.wait_ge(wlo_ready, split_no[old] + 1)
                src, n = block_src(*b)
                sp.dma_start(stage[:, i % 2, 0:n], src).then_inc(landed[i % 2], 16)
            for k in range(KD):
                sp.wait_ge(x_ready, 16 * L - 8 + k + 1)
                sp.dma_start(out_d[:, k, :], x[:, k, :]).then_inc(stored, 16)
            sp.wait_ge(stored, 16 * KD)

        @block.gpsimd
        def _(pool):
            pool.dma_start(tmp[3][:, :].bitcast(I32), pos_d.partition_broadcast(P)).then_inc(pos_in, 16)
            def layer_rows(l):
                if l:
                    pool.wait_ge(lo_ready, split(l - 1, "ff", NPAIR - 1) + 1)
                    pool.wait_ge(tile_done, tile(l - 1, "w2", 7) + 1)
                pool.dma_start(rows[:, :], rows_d[l].partition_broadcast(P)).then_inc(rows_in, 16)
                pool.dma_start(ws[:, :, :], ws_d[l]).then_inc(ws_in, 16)
                pool.wait_ge(ws_in, 16 * (l + 1))
                nc.gpsimd.affine_select(out=ws[:, :, :], in_=ws[:, :, :], compare_op=ALU.is_ge, fill=0.0, base=0,
                                        pattern=[[0, 4], [1, 128]], channel_multiplier=-1).then_inc(ws_ready, 1)
            layer_rows(0)
            for i, b in enumerate(kinds):
                n = block_len(b)
                slot = at[b] % 2
                pool.wait_ge(whi_ready, i + 1)
                if i >= 2:
                    block_is_used(pool, kinds[i - 2])
                nc.gpsimd.tensor_tensor(wlo[:, i % 2, 0:n], stage[:, slot, 0:n], whi[:, i % 2, 0:n].bitcast(F32),
                                        ALU.subtract).then_inc(wlo_ready, 1)
                if b == ("w2", b[1], 11) and b[1] + 1 < L:
                    layer_rows(b[1] + 1)

        @block.scalar
        def _(act):
            A = nc.scalar.activation
            own = [0]
            done = [0]

            def chain(ins):
                ins.then_inc(act_own, 1)
                own[0] += 1

            def sync():
                act.wait_ge(act_own, own[0])

            def weights(upto):
                while done[0] <= min(upto, len(kinds) - 1):
                    i = done[0]
                    b = kinds[i]
                    n = block_len(b)
                    slot = at[b] % 2
                    act.wait_ge(landed[slot], 16 * (at[b] // 2 + 1))
                    if i >= 2:
                        block_is_used(act, kinds[i - 2])
                    A(whi[:, i % 2, 0:n], stage[:, slot, 0:n], ACT.Copy).then_inc(whi_ready, 1)
                    done[0] += 1

            def squares(n, k, src):
                if 8 * n + k >= 2:
                    act.wait_ge(ss_done, 8 * n + k - 1)
                A(sq[k % 2][:, :], src, ACT.Square).then_inc(sq_ready, 1)

            def deviation(n):
                act.wait_ge(ss_done, 8 * n + 8)
                A(std[:, 0:NT], b6[:, 0:NT], ACT.Sqrt, bias=eps, scale=1.0 / D).then_inc(std_ready, 1)

            def pre_norm(l, which):
                n = 4 * l + 2 * which
                for k in range(KD):
                    if n:
                        act.wait_ge(x_ready, 8 * (2 * l + which - 1) + k + 1)
                    elif k == 0:
                        act.wait_ge(x_in, 16)
                    squares(n, k, x[:, k, :])
                weights(split_no[("w1", l, 0) if which else ("win", l, 0)])
                deviation(n)
                name = "h2" if which else "h1"
                shift = modcols(3 if which else 0)
                for k in range(KD):
                    act.wait_ge(f_ready, split(l, name, k) + 1)
                    A(hh[:, k, :], tmp[k % 2][:, :], ACT.Identity, bias=shift[:, k:k + 1]).then_inc(hi_ready, 1)

            act.wait_ge(const_in, 48)
            A(cact[:, :], ccol[:, :], ACT.Silu).then_inc(cact_ready, 1)
            act.wait_ge(lb_a, 1)
            A(lbt[:, 0:2, :], lbt[:, 0:2, :], ACT.Exp).then_inc(lb_b, 1)
            act.wait_ge(ang_ready, 1)
            A(cosb[:, :], tmp[0][:, :], ACT.Sin).then_inc(trig_ready, 1)
            A(sinb[:, :], tmp[1][:, :], ACT.Sin).then_inc(trig_ready, 1)

            for l in range(L):
                sb0 = split_no[("win", l, 0)]
                pre_norm(l, 0)
                for b in range(NFRONT):
                    weights(sb0 + b + 1)
                    name = FRONT[b]
                    first = b == 0 or FRONT[b - 1] != name
                    for j in range(2):
                        i = j if first else 2 + j
                        t = tile(l, name, i)
                        if name == "aq" or (name == "kv" and j == 0):
                            continue
                        act.wait_ge(tile_done, t + 1)
                        a = acc[t % 4]
                        if name == "hf":
                            chain(A(bb[:, i, :], a[:, :], ACT.Sigmoid))
                            A(hk[:, i, :], a[:, :], ACT.Sigmoid, scale=-1.0).then_inc(acc_free[t % 4], 1)
                        elif name == "hq":
                            A(hqs[:, i, :], a[:, :], ACT.Silu).then_inc(acc_free[t % 4], 1)
                        elif name == "hg":
                            A(hgs[:, i, :], a[:, :], ACT.Silu).then_inc(acc_free[t % 4], 1)
                        elif name == "gu":
                            A(gut[:, i, :], a[:, :], ACT.Gelu_apprx_tanh).then_inc(acc_free[t % 4], 1)
                        elif name in ("gv", "hi"):
                            half = 0 if first else 1
                            dst = gvt if name == "gv" else itok
                            A(dst[:, 2 * j:2 * j + 2, 256 * half:256 * half + 256],
                              a[:, :].rearrange("p (t n) -> p t n", t=2),
                              ACT.Gelu_apprx_tanh if name == "gv" else ACT.Copy).then_inc(acc_free[t % 4], 1)
                        else:
                            A(vt[:, :, :], a[:, :].rearrange("p (t n) -> p t n", t=NT), ACT.Copy).then_inc(acc_free[t % 4], 1)
                    if name == "kv":
                        evacuated(act, tile(l, "kv", 0))
                        for j in range(2):
                            for o in range(2):
                                A(kd[64 * o:64 * o + 64, j, :], tmp[2][64 * j:64 * j + 64, :], ACT.Copy).then_inc(kd_ready, 1)
                act.wait_ge(vvar, l + 1)
                A(vstd[:, 0, :], mv[:, :, 1], ACT.Sqrt, bias=eps).then_inc(vsd, 1)
                for g in range(4):
                    s = split(l, "ya", g)
                    act.wait_ge(f_ready, s + 1)
                    A(yah[:, g, :], tmp[2 + g % 2][:, :], ACT.Copy).then_inc(hi_ready, 1)
                for h in range(HEADS):
                    q = HEADS * l + h
                    act.wait_ge(forget_ready, q + 1)
                    A(tmp[0][:, :], bb[:, h, :], ACT.Ln).then_inc(log_ready, 1)
                    act.wait_ge(diff_ready, q + 1)
                    chain(A(tmp[0][:, :], tmp[0][:, :], ACT.Exp))
                    chain(A(tmp[1][:, :], bb[:, h, :], ACT.Exp))
                    chain(A(elast[:, :], bb[:, h, :].rearrange("p (c t) -> p c t", t=CH)[:, :, CH - 1], ACT.Exp))
                    A(tmp[2][:, :], tmp[2][:, :], ACT.Exp).then_inc(exp_ready, 1)
                    for i in range(NSUB):
                        if i == 4:
                            act.wait_ge(khT_done, q + 1)
                            A(khT[:, :, :], b6[:, :].rearrange("p (t n) -> p t n", t=NT), ACT.Copy).then_inc(khT_copied, 1)
                        act.wait_ge(kdiff, NSUB * q + i + 1)
                        v = kt[:, i % 4, :, 0:SUB * (i + 1)]
                        A(v, v, ACT.Exp).then_inc(kexp, 1)
                    act.wait_ge(o_done, q + 1)
                    A(bb[:, h, :], b5[:, :], ACT.Copy).then_inc(o_copied, 1)
                for h in range(HEADS):
                    q = HEADS * l + h
                    act.wait_ge(o_copied, q + 1)
                    if h >= 2:
                        act.wait_ge(oss_done, q - 1)
                    A(sq[h % 2][:, :], bb[:, h, :], ACT.Square).then_inc(osq_ready, 1)
                act.wait_ge(oss_done, HEADS * (l + 1))
                A(std[:, :], b6[:, 0:16], ACT.Sqrt, bias=eps, scale=1.0 / 128).then_inc(ostd, 1)
                for h in range(HEADS):
                    act.wait_ge(f_ready, split(l, "yc", h) + 1)
                    A(ych[:, h, :], tmp[h % 2][:, :], ACT.Copy).then_inc(hi_ready, 1)
                for n in range(NT):
                    for j in range(2):
                        a = 8 * l + 2 * n + j
                        w = 256 if n else 128
                        act.wait_ge(max_ready, a + 1)
                        for i in range(4):
                            chain(A(pm[:, i, 0:w], pm[:, i, 0:w], ACT.Exp, bias=amx[:, 1, i:i + 1], accum_out=ars[:, 0, i:i + 1]))
                        A(ars[:, 1, :], amx[:, 2, :], ACT.Exp).then_inc(p_exp, 1)
                        if n:
                            act.wait_ge(pt_done, a + 1)
                            A(pts[:, 0, :, :], b6[:, :].rearrange("p (t n) -> p t n", t=4), ACT.Copy).then_inc(pt_copied_a, 1)
                        act.wait_ge(pv_done, a + 1)
                        A(ybh[:, 2 * j:2 * j + 2, P * n:P * n + P],
                          b6[:, 0:256].rearrange("p (t n) -> p t n", t=2), ACT.Copy).then_inc(ybh_ready, 1)
                for mp in range(NMP):
                    for br in range(3):
                        weights(split_no[("win", l, NFRONT + 3 * mp + br)] + 1)
                        for j in range(2):
                            t = tile(l, "gate", 6 * mp + 2 * br + j)
                            act.wait_ge(tile_done, t + 1)
                            if mp and br == 0 and j == 0:
                                act.wait_ge(f_ready, split(l, "mg", 2 * mp - 1) + 1)
                            A(gates[:, 2 * br + j, :], acc[t % 4][:, :], ACT.Sigmoid).then_inc(acc_free[t % 4], 1)
                    for j in range(2):
                        m = 2 * mp + j
                        weights(split_no[("proj", l, m)] + 1)
                        act.wait_ge(f_ready, split(l, "mg", m) + 1)
                        A(mgh[:, m, :], tmp[2 + m % 2][:, :], ACT.Copy).then_inc(hi_ready, 1)
                n = 4 * l + 1
                for m in range(KD):
                    if m % 2 == 0:
                        weights(split_no[("wout", l, min(m // 2 + 1, 3))])
                    t = tile(l, "wout", m)
                    act.wait_ge(tile_done, t + 1)
                    squares(n, m, acc[t % 4][:, :])
                deviation(n)
                pre_norm(l, 1)
                for p in range(NPAIR):
                    weights(split_no[("w1", l, p)] + 1)
                    tg, tv = tile(l, "w1", 2 * p), tile(l, "w1", 2 * p + 1)
                    for j, t in enumerate((tg, tv)):
                        c0 = C_CONV + 8 * p + 4 * j
                        act.wait_ge(tile_done, t + 1)
                        if p >= 2 and j == 0:
                            act.wait_ge(f_ready, split(l, "ff", p - 2) + 1)
                        A(tmp[2 * (p % 2) + j][:, :], acc[t % 4][:, :], ACT.Identity, bias=cols[:, l, c0 + 3:c0 + 4],
                          scale=cols[:, l, c0 + 2:c0 + 3]).then_inc(conv0, 1)
                    evacuated(act, tv)
                    A(tmp[2 * (p % 2)][:, :], tmp[2 * (p % 2)][:, :], ACT.Silu).then_inc(silu_done, 1)
                    act.wait_ge(f_ready, split(l, "ff", p) + 1)
                    A(acth[:, p, :], tmp[2 * (p % 2)][:, :], ACT.Copy).then_inc(hi_ready, 1)
                n = 4 * l + 3
                for m in range(KD):
                    if m % 2 == 0:
                        weights(split_no[("w2", l, 3 * (m // 2) + 1)])
                        weights(split_no[("w2", l, 3 * (m // 2) + 2)])
                        if m + 2 < KD:
                            weights(split_no[("w2", l, 3 * (m // 2) + 3)])
                    t = tile(l, "w2", m)
                    act.wait_ge(tile_done, t + 1)
                    squares(n, m, acc[t % 4][:, :])
                deviation(n)

        @block.vector
        def _(dve):
            V = nc.vector
            own = [0]

            def chain(ins):
                ins.then_inc(dve_own, 1)
                own[0] += 1

            def sync():
                dve.wait_ge(dve_own, own[0])

            def free(t, ins):
                ins.then_inc(acc_free[t % 4], 1)

            def lo(s, dst, src, hi, shift=None):
                dve.wait_ge(hi_ready, s + 1)
                if shift is None:
                    V.tensor_tensor(dst, src, hi.bitcast(F32), ALU.subtract).then_inc(lo_ready, 1)
                else:
                    V.scalar_tensor_tensor(out=dst, in0=src, scalar=shift, in1=hi.bitcast(F32), op0=ALU.add,
                                           op1=ALU.subtract).then_inc(lo_ready, 1)

            def take_mod(i, c0, c1, l):
                dve.wait_ge(ada_used, ada_no[("ada", l, c1 // 2 - 1)] + 1)
                V.tensor_tensor(mod[:, c0:c1], b7[:, c0:c1], cols[:, l, C_ADA + c0:C_ADA + c1], ALU.add).then_inc(mod_read, 1)
                dve.wait_ge(mod_read, i)

            def broadcast_rstd(n):
                dve.wait_ge(std_ready, n + 1)
                chain(V.reciprocal(rstd[:, 0:NT], std[:, 0:NT]))
                sync()
                V.tensor_tensor(tmp[3][:, :].rearrange("p (t n) -> p t n", t=NT),
                                ident.unsqueeze(1).broadcast_to([P, NT, P]),
                                rstd[:, 0:NT].unsqueeze(2).broadcast_to([P, NT, P]), ALU.mult).then_inc(diag_ready, 1)

            def pre_norm(l, which):
                n = 4 * l + 2 * which
                g0 = C_NFPRE if which else C_NMPRE
                chain(V.scalar_tensor_tensor(out=cA[:, which, :], in0=modcols(4 if which else 1), scalar=1.0,
                                             in1=cols[:, l, g0:g0 + 8], op0=ALU.add, op1=ALU.mult))
                broadcast_rstd(n)
                name = "h2" if which else "h1"
                shift = modcols(3 if which else 0)
                dve.wait_ge(bc_ready, n + 1)
                sync()
                for k in range(KD + 1):
                    if k < KD:
                        if k >= 2:
                            dve.wait_ge(lo_ready, split(l, name, k - 2) + 1)
                        V.scalar_tensor_tensor(out=tmp[k % 2][:, :], in0=x[:, k, :], scalar=cA[:, which, k:k + 1],
                                               in1=b6[:, :], op0=ALU.mult, op1=ALU.mult).then_inc(f_ready, 1)
                    if k:
                        s = split(l, name, k - 1)
                        lo(s, hl[:, k - 1, :], tmp[(k - 1) % 2][:, :], hh[:, k - 1, :], shift[:, k - 1:k])

            def take_y(l, name):
                for m in range(KD):
                    t = tile(l, name, m)
                    n = 4 * l + (1 if name == "wout" else 3)
                    dve.wait_ge(sq_ready, 8 * n + m + 1)
                    free(t, V.tensor_copy(y[:, m, :], acc[t % 4][:, :]))
                evacuated(dve, t)

            def post_norm(l, which):
                n = 4 * l + 1 + 2 * which
                g0 = C_NFPOST if which else C_NMPOST
                chain(V.tensor_tensor(cG[:, which, :], modcols(5 if which else 2), cols[:, l, g0:g0 + 8], ALU.mult))
                broadcast_rstd(n)
                dve.wait_ge(bc_ready, n + 1)
                sync()
                for k in range(KD):
                    chain(V.scalar_tensor_tensor(out=y[:, k, :], in0=y[:, k, :], scalar=cG[:, which, k:k + 1],
                                                 in1=b6[:, :], op0=ALU.mult, op1=ALU.mult))
                    sync()
                    V.tensor_tensor(x[:, k, :], x[:, k, :], y[:, k, :], ALU.add).then_inc(x_ready, 1)

            dve.wait_ge(const_in, 48)
            lg = [cols[:, l, C_LB:C_LB + HEADS] for l in range(L)]
            chain(V.tensor_tensor(lbt[:, 2, :], lg[0], lg[1], ALU.max))
            sync()
            chain(V.tensor_tensor(lbt[:, 0, :], lg[0], lbt[:, 2, :], ALU.subtract))
            V.tensor_tensor(lbt[:, 1, :], lg[1], lbt[:, 2, :], ALU.subtract).then_inc(lb_a, 1)
            dve.wait_ge(lb_b, 1)
            chain(V.tensor_tensor(lbt[:, 2, :], lbt[:, 0, :], lbt[:, 1, :], ALU.add))
            sync()
            chain(V.reciprocal(lbt[:, 3, :], lbt[:, 2, :]))
            sync()
            chain(V.tensor_tensor(lbt[:, 0, :], lbt[:, 0, :], lbt[:, 3, :], ALU.mult))
            chain(V.tensor_tensor(lbt[:, 1, :], lbt[:, 1, :], lbt[:, 3, :], ALU.mult))
            sync()
            chain(V.tensor_tensor(lbt[:, 2, :], lbt[:, 0, :], lbt[:, 1, :], ALU.add))
            chain(V.tensor_tensor(lbs[:, 0, 0, :], lbt[:, 0, :], lbt[:, 0, :], ALU.subtract))
            sync()
            chain(V.tensor_tensor(lbs[:, 1, 0, :], lbt[:, 2, :], lbt[:, 0, :], ALU.subtract))
            sync()
            chain(V.tensor_scalar(lbs[:, :, 1, :], lbs[:, :, 0, :], -1.0, 1.0, ALU.mult, ALU.add))
            dve.wait_ge(pos_in, 16)
            chain(V.tensor_copy(tmp[2][:, :], tmp[3][:, :].bitcast(I32)))
            sync()
            chain(V.tensor_scalar(tmp[2][:, :], tmp[2][:, :], const[:, K_INV:K_INV + 1], None, ALU.mult))
            sync()
            for o, dst, turn in ((0, 0, 0.25), (1, 1, 0.0)):
                r = tmp[dst][:, :]
                chain(V.tensor_scalar(tmp[3][:, :], tmp[2][:, :], 1.0 / TWO_PI, turn, ALU.mult, ALU.add))
                sync()
                chain(V.tensor_scalar(tmp[3][:, :], tmp[3][:, :], MAGIC, None, ALU.add))
                sync()
                chain(V.tensor_scalar(tmp[3][:, :], tmp[3][:, :], -MAGIC, None, ALU.add))
                sync()
                chain(V.scalar_tensor_tensor(out=r, in0=tmp[3][:, :], scalar=-TWO_PI_HI, in1=tmp[2][:, :], op0=ALU.mult, op1=ALU.add))
                sync()
                chain(V.scalar_tensor_tensor(out=r, in0=tmp[3][:, :], scalar=-TWO_PI_LO, in1=r, op0=ALU.mult, op1=ALU.add))
                sync()
                if turn:
                    chain(V.tensor_scalar(r, r, TWO_PI / 4, PI_SAFE, ALU.add, ALU.min))
                    sync()
                    chain(V.tensor_scalar(r, r, -PI_SAFE, None, ALU.max))
                else:
                    sync()
                    V.tensor_scalar(r, r, PI_SAFE, -PI_SAFE, ALU.min, ALU.max).then_inc(ang_ready, 1)
            dve.wait_ge(trig_ready, 2)
            chain(V.tensor_scalar(sinb[:, :], sinb[:, :], const[:, K_SGN:K_SGN + 1], None, ALU.mult))
            take_mod(1, 0, 16, 0)

            def rotate(t, dst, before=None):
                a = acc[t % 4]
                dve.wait_ge(tile_done, t + 1)
                chain(V.tensor_tensor(dst, a[:, :], cosb[:, :], ALU.mult))
                if before is not None:
                    evacuated(dve, before)
                for u in range(4):
                    w = u ^ 1
                    chain(V.tensor_tensor(tmp[3][32 * u:32 * u + 32, :], a[32 * w:32 * w + 32, :],
                                          sinb[32 * u:32 * u + 32, :], ALU.mult))
                sync()

            for l in range(L):
                if l:
                    take_mod(3 * l + 1, 0, 16, l)
                pre_norm(l, 0)
                t = tile(l, "kv", 0)
                rotate(t, tmp[2][:, :])
                free(t, V.tensor_tensor(tmp[2][:, :], tmp[2][:, :], tmp[3][:, :], ALU.add))
                for i in range(4):
                    t = tile(l, "aq", i)
                    rotate(t, aqr[:, i, :], t - 1 if i else tile(l, "kv", 0))
                    free(t, V.tensor_tensor(aqr[:, i, :], aqr[:, i, :], tmp[3][:, :], ALU.add))
                evacuated(dve, tile(l, "gv", 3))
                for i in range(NT):
                    chain(V.bn_stats(bn[:, i, :], gvt[:, i, :]))
                sync()
                for i in range(NT):
                    ins = V.bn_aggr(mv[:, i, :], bn[:, i, :])
                    if i < NT - 1:
                        chain(ins)
                ins.then_inc(vvar, 1)
                dve.wait_ge(vsd, l + 1)
                chain(V.reciprocal(vstd[:, 1, :], vstd[:, 0, :]))
                sync()
                for i in range(NT):
                    chain(V.tensor_scalar(gvt[:, i, :], gvt[:, i, :], mv[:, i, 0:1], vstd[:, 1, i:i + 1], ALU.subtract, ALU.mult))
                dve.wait_ge(rows_in, 16 * (l + 1))
                sync()
                for i in range(NT):
                    chain(V.tensor_tensor(gvt[:, i, :], gvt[:, i, :], rows[:, R_G:R_G + 512], ALU.mult))
                chain(V.tensor_copy(sink[:, :], rows[:, R_SINK:R_SINK + 8]))
                sync()
                for i in range(NT):
                    V.tensor_tensor(gvt[:, i, :], gvt[:, i, :], rows[:, R_B:R_B + 512], ALU.add).then_inc(vn_ready, 1)
                bs = rows[:, R_BS:R_BS + 512].rearrange("p (g t) -> p g t", g=4)
                evacuated(dve, tile(l, "gu", 3))
                for g in range(5):
                    if g < 4:
                        dve.wait_ge(sgu_done, 4 * l + g + 1)
                        u = tmp[g % 2]
                        chain(V.tensor_tensor(u[:, :].rearrange("p (c t) -> p c t", c=NT),
                                              small[g][:, :].rearrange("p (c t) -> p c t", c=NT),
                                              bs[:, g:g + 1, :].broadcast_to([P, NT, P]), ALU.add))
                        sync()
                        V.tensor_tensor(tmp[2 + g % 2][:, :], u[:, :], gut[:, g, :], ALU.mult).then_inc(f_ready, 1)
                    if g:
                        if g == 1:
                            dve.wait_ge(sgu_done, 4 * l + 4)
                        lo(split(l, "ya", g - 1), yal[:, g - 1, :], tmp[2 + (g - 1) % 2][:, :], yah[:, g - 1, :])
                dve.wait_ge(lo_ready, split(l, "ya", 3) + 1)
                chain(V.memset(kt[:, :, :, :], 0.0))
                chain(V.memset(asb[:, :], 0.0))
                evacuated(dve, tile(l, "hf", 3))
                evacuated(dve, tile(l, "hq", 3))
                sync()
                for h in range(HEADS):
                    q = HEADS * l + h
                    lb, lb1 = lbs[:, l, 0, h:h + 1], lbs[:, l, 1, h:h + 1]
                    b3 = bb[:, h, :].rearrange("p (g t) -> p g t", t=SUB)
                    bc = bb[:, h, :].rearrange("p (c t) -> p c t", t=CH)
                    kc = hk[:, h, :].rearrange("p (c t) -> p c t", t=CH)
                    chain(V.tensor_scalar(bb[:, h, :], bb[:, h, :], lb1, lb, ALU.mult, ALU.add))
                    chain(V.tensor_scalar(hk[:, h, :], hk[:, h, :], lb1, None, ALU.mult))
                    sync()
                    if h:
                        dve.wait_ge(o_done, q)
                    V.tensor_scalar(bb[:, h, :], bb[:, h, :], MIN_FORGET, None, ALU.max).then_inc(forget_ready, 1)
                    dve.wait_ge(log_ready, q + 1)
                    for c in range(NCH):
                        v = slice(CH * c, CH * c + CH)
                        chain(V.tensor_tensor_scan(bb[:, h, v], tmp[0][:, v], tmp[0][:, v], 0.0, ALU.add, ALU.bypass))
                    sync()
                    chain(V.tensor_tensor(tmp[0][:, :].rearrange("p (g t) -> p g t", t=SUB), b3,
                                          b3[:, :, MID:MID + 1].broadcast_to([P, S // SUB, SUB]), ALU.subtract))
                    V.tensor_tensor(tmp[2][:, :].rearrange("p (c t) -> p c t", t=CH),
                                    bc[:, :, CH - 1:CH].broadcast_to([P, NCH, CH]), bc, ALU.subtract).then_inc(diff_ready, 1)

                    def key_diff(i):
                        n = SUB * (i + 1)
                        if i >= 4:
                            dve.wait_ge(a_done, NSUB * q + i - 3)
                        elif h:
                            chain(V.memset(kt[:, i, :, n:n + 4 * SUB], 0.0))
                        m = SUB * i + MID
                        V.tensor_tensor(kt[:, i % 4, :, 0:n], bc[:, :, m:m + 1].broadcast_to([P, NCH, n]), bc[:, :, 0:n],
                                        ALU.subtract).then_inc(kdiff, 1)

                    def key_tile(i):
                        n = SUB * (i + 1)
                        dve.wait_ge(kexp, NSUB * q + i + 1)
                        v = kt[:, i % 4, :, 0:n]
                        V.tensor_tensor(v, v, kc[:, :, 0:n], ALU.mult).then_inc(kt_ready, 1)

                    for i in range(4):
                        key_diff(i)
                    dve.wait_ge(exp_ready, q + 1)
                    chain(V.scalar_tensor_tensor(out=tmp[0][:, :], in0=hqs[:, h, :], scalar=HG_SCALE, in1=tmp[0][:, :],
                                                 op0=ALU.mult, op1=ALU.mult))
                    chain(V.scalar_tensor_tensor(out=tmp[1][:, :], in0=hqs[:, h, :], scalar=HG_SCALE, in1=tmp[1][:, :],
                                                 op0=ALU.mult, op1=ALU.mult))
                    sync()
                    V.tensor_tensor(tmp[2][:, :], hk[:, h, :], tmp[2][:, :], ALU.mult).then_inc(qk_ready, 1)
                    for i in range(4):
                        key_tile(i)
                    for i in range(4, NSUB):
                        key_diff(i)
                    for i in range(4, NSUB):
                        key_tile(i)
                    dve.wait_ge(ds_done, q + 1)
                    for c in range(NCH - 1):
                        src = (b6 if c % 2 else b7)[:, P * (c // 2):P * (c // 2) + P]
                        if c == 0:
                            ins = V.tensor_copy(states[:, 0, :], src)
                        else:
                            ins = V.scalar_tensor_tensor(out=states[:, c, :], in0=states[:, c - 1, :], scalar=elast[:, c:c + 1],
                                                         in1=src, op0=ALU.mult, op1=ALU.add)
                        if c < NCH - 2:
                            chain(ins)
                            sync()
                        else:
                            ins.then_inc(state_ready, 1)
                    dve.wait_ge(a_done, NSUB * (q + 1))
                    V.copy_predicated(asb[:, :].rearrange("p (c t) -> p c t", c=NT),
                                      const[:, K_HM:K_HM + P].bitcast(U32).unsqueeze(1).broadcast_to([P, NT, P]),
                                      b4[:, :].rearrange("p (c t) -> p c t", c=NT)).then_inc(masked, 1)
                dve.wait_ge(ostd, l + 1)
                chain(V.reciprocal(rstd[:, :], std[:, :]))
                sync()
                evacuated(dve, tile(l, "hg", 3))
                for h in range(HEADS):
                    q = HEADS * l + h
                    if h:
                        dve.wait_ge(obc, q)
                    V.tensor_tensor(tmp[3][:, :].rearrange("p (t n) -> p t n", t=NT),
                                    ident.unsqueeze(1).broadcast_to([P, NT, P]),
                                    rstd[:, 4 * h:4 * h + 4].unsqueeze(2).broadcast_to([P, NT, P]),
                                    ALU.mult).then_inc(odiag, 1)
                    dve.wait_ge(obc, q + 1)
                    t2 = tmp[2]
                    chain(V.scalar_tensor_tensor(out=t2[:, :], in0=bb[:, h, :], scalar=cols[:, l, C_GN:C_GN + 1],
                                                 in1=(b4 if h % 2 else b5)[:, :], op0=ALU.mult, op1=ALU.mult))
                    sync()
                    V.tensor_tensor(tmp[h % 2][:, :], t2[:, :], hgs[:, h, :], ALU.mult).then_inc(f_ready, 1)
                    lo(split(l, "yc", h), ycl[:, h, :], tmp[h % 2][:, :], ych[:, h, :])
                dve.wait_ge(kd_ready, 4 * (l + 1))
                for n in range(NT):
                    for j in range(2):
                        a = 8 * l + 2 * n + j
                        w = 256 if n else 128
                        mk = const[:, K_AM + 256 - w:K_AM + 256].unsqueeze(1).broadcast_to([P, 2, w])
                        dve.wait_ge(qk_done, a + 1)
                        for o in range(2):
                            chain(V.scalar_tensor_tensor(out=pm[:, o:4:2, 0:w],
                                                         in0=small[o][:, 0:2 * w].rearrange("p (h k) -> p h k", h=2),
                                                         scalar=AT_SCALE, in1=mk, op0=ALU.mult, op1=ALU.add))
                        sync()
                        chain(V.tensor_reduce(amx[:, 0, :], pm[:, :, 0:w], AX_X, ALU.max))
                        sync()
                        sk = sink[:, 4 * j:4 * j + 4]
                        chain(V.tensor_tensor(amx[:, 0, :], amx[:, 0, :], sk, ALU.max))
                        sync()
                        chain(V.tensor_scalar(amx[:, 1, :], amx[:, 0, :], -1.0, None, ALU.mult))
                        V.tensor_tensor(amx[:, 2, :], sk, amx[:, 0, :], ALU.subtract).then_inc(max_ready, 1)
                        dve.wait_ge(p_exp, a + 1)
                        chain(V.tensor_tensor(ars[:, 2, :], ars[:, 0, :], ars[:, 1, :], ALU.add))
                        sync()
                        chain(V.reciprocal(ars[:, 2, :], ars[:, 2, :]))
                        sync()
                        V.tensor_tensor(pm[:, :, 0:w], pm[:, :, 0:w], ars[:, 2, :].unsqueeze(2).broadcast_to([P, 4, w]),
                                        ALU.mult).then_inc(p_ready, 1)
                        dve.wait_ge(pt_done, a + 1)
                        V.tensor_copy(pts[:, 1, :, :], b7[:, :].rearrange("p (t n) -> p t n", t=4)).then_inc(pt_copied_v, 1)
                        dve.wait_ge(ybh_ready, a + 1)
                        v = slice(P * n, P * n + P)
                        V.tensor_tensor(ybl[:, 2 * j:2 * j + 2, v], b6[:, 0:256].rearrange("p (t n) -> p t n", t=2),
                                        ybh[:, 2 * j:2 * j + 2, v].bitcast(F32), ALU.subtract).then_inc(yb_ready, 1)
                for m in range(KD):
                    evacuated(dve, tile(l, "gate", 6 * (m // 2) + 5))
                    T, U = tmp[2 + m % 2], sq[0]
                    for br in range(3):
                        t = tile(l, "proj", 3 * m + br)
                        dve.wait_ge(tile_done, t + 1)
                        dst = T if br == 0 else U
                        free(t, V.tensor_tensor(dst[:, :], acc[t % 4][:, :], gates[:, 2 * br + m % 2, :], ALU.mult))
                        if br:
                            evacuated(dve, t)
                            ins = V.tensor_tensor(T[:, :], T[:, :], U[:, :], ALU.add)
                            if br == 1:
                                chain(ins)
                                sync()
                            else:
                                ins.then_inc(f_ready, 1)
                    lo(split(l, "mg", m), mgl[:, m, :], T[:, :], mgh[:, m, :])
                take_y(l, "wout")
                take_mod(3 * l + 2, 16, 40, l)
                post_norm(l, 0)
                pre_norm(l, 1)
                take_mod(3 * l + 3, 40, 48, l)
                for p in range(NPAIR):
                    for j in range(2):
                        t = tile(l, "w1", 2 * p + j)
                        c0 = C_CONV + 8 * p + 4 * j
                        a, T = acc[t % 4], tmp[2 * (p % 2) + j]
                        dve.wait_ge(conv0, 2 * (NPAIR * l + p) + j + 1)
                        chain(V.scalar_tensor_tensor(out=T[:, 1:S], in0=a[:, 0:S - 1], scalar=cols[:, l, c0 + 1:c0 + 2],
                                                     in1=T[:, 1:S], op0=ALU.mult, op1=ALU.add))
                        sync()
                        free(t, V.scalar_tensor_tensor(out=T[:, 2:S], in0=a[:, 0:S - 2], scalar=cols[:, l, c0:c0 + 1],
                                                       in1=T[:, 2:S], op0=ALU.mult, op1=ALU.add))
                    evacuated(dve, t)
                    T = tmp[2 * (p % 2)]
                    dve.wait_ge(silu_done, NPAIR * l + p + 1)
                    V.tensor_tensor(T[:, :], T[:, :], tmp[2 * (p % 2) + 1][:, :], ALU.mult).then_inc(f_ready, 1)
                    lo(split(l, "ff", p), actl[:, p, :], T[:, :], acth[:, p, :])
                take_y(l, "w2")
                post_norm(l, 1)

        @block.tensor
        def _(pe):
            MM = nc.tensor.matmul

            def sums_of_squares(n, k):
                pe.wait_ge(sq_ready, 8 * n + k + 1)
                if k == 0 and n:
                    pe.wait_ge(bc_read_sem(n), bc_read_val(n))
                for c in range(NT):
                    ins = MM(b6[:, c:c + 1], sq[k % 2][:, P * c:P * c + P], ones[:, 0:1], start=(k == 0 and c == 0),
                             stop=(k == KD - 1), skip_group_check=True)
                ins.then_inc(ss_done, 1)

            def bc_read_sem(n):
                return x_ready if n % 2 == 0 else lo_ready

            def bc_read_val(n):
                l, i = n // 4, n % 4
                return {0: 16 * l, 1: split(l, "h1", 7) + 1, 2: 16 * l + 8, 3: split(l, "h2", 7) + 1}[i]

            def broadcast(n):
                pe.wait_ge(diag_ready, n + 1)
                ins = MM(b6[:, :], ones, tmp[3][:, :], start=True, stop=True)
                ins.then_inc(bc_ready, 1)

            def weights_of(b):
                s = split_no[b]
                pe.wait_ge(whi_ready, s + 1)
                pe.wait_ge(wlo_ready, s + 1)
                return whi[:, s % 2, :], wlo[:, s % 2, :]

            def acquire(t):
                if t >= 4:
                    pe.wait_ge(acc_free[t % 4], t // 4)
                return acc[t % 4]

            def three(out, his, los, xh, xl, first, last):
                n = len(his)
                for k in range(n):
                    MM(out, his[k], xh[k], start=(first and k == 0), stop=False, skip_group_check=True)
                    MM(out, his[k], xl[k], start=False, stop=False, skip_group_check=True)
                for k in range(n):
                    ins = MM(out, los[k], xh[k], start=False, stop=(last and k == n - 1), skip_group_check=True)
                return ins

            def ada(l, j):
                b = ("ada", l, j)
                i = at[b]
                pe.wait_ge(landed[i % 2], 16 * (i // 2 + 1))
                w = stage[:, i % 2, :].rearrange("p (k n) -> p k n", k=KD)
                for c in range(2):
                    for k in range(KD):
                        ins = MM(b7[:, 2 * j + c:2 * j + c + 1], w[:, k, P * c:P * c + P], cact[:, k:k + 1],
                                 start=(k == 0), stop=(k == KD - 1), skip_group_check=True)
                ins.then_inc(ada_used, 1)

            def feature_tiles(b, width, names, xh, xl):
                hi, lo = weights_of(b)
                hi = hi.rearrange("p (k n) -> p k n", k=KD)
                lo = lo.rearrange("p (k n) -> p k n", k=KD)
                for c, t in names:
                    out = acquire(t)
                    ins = three(out[:, :], [hi[:, k, P * c:P * c + P] for k in range(KD)],
                                [lo[:, k, P * c:P * c + P] for k in range(KD)],
                                [xh[:, k, :] for k in range(KD)], [xl[:, k, :] for k in range(KD)], True, True)
                    ins.then_inc(tile_done, 1)

            def token_tiles(b, c0, width, tiles_):
                hi, lo = weights_of(b)
                hi = hi.rearrange("p (k n) -> p k n", k=KD)[:, :, c0:c0 + width]
                lo = lo.rearrange("p (k n) -> p k n", k=KD)[:, :, c0:c0 + width]
                per = 512 // width
                for i, t in enumerate(tiles_):
                    out = acquire(t)
                    for u in range(per):
                        tt = per * i + u
                        v = slice(P * tt, P * tt + P)
                        o = out[:, width * u:width * u + width]
                        for k in range(KD):
                            MM(o, hh[:, k, v], hi[:, k, :], start=(k == 0), stop=False, skip_group_check=True)
                            MM(o, hh[:, k, v], lo[:, k, :], start=False, stop=False, skip_group_check=True)
                        for k in range(KD):
                            ins = MM(o, hl[:, k, v], hi[:, k, :], start=False, stop=(k == KD - 1), skip_group_check=True)
                    ins.then_inc(tile_done, 1)

            pe.wait_ge(const_in, 48)
            pe.wait_ge(cact_ready, 1)
            for j in range(8):
                ada(0, j)

            for l in range(L):
                for k in range(KD):
                    sums_of_squares(4 * l, k)
                broadcast(4 * l)
                pe.wait_ge(lo_ready, split(l, "h1", KD - 1) + 1)
                for b in range(NFRONT):
                    name = FRONT[b]
                    first = b == 0 or FRONT[b - 1] != name
                    blk = ("win", l, b)
                    i0 = 0 if first else 2
                    if name in ("hi", "gv"):
                        token_tiles(blk, 0, 256, [tile(l, name, i0), tile(l, name, i0 + 1)])
                    elif name == "kv":
                        feature_tiles(blk, 256, [(0, tile(l, "kv", 0))], hh, hl)
                        token_tiles(blk, 128, 128, [tile(l, "kv", 1)])
                    else:
                        feature_tiles(blk, 256, [(0, tile(l, name, i0)), (1, tile(l, name, i0 + 1))], hh, hl)
                pe.wait_ge(vn_ready, NT * (l + 1))
                pe.wait_ge(ws_ready, l + 1)
                for g in range(4):
                    for c in range(NT):
                        ins = MM(small[g][:, P * c:P * c + P], gvt[:, c, P * g:P * g + P], ws[:, g, :], start=True, stop=True)
                    ins.then_inc(sgu_done, 1)
                evacuated(pe, tile(l, "hi", 3))
                pe.wait_ge(lo_ready, split(l, "ya", 3) + 1)
                for h in range(HEADS):
                    q = HEADS * l + h
                    hv = slice(P * h, P * h + P)
                    pe.wait_ge(qk_ready, q + 1)
                    for c in range(NT):
                        ins = nc.tensor.transpose(b6[:, P * c:P * c + P], tmp[2][:, P * c:P * c + P], ident)
                    ins.then_inc(khT_done, 1)
                    for i in range(NSUB):
                        if i == 4:
                            pe.wait_ge(khT_copied, q + 1)
                            for c in range(NCH - 1):
                                r = slice(CH * (c % 2), CH * (c % 2) + CH)
                                o = (b6 if c % 2 else b7)[:, P * (c // 2):P * (c // 2) + P]
                                ins = MM(o, khT[r, c // 2, :], itok[r, c // 2, hv], start=True, stop=True)
                            ins.then_inc(ds_done, 1)
                        pe.wait_ge(kt_ready, NSUB * q + i + 1)
                        q4 = tmp[0][:, :].rearrange("p (r c t) -> p r c t", r=NT, c=2)
                        o4 = b4[:, :].rearrange("p (r c t) -> p r c t", r=NT, c=2)
                        for r in range(NT):
                            v = slice(SUB * i, SUB * i + SUB)
                            ins = MM(o4[:, r, :, v], kt[:, i % 4, 2 * r:2 * r + 2, :], q4[:, r, :, v], start=(i == 0 and r == 0),
                                     stop=True, skip_group_check=True)
                        ins.then_inc(a_done, 1)
                    pe.wait_ge(state_ready, q + 1)
                    pe.wait_ge(masked, q + 1)
                    if h:
                        pe.wait_ge(o_copied, q)
                    for r in range(NT):
                        MM(b5[:, P * r:P * r + P], itok[:, r, hv], asb[:, P * r:P * r + P], start=True, stop=False,
                           skip_group_check=True)
                        for c in (2 * r, 2 * r + 1):
                            if c:
                                ins = MM(b5[:, CH * c:CH * c + CH], states[:, c - 1, :], tmp[1][:, CH * c:CH * c + CH],
                                         start=False, stop=True, skip_group_check=True)
                    ins.then_inc(o_done, 1)
                for h in range(HEADS):
                    q = HEADS * l + h
                    pe.wait_ge(osq_ready, q + 1)
                    for c in range(NT):
                        ins = MM(b6[:, 4 * h + c:4 * h + c + 1], sq[h % 2][:, P * c:P * c + P], ones[:, 0:1],
                                 start=True, stop=True)
                    ins.then_inc(oss_done, 1)
                for h in range(HEADS):
                    q = HEADS * l + h
                    pe.wait_ge(odiag, q + 1)
                    if h >= 2:
                        pe.wait_ge(f_ready, split(l, "yc", h - 2) + 1)
                    MM((b4 if h % 2 else b5)[:, :], ones, tmp[3][:, :], start=True, stop=True).then_inc(obc, 1)
                evacuated(pe, tile(l, "aq", 3))
                pe.wait_ge(kd_ready, 4 * (l + 1))
                evacuated(pe, tile(l, "kv", 1))
                pe.wait_ge(lo_ready, split(l, "yc", 3) + 1)

                def scores(n, j):
                    a = 8 * l + 2 * n + j
                    w = 256 if n else 128
                    if 2 * n + j:
                        pe.wait_ge(max_ready, a)
                    for i in range(4):
                        h = 4 * j + i
                        r = slice(64 * (h % 2), 64 * (h % 2) + 64)
                        ins = MM(small[i % 2][:, w * (i // 2):w * (i // 2) + w], aqr[r, h // 2, P * n:P * n + P],
                                 kd[r, j, P * (n + 1) - w:P * (n + 1)], start=True, stop=True)
                    ins.then_inc(qk_done, 1)

                scores(0, 0)
                for n in range(NT):
                    for j in range(2):
                        a = 8 * l + 2 * n + j
                        if (n, j) != (NT - 1, 1):
                            scores(n + (j == 1), 1 - j)
                        pe.wait_ge(p_ready, a + 1)
                        if 2 * n + j:
                            pe.wait_ge(yb_ready, a)
                        for half in range(0 if n else 1, 2):
                            o = 128 * half if n else 0
                            for i in range(4):
                                ins = nc.tensor.transpose((b7 if half else b6)[:, P * i:P * i + P], pm[:, i, o:o + P], ident)
                        ins.then_inc(pt_done, 1)
                        if n:
                            pe.wait_ge(pt_copied_a, 6 * l + 2 * (n - 1) + j + 1)
                        pe.wait_ge(pt_copied_v, a + 1)
                        for i in range(4):
                            o = b6[64 * (i % 2):64 * (i % 2) + 64, P * (i // 2):P * (i // 2) + P]
                            for half in range(0 if n else 1, 2):
                                ins = MM(o, vt[:, n - 1 + half, 64 * j:64 * j + 64], pts[:, half, i, :],
                                         start=(half == 0 or not n), stop=(half == 1), skip_group_check=True)
                        ins.then_inc(pv_done, 1)
                pe.wait_ge(yb_ready, 8 * (l + 1))
                for mp in range(NMP):
                    for br in range(3):
                        blk = ("win", l, NFRONT + 3 * mp + br)
                        t0 = tile(l, "gate", 6 * mp + 2 * br)
                        feature_tiles(blk, 256, [(0, t0), (1, t0 + 1)], hh, hl)
                    for j in range(3):
                        ada(l, 8 + 3 * mp + j)
                    for j in range(2):
                        m = 2 * mp + j
                        blk = ("proj", l, m)
                        hi, lo = weights_of(blk)
                        for br, (yh, yl) in enumerate(((yah, yal), (ybh, ybl), (ych, ycl))):
                            t = tile(l, "proj", 3 * m + br)
                            out = acquire(t)
                            ks = range(4)
                            ins = three(out[:, :], [hi[:, P * (4 * br + k):P * (4 * br + k) + P] for k in ks],
                                        [lo[:, P * (4 * br + k):P * (4 * br + k) + P] for k in ks],
                                        [yh[:, k, :] for k in ks], [yl[:, k, :] for k in ks], True, True)
                            ins.then_inc(tile_done, 1)
                pe.wait_ge(lo_ready, split(l, "mg", 7) + 1)
                for m in range(4):
                    feature_tiles(("wout", l, m), 256, [(0, tile(l, "wout", 2 * m)), (1, tile(l, "wout", 2 * m + 1))], mgh, mgl)
                    if m:
                        sums_of_squares(4 * l + 1, 2 * m - 2)
                        sums_of_squares(4 * l + 1, 2 * m - 1)
                sums_of_squares(4 * l + 1, 6)
                sums_of_squares(4 * l + 1, 7)
                broadcast(4 * l + 1)
                pe.wait_ge(mod_read, 3 * l + 2)
                for j in range(20, 24):
                    ada(l, j)
                for k in range(KD):
                    sums_of_squares(4 * l + 2, k)
                broadcast(4 * l + 2)
                pe.wait_ge(lo_ready, split(l, "h2", KD - 1) + 1)
                for p in range(NPAIR):
                    feature_tiles(("w1", l, p), 256, [(0, tile(l, "w1", 2 * p)), (1, tile(l, "w1", 2 * p + 1))], hh, hl)
                pe.wait_ge(lo_ready, split(l, "ff", NPAIR - 1) + 1)
                for mm in range(4):
                    outs = [tile(l, "w2", 2 * mm), tile(l, "w2", 2 * mm + 1)]
                    for third in range(3):
                        k0 = 8 * third
                        nk = min(8, NPAIR - k0)
                        hi, lo = weights_of(("w2", l, 3 * mm + third))
                        for c in range(2):
                            out = acquire(outs[c]) if third == 0 else acc[outs[c] % 4]
                            ks = range(nk)
                            ins = three(out[:, :], [hi[:, 256 * k + P * c:256 * k + P * c + P] for k in ks],
                                        [lo[:, 256 * k + P * c:256 * k + P * c + P] for k in ks],
                                        [acth[:, k0 + k, :] for k in ks], [actl[:, k0 + k, :] for k in ks],
                                        third == 0, third == 2)
                            if third == 2:
                                ins.then_inc(tile_done, 1)
                            elif c == 1:
                                ins.then_inc(third_used, 1)
                    if mm:
                        sums_of_squares(4 * l + 3, 2 * mm - 2)
                        sums_of_squares(4 * l + 3, 2 * mm - 1)
                sums_of_squares(4 * l + 3, 6)
                sums_of_squares(4 * l + 3, 7)
                broadcast(4 * l + 3)
                if l + 1 < L:
                    pe.wait_ge(mod_read, 3 * l + 3)
                    for j in range(8):
                        ada(l + 1, j)


def kernel(**inputs):
    import numpy as np
    import concourse.bacc as bacc
    from concourse.bass_utils import run_bass_kernel_spmd

    a = {k: np.asarray(v) for k, v in inputs.items()}

    def blocks(w, width):
        l, k, n = w.shape
        w = w.reshape(l, k // P, P, n // width, width).transpose(0, 3, 2, 1, 4)
        return np.ascontiguousarray(w).reshape(l, n // width, P, k // P * width)

    def columns(v):
        v = v.reshape(v.shape[:-1] + (v.shape[-1] // P, P))
        return np.moveaxis(v, -1, 0)

    w_in = a["w_in"]
    gu, gv, aq, kv, hq, hf, hi, hg = (w_in[:, :, s:e] for s, e in (
        (0, 512), (512, 1024), (1024, 1536), (1536, 1792), (1792, 2304), (2304, 2816), (2816, 3328), (3328, 3840)))
    g = w_in[:, :, 3840:].reshape(L, D, 3, NMP, 256).transpose(0, 1, 3, 2, 4).reshape(L, D, 3 * D)
    win = blocks(np.concatenate([hf, hq, hi, gv, gu, kv, aq, hg, g], axis=2), 256)
    proj = blocks(np.concatenate([a["proj_a"], a["proj_b"], a["proj_c"]], axis=1), P)
    w1 = a["ffn_w1"].reshape(L, D, 2, NPAIR, P).transpose(0, 1, 3, 2, 4).reshape(L, D, 2 * FF)

    conv = np.concatenate([a["ffn_conv_w"], a["ffn_conv_b"][:, None, :]], axis=1)
    conv = conv.reshape(L, 4, 2, NPAIR, P).transpose(4, 0, 3, 2, 1).reshape(P, L, NPAIR * 8)
    cols = np.concatenate([columns(a[n]) for n in ("ada_b", "norm_mix_pre", "norm_mix_post", "norm_ffn_pre",
                                                   "norm_ffn_post", "hg_lb_logits", "hg_gnorm")] + [conv], axis=2)
    rows = np.concatenate([a["gm_ln_g"], a["gm_ln_b"], a["gm_bs"].reshape(L, 512), a["attn_sinks"]], axis=1)

    const = np.zeros((P, NCONST), np.float32)
    i = np.arange(P)
    const[:, K_ID:K_ID + P] = np.eye(P)
    const[:, K_ONE:K_ONE + P] = 1.0
    delta = i[:, None] + P - np.arange(256)[None, :]
    const[:, K_AM:K_AM + 256] = np.where((delta >= 0) & (delta < 128), 0.0, -1e30)
    const[:, K_HM:K_HM + P] = (i[:, None] // CH == i[None, :] // CH) & (i[:, None] <= i[None, :])
    const[:, K_INV] = np.float32(10000.0) ** (-(i % 32).astype(np.float32) / np.float32(32))
    const[:, K_SGN] = np.where(i // 32 % 2 == 0, -1.0, 1.0)
    const[:, K_EPS] = EPS

    arrays = {
        "xT": np.ascontiguousarray(a["x"][0].reshape(S, KD, P).transpose(2, 1, 0)),
        "c": np.ascontiguousarray(a["c"][0].reshape(KD, P).T),
        "pos": np.ascontiguousarray(a["positions"][0]),
        "cols": np.ascontiguousarray(cols),
        "rows": np.ascontiguousarray(rows),
        "const": const,
        "ws": np.ascontiguousarray(a["gm_ws"].transpose(0, 3, 1, 2)),
        "ada": blocks(a["ada_w"], 256),
        "win": win,
        "proj": proj,
        "wout": blocks(a["w_out"], 256),
        "w1": blocks(w1, 256),
        "w2": blocks(a["ffn_w2"], 256),
    }
    nc = bacc.Bacc("TRN2", target_bir_lowering=False, num_devices=1)
    args = [nc.dram_tensor(n, v.shape, mybir.dt.from_np(v.dtype), kind="ExternalInput").ap() for n, v in arrays.items()]
    out = nc.dram_tensor("out", (P, KD, S), F32, kind="ExternalOutput").ap()
    trunk(nc, *args, out)
    r = run_bass_kernel_spmd(nc, [arrays], core_ids=[0])
    got = r.results[0]["out"]
    return np.ascontiguousarray(got.transpose(2, 1, 0)).reshape(1, S, D)
```

```python
from contextlib import ExitStack

import concourse.bass as bass
from concourse import mybir

ALU = mybir.AluOpType
ACT = mybir.ActivationFunctionType
F32 = mybir.dt.float32
F32R = mybir.dt.float32r
I32 = mybir.dt.int32
U32 = mybir.dt.uint32
AX_X = mybir.AxisListType.X

P = 128
D = 1024
S = 512
L = 2
KD = D // P
NT = S // P
EPS = 1e-6
FF = 2816
NPAIR = FF // P
HEADS = 4
CH = 64
NCH = S // CH
SUB = 8
NSUB = CH // SUB
MID = SUB // 2 - 1
MIN_FORGET = 1e-6
HG_SCALE = 128 ** -0.5
AT_SCALE = 64 ** -0.5
MAGIC = 12582912.0
TWO_PI = 6.283185307179586
TWO_PI_HI = 6.28125
TWO_PI_LO = TWO_PI - TWO_PI_HI
PI_SAFE = 3.1415925

C_ADA, C_NMPRE, C_NMPOST, C_NFPRE, C_NFPOST, C_LB, C_GN, C_CONV = 0, 48, 56, 64, 72, 80, 84, 85
NCOL = C_CONV + NPAIR * 2 * 4
K_ID, K_ONE, K_AM, K_HM, K_INV, K_SGN, K_EPS = 0, 128, 256, 512, 640, 641, 642
NCONST = 643
R_BS, R_SINK = 0, 512
NROW = 520

NMP = 4
BLK = 1024
STAGES = 4
RING = 3
KTS = 5


BRANCHES = ("a", "c", "b")
NSTEP = 3 * NMP
BLOCKS = [(n, i) for n in ("hf", "hq", "hi", "hg", "gv", "gu") for i in range(4)]
BLOCKS += [("kv", 0), ("kv", 1)] + [("aq", i) for i in range(4)]
NFRONT = len(BLOCKS)
for s in range(NSTEP):
    BLOCKS += [("gate", 2 * s), ("gate", 2 * s + 1), ("proj", s)]
BLOCKS += [("wout", i) for i in range(8)] + [("w1", i) for i in range(2 * NPAIR)] + [("w2", i) for i in range(24)]
BLOCK_AT = {b: i for i, b in enumerate(BLOCKS)}
NBLOCK = len(BLOCKS)

ADA_PAIR = {1: 6, 5: 7, 9: 8, 13: 9, 17: 10, 21: 11}


def ada_after(l, block):
    name, i = block
    if name == "gate":
        return [(l, 16 + i)]
    if name == "w1":
        n = i // 2 + (2 if i // 2 >= 2 else i // 2)
        cols = ([n] if i % 2 == 0 else []) + ([n + 1] if i in (1, 3) else [])
        return [(l, 40 + c) if c < 8 else (l + 1, c - 8) for c in cols if c < 8 or l + 1 < L]
    return []


def weight_stream():
    out = []
    for l in range(L):
        for b in BLOCKS:
            out.append((l, b))
            out += [("ada", x, c) for x, c in ada_after(l, b)]
    return out


TILES = [(n, i) for n in ("hf", "hq", "hi", "hg", "gv", "gu") for i in range(4)]
TILES += [("kv", 0), ("kv", 1)] + [("aq", i) for i in range(4)]
for s in range(NSTEP):
    if s >= 2 and s % 2 == 0:
        TILES += [("ada", s // 2 - 1)]
    TILES += [("gate", 2 * s)]
    if s == 0:
        TILES += [("oss", 0)]
    TILES += [("gate", 2 * s + 1), ("proj", 2 * s), ("proj", 2 * s + 1)]
TILES += [("wout", 0), ("ada", 5)] + [("wout", i) for i in range(1, 8)]
for p in range(NPAIR):
    TILES += [("w1", 2 * p), ("w1", 2 * p + 1)]
    if p in ADA_PAIR:
        TILES += [("ada", ADA_PAIR[p])]
TILES += [("w2", i) for i in range(8)]
TILE_AT = {t: i for i, t in enumerate(TILES)}
NTILE = len(TILES)

PARTS = [(n, i) for n in ("hi", "gv") for i in (0, 2)] + [("w2", i) for i in range(24) if i % 3 < 2]
PART_AT = {b: i for i, b in enumerate(sorted(PARTS, key=BLOCK_AT.get))}

SPLITS = [("h1", k) for k in range(8)] + [("ya", g) for g in range(4)] + [("yc", h) for h in range(4)]
SPLITS += [("mg", m) for m in range(8)] + [("h2", k) for k in range(8)] + [("ff", p) for p in range(NPAIR)]
NSPLIT = len(SPLITS)
SPLIT_AT = {t: i for i, t in enumerate(SPLITS)}

POOL_K = (1, 4, 6)
HG_BLOCKS = BLOCKS[BLOCK_AT[("hi", 0)]:NFRONT]


def tile(l, name, i):
    return l * NTILE + TILE_AT[(name, i)]


def split(l, name, i):
    return l * NSPLIT + SPLIT_AT[(name, i)]


def last_tile(b):
    name, i = b
    return ("proj", 2 * i + 1) if name == "proj" else ("w2", i // 3) if name == "w2" else b


def ada_tiles(l):
    return 12 if l + 1 < L else 8


def trunk(nc, xT_d, c_d, pos_d, cols_d, rows_d, ln_d, const_d, ws_d, ada_d, win_d, proj_d, wout_d, w1_d, w2_d, out_d):
    stream = weight_stream()
    at = {b: i for i, b in enumerate(stream)}
    kinds = [b for b in stream if b[0] != "ada"]
    adas = [b for b in stream if b[0] == "ada"]
    ada_no = {b: i for i, b in enumerate(adas)}

    ctx = ExitStack()
    with ctx:
        def sem(name):
            return ctx.enter_context(nc.semaphore(name))

        KB = 1024
        SLAB = 212832
        start = (nc.sbuf_base + 63) // 64 * 64
        ctx.enter_context(nc.sbuf_tensor("slab", [P, SLAB // 4], F32))

        cursor = [start]

        def place(name, shape, dt, where=None):
            if where is None:
                where = cursor[0]
                n = 4
                for s in shape[1:]:
                    n *= s
                cursor[0] += (n + 31) // 32 * 32
                assert cursor[0] <= start + SLAB, (name, cursor[0] - start)
            return nc.alloc_sbuf_tensor_at(name, shape, dt, offset=where)

        x = place("x", [P, KD, S], F32)
        H0 = cursor[0]
        hh = place("hh", [P, KD, S], F32R)
        hl = place("hl", [P, KD, S], F32R)
        y = place("y", [P, KD, S], F32, H0)
        stage = place("stage", [P, STAGES, BLK], F32)
        whi = place("whi", [P, RING, BLK], F32R)
        wlo = place("wlo", [P, RING, BLK], F32R)
        R0 = cursor[0]
        cursor[0] += 104 * KB

        def at_kb(name, shape, dt, kb):
            return place(name, shape, dt, R0 + int(kb * KB))

        ada0 = at_kb("ada0", [P, 16, BLK], F32, 0)
        hf32 = at_kb("hf32", [P, KD, S], F32, 0)
        gut = at_kb("gut", [P, 4, S], F32, 0)
        yah = at_kb("yah", [P, 4, S], F32R, 0)
        gvt = at_kb("gvt", [P, NT, 512], F32, 8)
        yal = at_kb("yal", [P, 4, S], F32R, 8)
        hqs = at_kb("hqs", [P, HEADS, S], F32, 16)
        ych = at_kb("ych", [P, 4, S], F32R, 16)
        hk = at_kb("hk", [P, HEADS, S], F32, 24)
        ycl = at_kb("ycl", [P, 4, S], F32R, 24)
        lnrow = at_kb("lnrow", [P, 2, 512], F32, 32)
        aqr = at_kb("aqr", [P, 4, S], F32, 32)
        ybh = at_kb("ybh", [P, 4, S], F32R, 32)
        itok = at_kb("itok", [P, NT, 512], F32, 40)
        ybl = at_kb("ybl", [P, 4, S], F32R, 40)
        bb = at_kb("bb", [P, HEADS, S], F32, 48)
        hgs = at_kb("hgs", [P, HEADS, S], F32, 56)
        mg = at_kb("mg", [P, KD, S], F32, 48)
        mgh = at_kb("mgh", [P, KD, S], F32R, 0)
        mgl = at_kb("mgl", [P, KD, S], F32R, 16)
        kd = at_kb("kd", [P, 2, S], F32, 64)
        vt = at_kb("vt", [P, NT, 128], F32, 68)
        khT = at_kb("khT", [P, NT, 128], F32, 70)
        states = at_kb("states", [P, NCH - 1, 128], F32, 72)
        asb = at_kb("asb", [P, S], F32, 75.5)
        gates = at_kb("gates", [P, 4, S], F32, 70)
        kt = at_kb("kt", [P, KTS, NCH, CH], F32, 78)
        odg = at_kb("odg", [P, 16, P], F32, 78)
        pm = at_kb("pm", [P, 4, 256], F32, 78)
        pts = at_kb("pts", [P, 2, 4, 128], F32, 82)
        tmp = [at_kb(f"tmp{i}", [P, S], F32, 88 + 2 * i) for i in range(5)]
        sq = [at_kb(f"sq{i}", [P, S], F32, 98 + 2 * i) for i in range(2)]
        ada_sum = at_kb("ada_sum", [P, 4, P], F32, 102)
        acth = at_kb("acth", [P, NPAIR, S], F32R, 0)
        actl = at_kb("actl", [P, NPAIR, S], F32R, 44)
        hgset = [(tmp[0], tmp[1], tmp[2]), (tmp[4], sq[0], sq[1])]
        osq = [tmp[0], tmp[1], tmp[4], sq[0]]

        cosb = place("cosb", [P, S], F32)
        sinb = place("sinb", [P, S], F32)
        const = place("const", [P, NCONST], F32)
        cols = place("cols", [P, L, NCOL], F32)
        rows = place("rows", [P, NROW], F32)
        ws = place("ws", [P, 4, 128], F32)
        mod = place("mod", [P, 48], F32)
        ccol = place("ccol", [P, KD], F32)
        cact = place("cact", [P, KD], F32)
        cA = place("cA", [P, 2, KD], F32)
        cG = place("cG", [P, 2, KD], F32)
        lbs = place("lbs", [P, L, 2, HEADS], F32)
        lbt = place("lbt", [P, 4, HEADS], F32)
        std = place("std", [P, 16], F32)
        rstd = place("rstd", [P, 16], F32)
        mv = place("mv", [P, NT, 2], F32)
        vstd = place("vstd", [P, 2, NT], F32)
        amx = place("amx", [P, 3, 4], F32)
        ars = place("ars", [P, 3, 4], F32)
        elast = place("elast", [P, 2, NCH], F32)
        bn = place("bn", [P, NT, 6], F32, R0 + 102 * KB)

        ident = const[:, K_ID:K_ID + P]
        ones = const[:, K_ONE:K_ONE + P]
        eps = const[:, K_EPS:K_EPS + 1]

        acc = [ctx.enter_context(nc.psum_tensor(f"acc{i}", [P, S], F32)) for i in range(4)]
        b4, b5, b6, b7 = [ctx.enter_context(nc.psum_tensor(f"bank{i}", [P, S], F32)) for i in range(4, 8)]
        small = [b4, b5, b6, b7]
        hbank = [b4, b5]

        const_in = sem("const_in")
        x_in = sem("x_in")
        pos_in = sem("pos_in")
        rows_in = sem("rows_in")
        ws_in = sem("ws_in")
        ada0_in = [sem(f"ada0_in{i}") for i in range(4)]
        stored = sem("stored")
        landed = [sem(f"landed{i}") for i in range(STAGES)]
        whi_ready = sem("whi_ready")
        wlo_ready = sem("wlo_ready")
        part_used = sem("part_used")
        ada_used = sem("ada_used")
        ada_summed = sem("ada_summed")
        tile_done = sem("tile_done")
        acc_free = [sem(f"acc_free{i}") for i in range(4)]
        f_ready = sem("f_ready")
        hi_ready = sem("hi_ready")
        lo_ready = sem("lo_ready")
        x_ready = sem("x_ready")
        x_ready_pool = sem("x_ready_pool")
        y_scaled = sem("y_scaled")
        sq_ready = sem("sq_ready")
        ss_done = sem("ss_done")
        std_ready = sem("std_ready")
        diag_ready = sem("diag_ready")
        bc_ready = sem("bc_ready")
        cact_ready = sem("cact_ready")
        ada0_done = sem("ada0_done")
        mod0_read = sem("mod0_read")
        ang_ready = sem("ang_ready")
        trig_ready = sem("trig_ready")
        lb_a = sem("lb_a")
        lb_b = sem("lb_b")
        dve_own = sem("dve_own")
        act_own = sem("act_own")
        kd_ready = sem("kd_ready")
        ws_ready = sem("ws_ready")
        vvar = sem("vvar")
        vsd = sem("vsd")
        vn_ready = sem("vn_ready")
        sgu_done = sem("sgu_done")
        forget_ready = sem("forget_ready")
        log_ready = sem("log_ready")
        diff_ready = sem("diff_ready")
        exp_ready = sem("exp_ready")
        kdiff = sem("kdiff")
        kexp = sem("kexp")
        kt_ready = sem("kt_ready")
        qk_ready = sem("qk_ready")
        khT_done = sem("khT_done")
        khT_copied = sem("khT_copied")
        ds_done = sem("ds_done")
        state_ready = sem("state_ready")
        a_done = sem("a_done")
        masked = sem("masked")
        o_done = sem("o_done")
        o_copied = sem("o_copied")
        osq_ready = sem("osq_ready")
        odiag = sem("odiag")
        obc = sem("obc")
        qk_done = sem("qk_done")
        max_ready = sem("max_ready")
        p_exp = sem("p_exp")
        p_ready = sem("p_ready")
        pt_done = sem("pt_done")
        pt_copied_a = sem("pt_copied_a")
        pt_copied_v = sem("pt_copied_v")
        pv_done = sem("pv_done")
        ybh_ready = sem("ybh_ready")
        yb_ready = sem("yb_ready")
        conv0 = sem("conv0")
        silu_done = sem("silu_done")

        numbers = {}
        for l in range(L):
            for t in TILES:
                if t[0] != "ada" or t[1] < ada_tiles(l):
                    numbers[(l,) + t] = len(numbers)

        def tile(l, name, i):
            return numbers[(l, name, i)]

        def evacuated(eng, t):
            eng.wait_ge(acc_free[t % 4], t // 4 + 1)

        def block_is_used(eng, lb):
            l, b = lb
            if b in PART_AT:
                eng.wait_ge(part_used, len(PART_AT) * l + PART_AT[b] + 1)
            else:
                eng.wait_ge(tile_done, tile(l, *last_tile(b)) + 1)

        def x_updated(eng, n, k):
            if k in POOL_K:
                eng.wait_ge(x_ready_pool, len(POOL_K) * (n - 1) + POOL_K.index(k) + 1)
            else:
                own = [i for i in range(KD) if i not in POOL_K]
                eng.wait_ge(x_ready, len(own) * (n - 1) + own.index(k) + 1)

        block = ctx.enter_context(nc.Block())

        def block_src(item):
            if item[0] == "ada":
                return ada_d[item[1], item[2]], BLK
            l, (name, i) = item
            if name == "gate":
                return win_d[l, NFRONT + i], BLK
            if name == "proj":
                return proj_d[l, i], BLK
            if name == "wout":
                return wout_d[l, i], BLK
            if name == "w1":
                return w1_d[l, i], BLK
            if name == "w2":
                k0 = 8 * (i % 3)
                n = min(8, NPAIR - k0) * P
                return w2_d[l, i // 3, :, k0 * P:k0 * P + n], n
            return win_d[l, BLOCK_AT[(name, i)]], BLK

        def modcols(part):
            return mod[:, 8 * part:8 * part + 8]

        @block.sync
        def _(sp):
            sp.dma_start(ccol[:, :], c_d).then_inc(const_in, 16)
            sp.dma_start(const[:, :], const_d).then_inc(const_in, 16)
            sp.dma_start(cols[:, :, :], cols_d).then_inc(const_in, 16)
            for i in range(4):
                sp.dma_start(ada0[:, 4 * i:4 * i + 4, :], ada_d[0, 4 * i:4 * i + 4].rearrange("c p n -> p c n")).then_inc(ada0_in[i], 16)
                if i == 1:
                    sp.dma_start(x[:, :, :], xT_d).then_inc(x_in, 16)
            for i, b in enumerate(stream):
                if i >= STAGES:
                    old = stream[i - STAGES]
                    if old[0] == "ada":
                        sp.wait_ge(ada_used, ada_no[old] + 1)
                    else:
                        sp.wait_ge(wlo_ready, kinds.index(old) + 1)
                src, n = block_src(b)
                sp.dma_start(stage[:, i % STAGES, 0:n], src).then_inc(landed[i % STAGES], 16)
            for k in range(KD):
                x_updated(sp, 2 * L, k)
                sp.dma_start(out_d[:, k, :], x[:, k, :]).then_inc(stored, 16)
            sp.wait_ge(stored, 16 * KD)

        @block.gpsimd
        def _(pool):
            pool.dma_start(tmp[3][:, :].bitcast(I32), pos_d.partition_broadcast(P)).then_inc(pos_in, 16)

            def layer_rows(l):
                if l:
                    pool.wait_ge(tile_done, tile(l - 1, "w2", 7) + 1)
                else:
                    pool.wait_ge(ada0_done, 1)
                pool.dma_start(lnrow[:, :, :], ln_d[l].partition_broadcast(P)).then_inc(rows_in, 16)
                pool.dma_start(rows[:, :], rows_d[l].partition_broadcast(P)).then_inc(rows_in, 16)
                pool.dma_start(ws[:, :, :], ws_d[l]).then_inc(ws_in, 16)
                pool.wait_ge(ws_in, 16 * (l + 1))
                nc.gpsimd.affine_select(out=ws[:, :, :], in_=ws[:, :, :], compare_op=ALU.is_ge, fill=0.0, base=0,
                                        pattern=[[0, 4], [1, 128]], channel_multiplier=-1).then_inc(ws_ready, 1)

            def update_x(n):
                for i, k in enumerate(POOL_K):
                    pool.wait_ge(y_scaled, len(POOL_K) * (n - 1) + i + 1)
                    nc.gpsimd.tensor_tensor(x[:, k, :], x[:, k, :], y[:, k, :], ALU.add).then_inc(x_ready_pool, 1)

            layer_rows(0)
            for i, item in enumerate(kinds):
                l, b = item
                n = block_src(item)[1]
                slot = at[item] % STAGES
                pool.wait_ge(whi_ready, i + 1)
                if i >= RING:
                    block_is_used(pool, kinds[i - RING])
                nc.gpsimd.tensor_tensor(wlo[:, i % RING, 0:n], stage[:, slot, 0:n], whi[:, i % RING, 0:n].bitcast(F32),
                                        ALU.subtract).then_inc(wlo_ready, 1)
                if b == ("wout", 7):
                    update_x(2 * l + 1)
                if b == ("w2", 23):
                    update_x(2 * l + 2)
                    if l + 1 < L:
                        layer_rows(l + 1)

        @block.scalar
        def _(act):
            A = nc.scalar.activation
            own = [0]
            done = [0]

            def chain(ins):
                ins.then_inc(act_own, 1)
                own[0] += 1

            def sync():
                act.wait_ge(act_own, own[0])

            def weights(l, b, ahead=0):
                upto = NBLOCK * l + BLOCK_AT[b] + ahead
                while done[0] <= min(upto, len(kinds) - 1):
                    i = done[0]
                    n = block_src(kinds[i])[1]
                    slot = at[kinds[i]] % STAGES
                    act.wait_ge(landed[slot], 16 * (at[kinds[i]] // STAGES + 1))
                    if i >= RING:
                        block_is_used(act, kinds[i - RING])
                    A(whi[:, i % RING, 0:n], stage[:, slot, 0:n], ACT.Copy).then_inc(whi_ready, 1)
                    done[0] += 1

            def squares(n, k, src):
                if 8 * n + k >= 2:
                    act.wait_ge(ss_done, 8 * n + k - 1)
                A(sq[k % 2][:, :], src, ACT.Square).then_inc(sq_ready, 1)

            def deviation(n):
                act.wait_ge(ss_done, 8 * n + 8)
                A(std[:, 0:NT], b6[:, 0:NT], ACT.Sqrt, bias=eps, scale=1.0 / D).then_inc(std_ready, 1)

            def pre_norm(l, which):
                n = 4 * l + 2 * which
                for k in range(KD):
                    if n:
                        x_updated(act, 2 * l + which, k)
                    elif k == 0:
                        act.wait_ge(x_in, 16)
                    squares(n, k, x[:, k, :])
                deviation(n)
                weights(l, ("w1", 1) if which else ("hf", 1))
                name = "h2" if which else "h1"
                shift = modcols(3 if which else 0)
                for k in range(KD):
                    act.wait_ge(f_ready, split(l, name, k) + 1)
                    A(hh[:, k, :], hf32[:, k, :], ACT.Identity, bias=shift[:, k:k + 1]).then_inc(hi_ready, 1)

            def take(l, name, i):
                if (name, i) in PART_AT or name == "aq":
                    return
                if name in ("gv", "hi"):
                    for j in range(2):
                        t = tile(l, name, i - 1 + j)
                        act.wait_ge(tile_done, t + 1)
                        dst = gvt if name == "gv" else itok
                        half = 256 * (i // 2)
                        A(dst[:, 2 * j:2 * j + 2, half:half + 256], acc[t % 4][:, :].rearrange("p (t n) -> p t n", t=2),
                          ACT.Gelu_apprx_tanh if name == "gv" else ACT.Copy).then_inc(acc_free[t % 4], 1)
                    return
                t = tile(l, name, i)
                a = acc[t % 4][:, :]
                if (name, i) == ("kv", 0):
                    evacuated(act, t)
                    for j in range(2):
                        A(kd[64 - 64 * j:128 - 64 * j, j, :], kd[64 * j:64 * j + 64, j, :], ACT.Copy).then_inc(kd_ready, 1)
                    return
                act.wait_ge(tile_done, t + 1)
                if name == "hf":
                    chain(A(bb[:, i, :], a, ACT.Sigmoid))
                    ins = A(hk[:, i, :], a, ACT.Sigmoid, scale=-1.0)
                elif name == "hq":
                    ins = A(hqs[:, i, :], a, ACT.Silu)
                elif name == "hg":
                    ins = A(hgs[:, i, :], a, ACT.Silu)
                elif name == "gu":
                    ins = A(gut[:, i, :], a, ACT.Gelu_apprx_tanh)
                else:
                    ins = A(vt[:, :, :], a.rearrange("p (t n) -> p t n", t=NT), ACT.Copy)
                ins.then_inc(acc_free[t % 4], 1)

            def hg_step(l, step):
                h, half = step // 2, step % 2
                q = HEADS * l + h
                t0, t1, t2 = hgset[h % 2]
                if half == 0:
                    act.wait_ge(forget_ready, q + 1)
                    A(t0[:, :], bb[:, h, :], ACT.Ln).then_inc(log_ready, 1)
                    act.wait_ge(diff_ready, q + 1)
                    chain(A(t0[:, :], t0[:, :], ACT.Exp))
                    chain(A(t1[:, :], bb[:, h, :], ACT.Exp))
                    chain(A(elast[:, h % 2, :], bb[:, h, :].rearrange("p (c t) -> p c t", t=CH)[:, :, CH - 1], ACT.Exp))
                    A(t2[:, :], t2[:, :], ACT.Exp).then_inc(exp_ready, 1)
                else:
                    act.wait_ge(khT_done, q + 1)
                    A(khT[:, :, :], b6[:, :].rearrange("p (t n) -> p t n", t=NT), ACT.Copy).then_inc(khT_copied, 1)
                for i in range(4 * half, 4 * half + 4):
                    act.wait_ge(kdiff, NSUB * q + i + 1)
                    v = kt[:, i % KTS, :, 0:SUB * (i + 1)]
                    A(v, v, ACT.Exp).then_inc(kexp, 1)

            def hg_output(l, h):
                q = HEADS * l + h
                act.wait_ge(o_done, q + 1)
                A(bb[:, h, :], hbank[h % 2][:, :], ACT.Copy).then_inc(o_copied, 1)

            def attention_exp(l, u):
                a = 8 * l + u
                w = 256 if u // 2 else 128
                act.wait_ge(max_ready, a + 1)
                for i in range(4):
                    chain(A(pm[:, i, 0:w], pm[:, i, 0:w], ACT.Exp, bias=amx[:, 1, i:i + 1], accum_out=ars[:, 0, i:i + 1]))
                A(ars[:, 1, :], amx[:, 2, :], ACT.Exp).then_inc(p_exp, 1)

            act.wait_ge(const_in, 48)
            A(cact[:, :], ccol[:, :], ACT.Silu).then_inc(cact_ready, 1)
            act.wait_ge(lb_a, 1)
            A(lbt[:, 0:2, :], lbt[:, 0:2, :], ACT.Exp).then_inc(lb_b, 1)
            act.wait_ge(ang_ready, 1)
            A(cosb[:, :], tmp[0][:, :], ACT.Sin).then_inc(trig_ready, 1)
            A(sinb[:, :], tmp[1][:, :], ACT.Sin).then_inc(trig_ready, 1)

            for l in range(L):
                pre_norm(l, 0)
                for b in BLOCKS[:NFRONT]:
                    weights(l, b, 2)
                    if b in HG_BLOCKS:
                        i = HG_BLOCKS.index(b)
                        if i % 2 == 0 and i // 2 < 2 * HEADS:
                            hg_step(l, i // 2)
                        if i % 4 == 1 and 9 <= i <= 17:
                            hg_output(l, (i - 9) // 4)
                    take(l, *b)
                    if b == ("gu", 3):
                        act.wait_ge(vvar, l + 1)
                        A(vstd[:, 0, :], mv[:, :, 1], ACT.Sqrt, bias=eps).then_inc(vsd, 1)
                hg_output(l, 3)
                for h in range(HEADS):
                    act.wait_ge(o_copied, HEADS * (l + 1))
                    A(osq[h][:, :], bb[:, h, :], ACT.Square).then_inc(osq_ready, 1)
                for g in range(4):
                    act.wait_ge(f_ready, split(l, "ya", g) + 1)
                    A(yah[:, g, :], tmp[2 + g % 2][:, :], ACT.Copy).then_inc(hi_ready, 1)
                for s in range(NSTEP):
                    br, mp = s // NMP, s % NMP
                    u = s - 1
                    if 0 <= u < 8:
                        attention_exp(l, u)
                    for j in range(2):
                        weights(l, ("gate", 2 * s + j), 2)
                        t = tile(l, "gate", 2 * s + j)
                        act.wait_ge(tile_done, t + 1)
                        if s >= 2:
                            evacuated(act, tile(l, "proj", 2 * s - 4 + j))
                        A(gates[:, (2 * s + j) % 4, :], acc[t % 4][:, :], ACT.Sigmoid).then_inc(acc_free[t % 4], 1)
                        if s == 0 and j == 0:
                            t = tile(l, "oss", 0)
                            act.wait_ge(tile_done, t + 1)
                            A(std[:, :], acc[t % 4][:, 0:16], ACT.Sqrt, bias=eps, scale=1.0 / 128).then_inc(acc_free[t % 4], 1)
                            for h in range(HEADS):
                                act.wait_ge(f_ready, split(l, "yc", h) + 1)
                                A(ych[:, h, :], tmp[h % 2][:, :], ACT.Copy).then_inc(hi_ready, 1)
                        if 0 <= u < 8 and j == 0 and u // 2:
                            act.wait_ge(pt_done, 8 * l + u + 1)
                            A(pts[:, 0, :, :], b6[:, :].rearrange("p (t n) -> p t n", t=4), ACT.Copy).then_inc(pt_copied_a, 1)
                        if 0 <= u < 8 and j == 1:
                            act.wait_ge(pv_done, 8 * l + u + 1)
                            v = slice(P * (u // 2), P * (u // 2) + P)
                            A(ybh[:, 2 * (u % 2):2 * (u % 2) + 2, v],
                              b6[:, 0:256].rearrange("p (t n) -> p t n", t=2), ACT.Copy).then_inc(ybh_ready, 1)
                    weights(l, ("proj", s), 2)
                    if br == 2:
                        for m in (2 * mp, 2 * mp + 1):
                            act.wait_ge(f_ready, split(l, "mg", m) + 1)
                            A(mgh[:, m, :], tmp[m % 2][:, :], ACT.Copy).then_inc(hi_ready, 1)
                n = 4 * l + 1
                for m in range(KD):
                    weights(l, ("wout", m), 2)
                    t = tile(l, "wout", m)
                    act.wait_ge(tile_done, t + 1)
                    squares(n, m, acc[t % 4][:, :])
                deviation(n)
                pre_norm(l, 1)
                for p in range(NPAIR):
                    tg, tv = tile(l, "w1", 2 * p), tile(l, "w1", 2 * p + 1)
                    for j, t in enumerate((tg, tv)):
                        weights(l, ("w1", 2 * p + j), 2)
                        c0 = C_CONV + 8 * p + 4 * j
                        act.wait_ge(tile_done, t + 1)
                        if p >= 2 and j == 0:
                            act.wait_ge(lo_ready, split(l, "ff", p - 2) + 1)
                        A(tmp[2 * (p % 2) + j][:, :], acc[t % 4][:, :], ACT.Identity, bias=cols[:, l, c0 + 3:c0 + 4],
                          scale=cols[:, l, c0 + 2:c0 + 3]).then_inc(conv0, 1)
                    evacuated(act, tv)
                    A(tmp[2 * (p % 2)][:, :], tmp[2 * (p % 2)][:, :], ACT.Silu).then_inc(silu_done, 1)
                    act.wait_ge(f_ready, split(l, "ff", p) + 1)
                    A(acth[:, p, :], tmp[2 * (p % 2)][:, :], ACT.Copy).then_inc(hi_ready, 1)
                n = 4 * l + 3
                for m in range(KD):
                    weights(l, ("w2", 3 * m))
                    weights(l, ("w2", 3 * m + 1))
                    weights(l, ("w2", 3 * m + 2), 2)
                    t = tile(l, "w2", m)
                    act.wait_ge(tile_done, t + 1)
                    squares(n, m, acc[t % 4][:, :])
                deviation(n)

        @block.vector
        def _(dve):
            V = nc.vector
            own = [0]

            def chain(ins):
                ins.then_inc(dve_own, 1)
                own[0] += 1

            def sync():
                dve.wait_ge(dve_own, own[0])

            def free(t, ins):
                ins.then_inc(acc_free[t % 4], 1)

            def lo(s, dst, src, hi, shift=None):
                dve.wait_ge(hi_ready, s + 1)
                if shift is None:
                    V.tensor_tensor(dst, src, hi.bitcast(F32), ALU.subtract).then_inc(lo_ready, 1)
                else:
                    V.scalar_tensor_tensor(out=dst, in0=src, scalar=shift, in1=hi.bitcast(F32), op0=ALU.add,
                                           op1=ALU.subtract).then_inc(lo_ready, 1)

            def ada_units(l, b):
                for x_l, c in ada_after(l, b):
                    item = ("ada", x_l, c)
                    i = at[item]
                    dve.wait_ge(landed[i % STAGES], 16 * (i // STAGES + 1))
                    w = stage[:, i % STAGES, :].rearrange("p (k n) -> p k n", k=KD)
                    chain(V.tensor_tensor(w, w, cact[:, :].unsqueeze(2).broadcast_to([P, KD, P]), ALU.mult))
                    n = ada_no[item]
                    if n % 4 == 0 and n >= 4:
                        dve.wait_ge(tile_done, ada_tile_of(n // 4 - 1) + 1)
                    sync()
                    V.tensor_reduce(ada_sum[:, n % 4, :], w.rearrange("p k n -> p n k"), AX_X, ALU.add).then_inc(ada_used, 1)

            def ada_tile_of(i):
                return sorted(v for k, v in numbers.items() if k[1] == "ada")[i]

            def take_ada(l, i):
                t = tile(l, "ada", i)
                layer, c0 = (l, 16 + 4 * i) if i < 8 else (l + 1, 4 * (i - 8))
                dve.wait_ge(tile_done, t + 1)
                free(t, V.tensor_tensor(mod[:, c0:c0 + 4], acc[t % 4][:, 0:4], cols[:, layer, C_ADA + c0:C_ADA + c0 + 4], ALU.add))

            def broadcast_rstd(n):
                dve.wait_ge(std_ready, n + 1)
                chain(V.reciprocal(rstd[:, 0:NT], std[:, 0:NT]))
                sync()
                V.tensor_tensor(tmp[3][:, :].rearrange("p (t n) -> p t n", t=NT),
                                ident.unsqueeze(1).broadcast_to([P, NT, P]),
                                rstd[:, 0:NT].unsqueeze(2).broadcast_to([P, NT, P]), ALU.mult).then_inc(diag_ready, 1)

            def pre_norm(l, which):
                n = 4 * l + 2 * which
                g0 = C_NFPRE if which else C_NMPRE
                if l or which:
                    last = tile(l, "ada", 5) if which else tile(l - 1, "ada", 11)
                    evacuated(dve, last)
                chain(V.scalar_tensor_tensor(out=cA[:, which, :], in0=modcols(4 if which else 1), scalar=1.0,
                                             in1=cols[:, l, g0:g0 + 8], op0=ALU.add, op1=ALU.mult))
                broadcast_rstd(n)
                name = "h2" if which else "h1"
                shift = modcols(3 if which else 0)
                dve.wait_ge(bc_ready, n + 1)
                sync()
                for k in range(KD):
                    V.scalar_tensor_tensor(out=hf32[:, k, :], in0=x[:, k, :], scalar=cA[:, which, k:k + 1],
                                           in1=b6[:, :], op0=ALU.mult, op1=ALU.mult).then_inc(f_ready, 1)
                for k in range(KD):
                    lo(split(l, name, k), hl[:, k, :], hf32[:, k, :], hh[:, k, :], shift[:, k:k + 1])

            def take_y(l, name, m):
                t = tile(l, name, m)
                n = 4 * l + (1 if name == "wout" else 3)
                dve.wait_ge(sq_ready, 8 * n + m + 1)
                free(t, V.tensor_copy(y[:, m, :], acc[t % 4][:, :]))

            def post_norm(l, which):
                n = 4 * l + 1 + 2 * which
                g0 = C_NFPOST if which else C_NMPOST
                evacuated(dve, tile(l, "ada", 7 if which else 5))
                chain(V.tensor_tensor(cG[:, which, :], modcols(5 if which else 2), cols[:, l, g0:g0 + 8], ALU.mult))
                broadcast_rstd(n)
                dve.wait_ge(bc_ready, n + 1)
                sync()
                evacuated(dve, tile(l, "w2" if which else "wout", KD - 1))
                for k in POOL_K + tuple(k for k in range(KD) if k not in POOL_K):
                    ins = V.scalar_tensor_tensor(out=y[:, k, :], in0=y[:, k, :], scalar=cG[:, which, k:k + 1],
                                                 in1=b6[:, :], op0=ALU.mult, op1=ALU.mult)
                    if k in POOL_K:
                        ins.then_inc(y_scaled, 1)
                    else:
                        chain(ins)
                        sync()
                        V.tensor_tensor(x[:, k, :], x[:, k, :], y[:, k, :], ALU.add).then_inc(x_ready, 1)

            def rotate(t, parts, before=None):
                a = acc[t % 4]
                dve.wait_ge(tile_done, t + 1)
                for r, dst in parts:
                    chain(V.tensor_tensor(dst, a[r, :], cosb[r, :], ALU.mult))
                if before is not None:
                    evacuated(dve, before)
                for u in range(4):
                    w = u ^ 1
                    chain(V.tensor_tensor(tmp[3][32 * u:32 * u + 32, :], a[32 * w:32 * w + 32, :],
                                          sinb[32 * u:32 * u + 32, :], ALU.mult))
                sync()
                for i, (r, dst) in enumerate(parts):
                    ins = V.tensor_tensor(dst, dst, tmp[3][r, :], ALU.add)
                    if i < len(parts) - 1:
                        chain(ins)
                    else:
                        free(t, ins)

            def hg_step(l, step):
                h, half = step // 2, step % 2
                q = HEADS * l + h
                t0, t1, t2 = hgset[h % 2]
                b3 = bb[:, h, :].rearrange("p (g t) -> p g t", t=SUB)
                bc = bb[:, h, :].rearrange("p (c t) -> p c t", t=CH)
                kc = hk[:, h, :].rearrange("p (c t) -> p c t", t=CH)

                def key_diff(i):
                    n = SUB * (i + 1)
                    wide = 0
                    if i >= KTS:
                        dve.wait_ge(a_done, NSUB * q + i - KTS + 1)
                    elif h:
                        old = i + KTS if i + KTS < NSUB else i
                        dve.wait_ge(a_done, NSUB * (q - 1) + old + 1)
                        wide = SUB * (old - i)
                    if wide:
                        chain(V.memset(kt[:, i % KTS, :, n:n + wide], 0.0))
                    m = SUB * i + MID
                    V.tensor_tensor(kt[:, i % KTS, :, 0:n], bc[:, :, m:m + 1].broadcast_to([P, NCH, n]), bc[:, :, 0:n],
                                    ALU.subtract).then_inc(kdiff, 1)

                def key_tile(i):
                    n = SUB * (i + 1)
                    dve.wait_ge(kexp, NSUB * q + i + 1)
                    if i % 4 == 0:
                        sync()
                    v = kt[:, i % KTS, :, 0:n]
                    V.tensor_tensor(v, v, kc[:, :, 0:n], ALU.mult).then_inc(kt_ready, 1)

                if half == 0:
                    lb, lb1 = lbs[:, l, 0, h:h + 1], lbs[:, l, 1, h:h + 1]
                    chain(V.tensor_scalar(bb[:, h, :], bb[:, h, :], lb1, lb, ALU.mult, ALU.add))
                    chain(V.tensor_scalar(hk[:, h, :], hk[:, h, :], lb1, None, ALU.mult))
                    sync()
                    if h >= 2:
                        dve.wait_ge(o_done, q - 1)
                    V.tensor_scalar(bb[:, h, :], bb[:, h, :], MIN_FORGET, None, ALU.max).then_inc(forget_ready, 1)
                    dve.wait_ge(log_ready, q + 1)
                    for c in range(NCH):
                        v = slice(CH * c, CH * c + CH)
                        chain(V.tensor_tensor_scan(bb[:, h, v], t0[:, v], t0[:, v], 0.0, ALU.add, ALU.bypass))
                    sync()
                    chain(V.tensor_tensor(t0[:, :].rearrange("p (g t) -> p g t", t=SUB), b3,
                                          b3[:, :, MID:MID + 1].broadcast_to([P, S // SUB, SUB]), ALU.subtract))
                    V.tensor_tensor(t2[:, :].rearrange("p (c t) -> p c t", t=CH),
                                    bc[:, :, CH - 1:CH].broadcast_to([P, NCH, CH]), bc, ALU.subtract).then_inc(diff_ready, 1)
                    for i in range(4):
                        key_diff(i)
                    dve.wait_ge(exp_ready, q + 1)
                    V_ = V.scalar_tensor_tensor
                    chain(V_(out=t0[:, :], in0=hqs[:, h, :], scalar=HG_SCALE, in1=t0[:, :], op0=ALU.mult, op1=ALU.mult))
                    chain(V_(out=t1[:, :], in0=hqs[:, h, :], scalar=HG_SCALE, in1=t1[:, :], op0=ALU.mult, op1=ALU.mult))
                    sync()
                    V.tensor_tensor(t2[:, :], hk[:, h, :], t2[:, :], ALU.mult).then_inc(qk_ready, 1)
                    for i in range(4):
                        key_tile(i)
                else:
                    for i in range(4, NSUB):
                        key_diff(i)
                    for i in range(4, NSUB):
                        key_tile(i)

            def hg_states(l, h):
                q = HEADS * l + h
                dve.wait_ge(ds_done, q + 1)
                if h:
                    dve.wait_ge(o_done, q)
                for c in range(NCH - 1):
                    src = (b6 if c % 2 else b7)[:, P * (c // 2):P * (c // 2) + P]
                    if c == 0:
                        ins = V.tensor_copy(states[:, 0, :], src)
                    else:
                        ins = V.scalar_tensor_tensor(out=states[:, c, :], in0=states[:, c - 1, :],
                                                     scalar=elast[:, h % 2, c:c + 1], in1=src, op0=ALU.mult, op1=ALU.add)
                    if c < NCH - 2:
                        chain(ins)
                        sync()
                    else:
                        ins.then_inc(state_ready, 1)
                dve.wait_ge(a_done, NSUB * (q + 1))
                V.copy_predicated(asb[:, :].rearrange("p (c t) -> p c t", c=NT),
                                  const[:, K_HM:K_HM + P].bitcast(U32).unsqueeze(1).broadcast_to([P, NT, P]),
                                  hbank[h % 2][:, :].rearrange("p (c t) -> p c t", c=NT)).then_inc(masked, 1)

            def softmax_max(l, u):
                a, n, j = 8 * l + u, u // 2, u % 2
                w = 256 if n else 128
                mk = const[:, K_AM + 256 - w:K_AM + 256].unsqueeze(1).broadcast_to([P, 2, w])
                dve.wait_ge(qk_done, a + 1)
                if u:
                    dve.wait_ge(pt_done, a)
                for o in range(2):
                    chain(V.scalar_tensor_tensor(out=pm[:, o:4:2, 0:w], in0=small[o][:, 0:2 * w].rearrange("p (h k) -> p h k", h=2),
                                                 scalar=AT_SCALE, in1=mk, op0=ALU.mult, op1=ALU.add))
                sync()
                chain(V.tensor_reduce(amx[:, 0, :], pm[:, :, 0:w], AX_X, ALU.max))
                sync()
                sk = rows[:, R_SINK + 4 * j:R_SINK + 4 * j + 4]
                chain(V.tensor_tensor(amx[:, 0, :], amx[:, 0, :], sk, ALU.max))
                sync()
                chain(V.tensor_scalar(amx[:, 1, :], amx[:, 0, :], -1.0, None, ALU.mult))
                V.tensor_tensor(amx[:, 2, :], sk, amx[:, 0, :], ALU.subtract).then_inc(max_ready, 1)

            def softmax_norm(l, u):
                a = 8 * l + u
                w = 256 if u // 2 else 128
                dve.wait_ge(p_exp, a + 1)
                chain(V.tensor_tensor(ars[:, 2, :], ars[:, 0, :], ars[:, 1, :], ALU.add))
                sync()
                chain(V.reciprocal(ars[:, 2, :], ars[:, 2, :]))
                sync()
                V.tensor_tensor(pm[:, :, 0:w], pm[:, :, 0:w], ars[:, 2, :].unsqueeze(2).broadcast_to([P, 4, w]),
                                ALU.mult).then_inc(p_ready, 1)

            dve.wait_ge(const_in, 48)
            lg = [cols[:, l, C_LB:C_LB + HEADS] for l in range(L)]
            chain(V.tensor_tensor(lbt[:, 2, :], lg[0], lg[1], ALU.max))
            sync()
            chain(V.tensor_tensor(lbt[:, 0, :], lg[0], lbt[:, 2, :], ALU.subtract))
            V.tensor_tensor(lbt[:, 1, :], lg[1], lbt[:, 2, :], ALU.subtract).then_inc(lb_a, 1)
            dve.wait_ge(lb_b, 1)
            chain(V.tensor_tensor(lbt[:, 2, :], lbt[:, 0, :], lbt[:, 1, :], ALU.add))
            sync()
            chain(V.reciprocal(lbt[:, 3, :], lbt[:, 2, :]))
            sync()
            chain(V.tensor_tensor(lbt[:, 0, :], lbt[:, 0, :], lbt[:, 3, :], ALU.mult))
            chain(V.tensor_tensor(lbt[:, 1, :], lbt[:, 1, :], lbt[:, 3, :], ALU.mult))
            sync()
            chain(V.tensor_tensor(lbt[:, 2, :], lbt[:, 0, :], lbt[:, 1, :], ALU.add))
            chain(V.tensor_tensor(lbs[:, 0, 0, :], lbt[:, 0, :], lbt[:, 0, :], ALU.subtract))
            sync()
            chain(V.tensor_tensor(lbs[:, 1, 0, :], lbt[:, 2, :], lbt[:, 0, :], ALU.subtract))
            sync()
            chain(V.tensor_scalar(lbs[:, :, 1, :], lbs[:, :, 0, :], -1.0, 1.0, ALU.mult, ALU.add))
            dve.wait_ge(pos_in, 16)
            chain(V.tensor_copy(tmp[2][:, :], tmp[3][:, :].bitcast(I32)))
            sync()
            chain(V.tensor_scalar(tmp[2][:, :], tmp[2][:, :], const[:, K_INV:K_INV + 1], None, ALU.mult))
            sync()
            for dst, turn in ((0, 0.25), (1, 0.0)):
                r = tmp[dst][:, :]
                chain(V.tensor_scalar(tmp[3][:, :], tmp[2][:, :], 1.0 / TWO_PI, turn, ALU.mult, ALU.add))
                sync()
                chain(V.tensor_scalar(tmp[3][:, :], tmp[3][:, :], MAGIC, None, ALU.add))
                sync()
                chain(V.tensor_scalar(tmp[3][:, :], tmp[3][:, :], -MAGIC, None, ALU.add))
                sync()
                chain(V.scalar_tensor_tensor(out=r, in0=tmp[3][:, :], scalar=-TWO_PI_HI, in1=tmp[2][:, :], op0=ALU.mult, op1=ALU.add))
                sync()
                chain(V.scalar_tensor_tensor(out=r, in0=tmp[3][:, :], scalar=-TWO_PI_LO, in1=r, op0=ALU.mult, op1=ALU.add))
                sync()
                if turn:
                    chain(V.tensor_scalar(r, r, TWO_PI / 4, PI_SAFE, ALU.add, ALU.min))
                    sync()
                    chain(V.tensor_scalar(r, r, -PI_SAFE, None, ALU.max))
                else:
                    sync()
                    V.tensor_scalar(r, r, PI_SAFE, -PI_SAFE, ALU.min, ALU.max).then_inc(ang_ready, 1)
            dve.wait_ge(trig_ready, 2)
            chain(V.tensor_scalar(sinb[:, :], sinb[:, :], const[:, K_SGN:K_SGN + 1], None, ALU.mult))
            dve.wait_ge(ada0_done, 1)
            chain(V.tensor_tensor(mod[:, 0:16], b7[:, 0:16], cols[:, 0, C_ADA:C_ADA + 16], ALU.add))
            sync()

            for l in range(L):
                pre_norm(l, 0)
                chain(V.memset(kt[:, :, :, :], 0.0))
                chain(V.memset(asb[:, :], 0.0))
                evacuated(dve, tile(l, "hf", 3))
                evacuated(dve, tile(l, "hq", 3))
                sync()
                for step in range(2 * HEADS):
                    hg_step(l, step)
                    if step >= 2 and step % 2 == 0:
                        hg_states(l, step // 2 - 1)
                evacuated(dve, tile(l, "gv", 3))
                for i in range(NT):
                    chain(V.bn_stats(bn[:, i, :], gvt[:, i, :]))
                sync()
                for i in range(NT):
                    ins = V.bn_aggr(mv[:, i, :], bn[:, i, :])
                    if i < NT - 1:
                        chain(ins)
                ins.then_inc(vvar, 1)
                dve.wait_ge(vsd, l + 1)
                chain(V.reciprocal(vstd[:, 1, :], vstd[:, 0, :]))
                sync()
                for i in range(NT):
                    chain(V.tensor_scalar(gvt[:, i, :], gvt[:, i, :], mv[:, i, 0:1], vstd[:, 1, i:i + 1], ALU.subtract, ALU.mult))
                dve.wait_ge(rows_in, 32 * (l + 1))
                sync()
                for i in range(NT):
                    chain(V.tensor_tensor(gvt[:, i, :], gvt[:, i, :], lnrow[:, 0, :], ALU.mult))
                sync()
                for i in range(NT):
                    V.tensor_tensor(gvt[:, i, :], gvt[:, i, :], lnrow[:, 1, :], ALU.add).then_inc(vn_ready, 1)
                dve.wait_ge(vn_ready, NT * (l + 1))
                hg_states(l, HEADS - 1)
                rotate(tile(l, "kv", 0), [(slice(0, 64), kd[0:64, 0, :]), (slice(64, 128), kd[64:128, 1, :])])
                for i in range(4):
                    t = tile(l, "aq", i)
                    rotate(t, [(slice(0, 128), aqr[:, i, :])], t - 1 if i else tile(l, "kv", 0))
                bs = rows[:, R_BS:R_BS + 512].rearrange("p (g t) -> p g t", g=4)
                evacuated(dve, tile(l, "gu", 3))
                dve.wait_ge(o_done, HEADS * (l + 1))
                for g in range(5):
                    if g < 4:
                        dve.wait_ge(sgu_done, 4 * l + g + 1)
                        if g >= 2:
                            dve.wait_ge(lo_ready, split(l, "ya", g - 2) + 1)
                        u = (tmp[2], tmp[3])[g % 2]
                        chain(V.tensor_tensor(u[:, :].rearrange("p (c t) -> p c t", c=NT),
                                              small[g][:, :].rearrange("p (c t) -> p c t", c=NT),
                                              bs[:, g:g + 1, :].broadcast_to([P, NT, P]), ALU.add))
                        sync()
                        V.tensor_tensor(u[:, :], u[:, :], gut[:, g, :], ALU.mult).then_inc(f_ready, 1)
                    if g:
                        if g == 1:
                            dve.wait_ge(sgu_done, 4 * l + 4)
                        lo(split(l, "ya", g - 1), yal[:, g - 1, :], tmp[2 + (g - 1) % 2][:, :], yah[:, g - 1, :])
                evacuated(dve, tile(l, "oss", 0))
                chain(V.reciprocal(rstd[:, :], std[:, :]))
                sync()
                V.tensor_tensor(odg[:, :, :], ident.unsqueeze(1).broadcast_to([P, 16, P]),
                                rstd[:, :].unsqueeze(2).broadcast_to([P, 16, P]), ALU.mult).then_inc(odiag, 1)
                dve.wait_ge(lo_ready, split(l, "ya", 3) + 1)
                evacuated(dve, tile(l, "hg", 3))
                dve.wait_ge(obc, HEADS * (l + 1))
                for h in range(HEADS):
                    t2 = tmp[2 + h % 2]
                    chain(V.scalar_tensor_tensor(out=t2[:, :], in0=bb[:, h, :], scalar=cols[:, l, C_GN:C_GN + 1],
                                                 in1=small[h][:, :], op0=ALU.mult, op1=ALU.mult))
                    if h >= 2:
                        dve.wait_ge(lo_ready, split(l, "yc", h - 2) + 1)
                    sync()
                    V.tensor_tensor(tmp[h % 2][:, :], t2[:, :], hgs[:, h, :], ALU.mult).then_inc(f_ready, 1)
                    lo(split(l, "yc", h), ycl[:, h, :], tmp[h % 2][:, :], ych[:, h, :])
                dve.wait_ge(lo_ready, split(l, "yc", 3) + 1)
                for s in range(NSTEP):
                    br, mp = s // NMP, s % NMP
                    u = s - 1
                    if 0 <= u < 8:
                        softmax_max(l, u)
                    ada_units(l, ("gate", 2 * s))
                    if 0 <= u < 8:
                        softmax_norm(l, u)
                    if s >= 2 and s % 2 == 0:
                        take_ada(l, s // 2 - 1)
                    if 0 <= u < 8:
                        dve.wait_ge(pt_done, 8 * l + u + 1)
                        V.tensor_copy(pts[:, 1, :, :], b7[:, :].rearrange("p (t n) -> p t n", t=4)).then_inc(pt_copied_v, 1)
                    ada_units(l, ("gate", 2 * s + 1))
                    if 0 <= u < 8:
                        dve.wait_ge(ybh_ready, 8 * l + u + 1)
                        v = slice(P * (u // 2), P * (u // 2) + P)
                        jj = slice(2 * (u % 2), 2 * (u % 2) + 2)
                        V.tensor_tensor(ybl[:, jj, v], b6[:, 0:256].rearrange("p (t n) -> p t n", t=2),
                                        ybh[:, jj, v].bitcast(F32), ALU.subtract).then_inc(yb_ready, 1)
                    for j in range(2):
                        m = 2 * mp + j
                        t = tile(l, "proj", 2 * s + j)
                        evacuated(dve, tile(l, "gate", 2 * s + j))
                        dve.wait_ge(tile_done, t + 1)
                        if br == 0:
                            free(t, V.tensor_tensor(mg[:, m, :], acc[t % 4][:, :], gates[:, (2 * s + j) % 4, :], ALU.mult))
                            continue
                        T = tmp[2 + j]
                        sync()
                        free(t, V.tensor_tensor(T[:, :], acc[t % 4][:, :], gates[:, (2 * s + j) % 4, :], ALU.mult))
                        if br == 1:
                            evacuated(dve, t)
                            chain(V.tensor_tensor(mg[:, m, :], mg[:, m, :], T[:, :], ALU.add))
                        else:
                            evacuated(dve, t)
                            if m >= 2:
                                dve.wait_ge(lo_ready, split(l, "mg", m - 2) + 1)
                            V.tensor_tensor(tmp[j][:, :], mg[:, m, :], T[:, :], ALU.add).then_inc(f_ready, 1)
                    if br == 2:
                        for m in (2 * mp, 2 * mp + 1):
                            lo(split(l, "mg", m), mgl[:, m, :], tmp[m % 2][:, :], mgh[:, m, :])
                for m in range(KD):
                    take_y(l, "wout", m)
                    if m == 0:
                        take_ada(l, 5)
                post_norm(l, 0)
                pre_norm(l, 1)
                for p in range(NPAIR):
                    ada_units(l, ("w1", 2 * p))
                    ada_units(l, ("w1", 2 * p + 1))
                    for j in range(2):
                        t = tile(l, "w1", 2 * p + j)
                        c0 = C_CONV + 8 * p + 4 * j
                        a, T = acc[t % 4], tmp[2 * (p % 2) + j]
                        dve.wait_ge(conv0, 2 * (NPAIR * l + p) + j + 1)
                        chain(V.scalar_tensor_tensor(out=T[:, 1:S], in0=a[:, 0:S - 1], scalar=cols[:, l, c0 + 1:c0 + 2],
                                                     in1=T[:, 1:S], op0=ALU.mult, op1=ALU.add))
                        sync()
                        free(t, V.scalar_tensor_tensor(out=T[:, 2:S], in0=a[:, 0:S - 2], scalar=cols[:, l, c0:c0 + 1],
                                                       in1=T[:, 2:S], op0=ALU.mult, op1=ALU.add))
                    evacuated(dve, t)
                    T = tmp[2 * (p % 2)]
                    dve.wait_ge(silu_done, NPAIR * l + p + 1)
                    V.tensor_tensor(T[:, :], T[:, :], tmp[2 * (p % 2) + 1][:, :], ALU.mult).then_inc(f_ready, 1)
                    lo(split(l, "ff", p), actl[:, p, :], T[:, :], acth[:, p, :])
                    if p in ADA_PAIR and ADA_PAIR[p] < ada_tiles(l):
                        take_ada(l, ADA_PAIR[p])
                for m in range(KD):
                    take_y(l, "w2", m)
                post_norm(l, 1)

        @block.tensor
        def _(pe):
            MM = nc.tensor.matmul

            def sums_of_squares(n, k):
                pe.wait_ge(sq_ready, 8 * n + k + 1)
                if k == 0:
                    bank_read(n)
                for c in range(NT):
                    ins = MM(b6[:, c:c + 1], sq[k % 2][:, P * c:P * c + P], ones[:, 0:1], start=(k == 0 and c == 0),
                             stop=(k == KD - 1), skip_group_check=True)
                ins.then_inc(ss_done, 1)

            def bank_read(n):
                l, i = n // 4, n % 4
                if i in (1, 3):
                    pe.wait_ge(lo_ready, split(l, "h1" if i == 1 else "h2", 7) + 1)
                elif n:
                    x_updated(pe, 2 * l + (i == 2), 7)

            def broadcast(n):
                pe.wait_ge(diag_ready, n + 1)
                MM(b6[:, :], ones, tmp[3][:, :], start=True, stop=True).then_inc(bc_ready, 1)

            def weights_of(l, b):
                s = NBLOCK * l + BLOCK_AT[b]
                pe.wait_ge(whi_ready, s + 1)
                return s % RING, s + 1

            def acquire(t):
                if t >= 4:
                    pe.wait_ge(acc_free[t % 4], t // 4)
                return acc[t % 4]

            def three(out, s, views, xh, xl, first=True, last=True, hi_wait=None, lo_wait=None):
                slot, ready = s
                n = len(xh)
                for k in range(n):
                    if hi_wait:
                        hi_wait(k)
                    MM(out, views(whi, slot, k), xh[k], start=(first and k == 0), stop=False, skip_group_check=True)
                pe.wait_ge(wlo_ready, ready)
                for k in range(n):
                    MM(out, views(wlo, slot, k), xh[k], start=False, stop=False, skip_group_check=True)
                if lo_wait != "later":
                    return low_part(out, s, views, xl, last, lo_wait)

            def low_part(out, s, views, xl, last=True, lo_wait=None):
                n = len(xl)
                for k in range(n):
                    if lo_wait:
                        lo_wait(k)
                    ins = MM(out, views(whi, s[0], k), xl[k], start=False, stop=(last and k == n - 1), skip_group_check=True)
                return ins

            def whole(w, slot, k):
                return w[:, slot, P * k:P * k + P]

            def feature_tile(l, b, t, xh, xl, **kw):
                out = acquire(t)
                three(out[:, :], weights_of(l, b), whole, [xh[:, k, :] for k in range(KD)], [xl[:, k, :] for k in range(KD)],
                      **kw).then_inc(tile_done, 1)

            def first_two(l, names, norm):
                hs = [hh[:, k, :] for k in range(KD)]
                ls = [hl[:, k, :] for k in range(KD)]
                held = []
                for i, b in enumerate(names):
                    t = tile(l, *b)
                    out = acquire(t)
                    s = weights_of(l, b)
                    three(out[:, :], s, whole, hs, ls, lo_wait="later",
                          hi_wait=None if i else (lambda k: pe.wait_ge(hi_ready, split(l, norm, k) + 1)))
                    held.append((out, s))
                for i, (out, s) in enumerate(held):
                    low_part(out[:, :], s, whole, ls,
                             lo_wait=None if i else (lambda k: pe.wait_ge(lo_ready, split(l, norm, k) + 1))).then_inc(tile_done, 1)

            def token_half(l, name, i):
                slot, ready = weights_of(l, (name, i))
                pe.wait_ge(wlo_ready, ready)
                k0 = 4 * (i % 2)
                for j in range(2):
                    t = tile(l, name, 2 * (i // 2) + j)
                    out = acquire(t) if i % 2 == 0 else acc[t % 4]
                    for u in range(2):
                        v = slice(P * (2 * j + u), P * (2 * j + u) + P)
                        o = out[:, 256 * u:256 * u + 256]
                        for k in range(4):
                            wh = whi[:, slot, 256 * k:256 * k + 256]
                            wl = wlo[:, slot, 256 * k:256 * k + 256]
                            MM(o, hh[:, k0 + k, v], wh, start=(i % 2 == 0 and u == 0 and k == 0), stop=False, skip_group_check=True)
                            MM(o, hh[:, k0 + k, v], wl, start=False, stop=False, skip_group_check=True)
                            ins = MM(o, hl[:, k0 + k, v], wh, start=False, stop=(i % 2 == 1 and k == 3), skip_group_check=True)
                    if i % 2:
                        ins.then_inc(tile_done, 1)
                if i % 2 == 0:
                    ins.then_inc(part_used, 1)

            def values(l):
                t = tile(l, "kv", 1)
                out = acquire(t)
                slot, ready = weights_of(l, ("kv", 1))
                pe.wait_ge(wlo_ready, ready)
                for u in range(NT):
                    v = slice(P * u, P * u + P)
                    for k in range(KD):
                        wh, wl = whole(whi, slot, k), whole(wlo, slot, k)
                        MM(out[:, v], hh[:, k, v], wh, start=(k == 0), stop=False, skip_group_check=True)
                        MM(out[:, v], hh[:, k, v], wl, start=False, stop=False, skip_group_check=True)
                        ins = MM(out[:, v], hl[:, k, v], wh, start=False, stop=(k == KD - 1), skip_group_check=True)
                ins.then_inc(tile_done, 1)

            def hg_step(l, step):
                h, half = step // 2, step % 2
                q = HEADS * l + h
                hv = slice(P * h, P * h + P)
                t0, t1, t2 = hgset[h % 2]
                if half == 0:
                    pe.wait_ge(qk_ready, q + 1)
                    if h:
                        pe.wait_ge(state_ready, q)
                    for c in range(NT):
                        ins = nc.tensor.transpose(b6[:, P * c:P * c + P], t2[:, P * c:P * c + P], ident)
                    ins.then_inc(khT_done, 1)
                    if h >= 2:
                        pe.wait_ge(o_copied, q - 1)
                else:
                    if h:
                        hg_out(l, h - 1)
                    else:
                        evacuated(pe, tile(l, "hi", 2))
                        evacuated(pe, tile(l, "hi", 3))
                    pe.wait_ge(khT_copied, q + 1)
                    for c in range(NCH - 1):
                        r = slice(CH * (c % 2), CH * (c % 2) + CH)
                        o = (b6 if c % 2 else b7)[:, P * (c // 2):P * (c // 2) + P]
                        ins = MM(o, khT[r, c // 2, :], itok[r, c // 2, hv], start=True, stop=True)
                    ins.then_inc(ds_done, 1)
                q4 = t0[:, :].rearrange("p (r c t) -> p r c t", r=NT, c=2)
                o4 = hbank[h % 2][:, :].rearrange("p (r c t) -> p r c t", r=NT, c=2)
                for i in range(4 * half, 4 * half + 4):
                    pe.wait_ge(kt_ready, NSUB * q + i + 1)
                    v = slice(SUB * i, SUB * i + SUB)
                    for r in range(NT):
                        ins = MM(o4[:, r, :, v], kt[:, i % KTS, 2 * r:2 * r + 2, :], q4[:, r, :, v],
                                 start=(i == 0 and r == 0), stop=True, skip_group_check=True)
                    ins.then_inc(a_done, 1)

            def hg_out(l, h):
                q = HEADS * l + h
                hv = slice(P * h, P * h + P)
                pe.wait_ge(state_ready, q + 1)
                pe.wait_ge(masked, q + 1)
                o = hbank[h % 2]
                for r in range(NT):
                    MM(o[:, P * r:P * r + P], itok[:, r, hv], asb[:, P * r:P * r + P], start=True, stop=False,
                       skip_group_check=True)
                    for c in (2 * r, 2 * r + 1):
                        if c:
                            ins = MM(o[:, CH * c:CH * c + CH], states[:, c - 1, :], hgset[h % 2][1][:, CH * c:CH * c + CH],
                                     start=False, stop=True, skip_group_check=True)
                ins.then_inc(o_done, 1)

            def scores(l, u):
                a, n, j = 8 * l + u, u // 2, u % 2
                w = 256 if n else 128
                if u:
                    pe.wait_ge(max_ready, a)
                for i in range(4):
                    h = 4 * j + i
                    r = slice(64 * (h % 2), 64 * (h % 2) + 64)
                    ins = MM(small[i % 2][:, w * (i // 2):w * (i // 2) + w], aqr[r, h // 2, P * n:P * n + P],
                             kd[r, j, P * (n + 1) - w:P * (n + 1)], start=True, stop=True)
                ins.then_inc(qk_done, 1)

            def turn(l, u):
                a, n = 8 * l + u, u // 2
                pe.wait_ge(p_ready, a + 1)
                if u:
                    pe.wait_ge(yb_ready, a)
                for half in range(0 if n else 1, 2):
                    o = 128 * half if n else 0
                    for i in range(4):
                        ins = nc.tensor.transpose((b7 if half else b6)[:, P * i:P * i + P], pm[:, i, o:o + P], ident)
                ins.then_inc(pt_done, 1)

            def attend(l, u):
                a, n, j = 8 * l + u, u // 2, u % 2
                if n:
                    pe.wait_ge(pt_copied_a, 6 * l + u - 1)
                pe.wait_ge(pt_copied_v, a + 1)
                for i in range(4):
                    o = b6[64 * (i % 2):64 * (i % 2) + 64, P * (i // 2):P * (i // 2) + P]
                    for half in range(0 if n else 1, 2):
                        ins = MM(o, vt[:, n - 1 + half, 64 * j:64 * j + 64], pts[:, half, i, :],
                                 start=(half == 0 or not n), stop=(half == 1), skip_group_check=True)
                ins.then_inc(pv_done, 1)

            done_adas = [0]

            def ada_tile(l, i):
                t = tile(l, "ada", i)
                out = acquire(t)
                done_adas[0] += 4
                pe.wait_ge(ada_used, done_adas[0])
                for c in range(4):
                    ins = MM(out[:, c:c + 1], ada_sum[:, c, :], ones[:, 0:1], start=True, stop=True)
                ins.then_inc(tile_done, 1)

            pe.wait_ge(const_in, 48)
            pe.wait_ge(cact_ready, 1)
            for c in range(16):
                if c % 4 == 0:
                    pe.wait_ge(ada0_in[c // 4], 16)
                for k in range(KD):
                    ins = MM(b7[:, c:c + 1], ada0[:, c, P * k:P * k + P], cact[:, k:k + 1], start=(k == 0), stop=(k == KD - 1),
                             skip_group_check=True)
                if c == 7:
                    for k in range(KD):
                        sums_of_squares(0, k)
            ins.then_inc(ada0_done, 1)

            for l in range(L):
                if l:
                    for k in range(KD):
                        sums_of_squares(4 * l, k)
                broadcast(4 * l)
                first_two(l, [("hf", 0), ("hf", 1)], "h1")
                for b in BLOCKS[2:NFRONT]:
                    name, i = b
                    if name in ("hi", "gv"):
                        token_half(l, name, i)
                    elif b == ("kv", 1):
                        values(l)
                    else:
                        feature_tile(l, b, tile(l, name, i), hh, hl)
                    if b in HG_BLOCKS:
                        i = HG_BLOCKS.index(b)
                        if i >= 2 and i % 2 == 0 and i // 2 - 1 < 2 * HEADS:
                            hg_step(l, i // 2 - 1)
                hg_out(l, HEADS - 1)
                pe.wait_ge(vn_ready, NT * (l + 1))
                pe.wait_ge(ws_ready, l + 1)
                for g in range(4):
                    if g < 2:
                        pe.wait_ge(o_copied, HEADS * (l + 1) - (g == 0))
                    for c in range(NT):
                        ins = MM(small[g][:, P * c:P * c + P], gvt[:, c, P * g:P * g + P], ws[:, g, :], start=True, stop=True)
                    ins.then_inc(sgu_done, 1)
                for s in range(NSTEP):
                    br, mp = s // NMP, s % NMP
                    u = s - 1
                    if s >= 2 and s % 2 == 0:
                        ada_tile(l, s // 2 - 1)
                    feature_tile(l, ("gate", 2 * s), tile(l, "gate", 2 * s), hh, hl)
                    if s == 0:
                        t = tile(l, "oss", 0)
                        out = acquire(t)
                        for h in range(HEADS):
                            pe.wait_ge(osq_ready, HEADS * l + h + 1)
                            for c in range(NT):
                                ins = MM(out[:, 4 * h + c:4 * h + c + 1], osq[h][:, P * c:P * c + P], ones[:, 0:1],
                                         start=True, stop=True)
                        ins.then_inc(tile_done, 1)
                    if 0 <= u < 8:
                        turn(l, u)
                    feature_tile(l, ("gate", 2 * s + 1), tile(l, "gate", 2 * s + 1), hh, hl)
                    if s == 0:
                        pe.wait_ge(odiag, l + 1)
                        for h in range(HEADS):
                            MM(small[h][:, :], ones, odg[:, 4 * h:4 * h + 4, :], start=True, stop=True).then_inc(obc, 1)
                    if 0 <= u < 8:
                        attend(l, u)
                    if mp == 0:
                        if br == 0:
                            pe.wait_ge(lo_ready, split(l, "ya", 3) + 1)
                        elif br == 1:
                            pe.wait_ge(lo_ready, split(l, "yc", 3) + 1)
                        else:
                            pe.wait_ge(yb_ready, 8 * (l + 1))
                    yh, yl = ((yah, yal), (ych, ycl), (ybh, ybl))[br]
                    w = weights_of(l, ("proj", s))
                    for j in range(2):
                        t = tile(l, "proj", 2 * s + j)
                        out = acquire(t)
                        three(out[:, :], w, lambda wt, slot, k: wt[:, slot, 256 * k + P * j:256 * k + P * j + P],
                              [yh[:, k, :] for k in range(4)], [yl[:, k, :] for k in range(4)]).then_inc(tile_done, 1)
                    if s == 0:
                        evacuated(pe, tile(l, "aq", 3))
                        pe.wait_ge(kd_ready, 2 * (l + 1))
                        evacuated(pe, tile(l, "kv", 1))
                        pe.wait_ge(f_ready, split(l, "yc", 3) + 1)
                    if s < 8:
                        scores(l, s)
                for m in range(KD):
                    kw = {} if m else {"hi_wait": lambda k: pe.wait_ge(hi_ready, split(l, "mg", k) + 1),
                                       "lo_wait": lambda k: pe.wait_ge(lo_ready, split(l, "mg", k) + 1)}
                    feature_tile(l, ("wout", m), tile(l, "wout", m), mgh, mgl, **kw)
                    if m == 0:
                        ada_tile(l, 5)
                    if m:
                        sums_of_squares(4 * l + 1, m - 1)
                sums_of_squares(4 * l + 1, KD - 1)
                broadcast(4 * l + 1)
                for k in range(KD):
                    sums_of_squares(4 * l + 2, k)
                broadcast(4 * l + 2)
                first_two(l, [("w1", 0), ("w1", 1)], "h2")
                for p in range(NPAIR):
                    for j in range(2):
                        if p:
                            feature_tile(l, ("w1", 2 * p + j), tile(l, "w1", 2 * p + j), hh, hl)
                    if p in ADA_PAIR and ADA_PAIR[p] < ada_tiles(l):
                        ada_tile(l, ADA_PAIR[p])
                for m in range(KD):
                    t = tile(l, "w2", m)
                    out = acquire(t)
                    for third in range(3):
                        k0 = 8 * third
                        nk = min(8, NPAIR - k0)
                        if m == 0:
                            pe.wait_ge(lo_ready, split(l, "ff", k0 + nk - 1) + 1)
                        ins = three(out[:, :], weights_of(l, ("w2", 3 * m + third)), whole,
                                    [acth[:, k0 + k, :] for k in range(nk)], [actl[:, k0 + k, :] for k in range(nk)],
                                    first=third == 0, last=third == 2)
                        ins.then_inc(tile_done if third == 2 else part_used, 1)
                    if m:
                        sums_of_squares(4 * l + 3, m - 1)
                sums_of_squares(4 * l + 3, KD - 1)
                broadcast(4 * l + 3)


def kernel(**inputs):
    import numpy as np
    import concourse.bacc as bacc
    from concourse.bass_utils import run_bass_kernel_spmd

    a = {k: np.asarray(v) for k, v in inputs.items()}

    def blocks(w, width):
        l, k, n = w.shape
        w = w.reshape(l, k // P, P, n // width, width).transpose(0, 3, 2, 1, 4)
        return np.ascontiguousarray(w).reshape(l, n // width, P, k // P * width)

    def columns(v):
        v = v.reshape(v.shape[:-1] + (v.shape[-1] // P, P))
        return np.moveaxis(v, -1, 0)

    w_in = a["w_in"]
    gu, gv, aq, kv, hq, hf, hi, hg = (w_in[:, :, s:e] for s, e in (
        (0, 512), (512, 1024), (1024, 1536), (1536, 1792), (1792, 2304), (2304, 2816), (2816, 3328), (3328, 3840)))
    g = w_in[:, :, 3840:].reshape(L, D, 3, D)[:, :, (0, 2, 1)].reshape(L, D, 3 * D)
    def token_blocks(w):
        w = w.reshape(L, 2, 4, P, 2, 256).transpose(0, 4, 1, 3, 2, 5)
        return np.ascontiguousarray(w).reshape(L, 4, P, BLK)

    parts = [blocks(hf, P), blocks(hq, P), token_blocks(hi), blocks(hg, P), token_blocks(gv), blocks(gu, P), blocks(kv, P),
             blocks(aq, P), blocks(g, P)]
    win = np.concatenate(parts, axis=1)
    proj = np.concatenate([blocks(a[n], 256) for n in ("proj_a", "proj_c", "proj_b")], axis=1)
    w1 = a["ffn_w1"].reshape(L, D, 2, NPAIR, P).transpose(0, 1, 3, 2, 4).reshape(L, D, 2 * FF)

    conv = np.concatenate([a["ffn_conv_w"], a["ffn_conv_b"][:, None, :]], axis=1)
    conv = conv.reshape(L, 4, 2, NPAIR, P).transpose(4, 0, 3, 2, 1).reshape(P, L, NPAIR * 8)
    cols = np.concatenate([columns(a[n]) for n in ("ada_b", "norm_mix_pre", "norm_mix_post", "norm_ffn_pre",
                                                   "norm_ffn_post", "hg_lb_logits", "hg_gnorm")] + [conv], axis=2)
    rows = np.concatenate([a["gm_bs"].reshape(L, 512), a["attn_sinks"]], axis=1)
    ln_rows = np.concatenate([a["gm_ln_g"], a["gm_ln_b"]], axis=1)

    const = np.zeros((P, NCONST), np.float32)
    i = np.arange(P)
    const[:, K_ID:K_ID + P] = np.eye(P)
    const[:, K_ONE:K_ONE + P] = 1.0
    delta = i[:, None] + P - np.arange(256)[None, :]
    const[:, K_AM:K_AM + 256] = np.where((delta >= 0) & (delta < 128), 0.0, -1e30)
    const[:, K_HM:K_HM + P] = (i[:, None] // CH == i[None, :] // CH) & (i[:, None] <= i[None, :])
    const[:, K_INV] = np.float32(10000.0) ** (-(i % 32).astype(np.float32) / np.float32(32))
    const[:, K_SGN] = np.where(i // 32 % 2 == 0, -1.0, 1.0)
    const[:, K_EPS] = EPS

    arrays = {
        "xT": np.ascontiguousarray(a["x"][0].reshape(S, KD, P).transpose(2, 1, 0)),
        "c": np.ascontiguousarray(a["c"][0].reshape(KD, P).T),
        "pos": np.ascontiguousarray(a["positions"][0]),
        "cols": np.ascontiguousarray(cols),
        "rows": np.ascontiguousarray(rows),
        "ln_rows": np.ascontiguousarray(ln_rows),
        "const": const,
        "ws": np.ascontiguousarray(a["gm_ws"].transpose(0, 3, 1, 2)),
        "ada": blocks(a["ada_w"], P),
        "win": win,
        "proj": proj,
        "wout": blocks(a["w_out"], P),
        "w1": blocks(w1, P),
        "w2": blocks(a["ffn_w2"], P),
    }
    nc = bacc.Bacc("TRN2", target_bir_lowering=False, num_devices=1)
    args = [nc.dram_tensor(n, v.shape, mybir.dt.from_np(v.dtype), kind="ExternalInput").ap() for n, v in arrays.items()]
    out = nc.dram_tensor("out", (P, KD, S), F32, kind="ExternalOutput").ap()
    trunk(nc, *args, out)
    r = run_bass_kernel_spmd(nc, [arrays], core_ids=[0])
    got = r.results[0]["out"]
    return np.ascontiguousarray(got.transpose(2, 1, 0)).reshape(1, S, D)
```

```python
from contextlib import ExitStack

import concourse.bass as bass
from concourse import mybir

ALU = mybir.AluOpType
ACT = mybir.ActivationFunctionType
F32 = mybir.dt.float32
F32R = mybir.dt.float32r
I32 = mybir.dt.int32
U32 = mybir.dt.uint32
AX_X = mybir.AxisListType.X

P = 128
D = 1024
S = 512
L = 2
KD = D // P
NT = S // P
EPS = 1e-6
FF = 2816
NPAIR = FF // P
HEADS = 4
CH = 64
NCH = S // CH
SUB = 8
NSUB = CH // SUB
MID = SUB // 2 - 1
MIN_FORGET = 1e-6
HG_SCALE = 128 ** -0.5
AT_SCALE = 64 ** -0.5
MAGIC = 12582912.0
TWO_PI = 6.283185307179586
TWO_PI_HI = 6.28125
TWO_PI_LO = TWO_PI - TWO_PI_HI
PI_SAFE = 3.1415925

C_ADA, C_NMPRE, C_NMPOST, C_NFPRE, C_NFPOST, C_LB, C_GN, C_CONV = 0, 48, 56, 64, 72, 80, 84, 85
NCOL = C_CONV + NPAIR * 2 * 4
K_ID, K_ONE, K_AM, K_HM, K_INV, K_SGN, K_EPS = 0, 128, 256, 512, 640, 641, 642
NCONST = 643
R_BS, R_SINK = 0, 512
NROW = 520

NMP = 4
BLK = 1024
STAGES = 4
RING = 3
KTS = 5


BRANCHES = ("a", "c", "b")
NSTEP = 3 * NMP
BLOCKS = [(n, i) for n in ("hf", "hq", "hi", "hg", "gv") for i in range(4)]
BLOCKS += [("kv", 0), ("kv", 1)] + [(n, i) for n in ("aq", "gu") for i in range(4)]
NFRONT = len(BLOCKS)
for s in range(NSTEP):
    BLOCKS += [("gate", 2 * s), ("gate", 2 * s + 1), ("proj", s)]
BLOCKS += [("wout", i) for i in range(8)] + [("w1", i) for i in range(2 * NPAIR)] + [("w2", i) for i in range(24)]
BLOCK_AT = {b: i for i, b in enumerate(BLOCKS)}
NBLOCK = len(BLOCKS)

ADA_PAIR = {4: 6, 8: 7, 11: 8, 15: 9, 18: 10, 21: 11}
ADA_TWICE = (8, 14)


def ada_after(l, block):
    name, i = block
    if name == "gate":
        return [(l, 16 + i)]
    if name == "w1":
        n = i // 2 + sum(i // 2 > p for p in ADA_TWICE)
        cols = [n] if i % 2 == 0 else [n + 1] if i // 2 in ADA_TWICE else []
        return [(l, 40 + c) if c < 8 else (l + 1, c - 8) for c in cols if c < 8 or l + 1 < L]
    return []


def weight_stream():
    out, adas = [], []
    for l in range(L):
        for b in BLOCKS:
            new = [("ada", x, c) for x, c in ada_after(l, b)]
            out += [(l, b)] + (new if b[0] == "gate" else [])
            adas += new
    return out, adas


TILES = [(n, i) for n in ("hf", "hq", "hi", "hg", "gv") for i in range(4)]
TILES += [("kv", 0), ("kv", 1)] + [(n, i) for n in ("aq", "gu") for i in range(4)]
TILES += [("oss", 0)]
for s in range(NSTEP):
    TILES += [("gate", 2 * s)]
    if s >= 2 and s % 2 == 0:
        TILES += [("ada", s // 2 - 1)]
    TILES += [("gate", 2 * s + 1), ("proj", 2 * s), ("proj", 2 * s + 1)]
TILES += [("wout", 0), ("ada", 5)] + [("wout", i) for i in range(1, 8)]
for p in range(NPAIR):
    TILES += [("w1", 2 * p), ("w1", 2 * p + 1)]
    if p in ADA_PAIR:
        TILES += [("ada", ADA_PAIR[p])]
TILES += [("w2", i) for i in range(8)]
TILE_AT = {t: i for i, t in enumerate(TILES)}
NTILE = len(TILES)

PARTS = [(n, i) for n in ("hi", "gv") for i in (0, 2)] + [("w2", i) for i in range(24) if i % 3 < 2]
PART_AT = {b: i for i, b in enumerate(sorted(PARTS, key=BLOCK_AT.get))}

SPLITS = [("h1", k) for k in range(8)] + [("ya", g) for g in range(4)] + [("yc", h) for h in range(4)]
SPLITS += [("mg", m) for m in range(8)] + [("h2", k) for k in range(8)] + [("ff", p) for p in range(NPAIR)]
NSPLIT = len(SPLITS)
SPLIT_AT = {t: i for i, t in enumerate(SPLITS)}

ROW_SPANS = ((0, 4), (8, 12), (12, 14))
DVE_COLS = (4, 5, 6, 7, 14, 15)
POOL_K = (1, 4, 6)
HG_BLOCKS = BLOCKS[BLOCK_AT[("hi", 0)]:NFRONT]


def tile(l, name, i):
    return l * NTILE + TILE_AT[(name, i)]


def split(l, name, i):
    return l * NSPLIT + SPLIT_AT[(name, i)]


def last_tile(b):
    name, i = b
    return ("proj", 2 * i + 1) if name == "proj" else ("w2", i // 3) if name == "w2" else b


def ada_tiles(l):
    return 12 if l + 1 < L else 8


def trunk(nc, xT_d, c_d, pos_d, cols_d, rows_d, ln_d, const_d, ws_d, ada_d, win_d, proj_d, wout_d, w1_d, w2_d, out_d):
    stream, adas = weight_stream()
    at = {b: i for i, b in enumerate(stream)}
    kinds = [b for b in stream if b[0] != "ada"]
    ffn_adas = [b for b in adas if b not in stream]
    ada_no = {b: i for i, b in enumerate(adas)}

    ctx = ExitStack()
    with ctx:
        def sem(name):
            return ctx.enter_context(nc.semaphore(name))

        KB = 1024
        SLAB = 212832
        start = (nc.sbuf_base + 63) // 64 * 64
        ctx.enter_context(nc.sbuf_tensor("slab", [P, SLAB // 4], F32))

        cursor = [start]

        def place(name, shape, dt, where=None):
            if where is None:
                where = cursor[0]
                n = 4
                for s in shape[1:]:
                    n *= s
                cursor[0] += (n + 31) // 32 * 32
                assert cursor[0] <= start + SLAB, (name, cursor[0] - start)
            return nc.alloc_sbuf_tensor_at(name, shape, dt, offset=where)

        x = place("x", [P, KD, S], F32)
        H0 = cursor[0]
        hh = place("hh", [P, KD, S], F32R)
        hl = place("hl", [P, KD, S], F32R)
        y = place("y", [P, KD, S], F32, H0)
        stage = place("stage", [P, STAGES, BLK], F32)
        whi = place("whi", [P, RING, BLK], F32R)
        wlo = place("wlo", [P, RING, BLK], F32R)
        R0 = cursor[0]
        cursor[0] += 102 * KB

        def at_kb(name, shape, dt, kb):
            return place(name, shape, dt, R0 + int(kb * KB))

        ada0 = at_kb("ada0", [P, 16, BLK], F32, 0)
        ada0_row = at_kb("ada0_row", [P, 3, S], F32, 64)
        ada0_sum = at_kb("ada0_sum", [P, len(DVE_COLS), P], F32, 70)
        hf32 = at_kb("hf32", [P, KD, S], F32, 0)
        gut = at_kb("gut", [P, 4, S], F32, 0)
        yah = at_kb("yah", [P, 4, S], F32R, 0)
        gvt = at_kb("gvt", [P, NT, 512], F32, 8)
        yal = at_kb("yal", [P, 4, S], F32R, 8)
        hqs = at_kb("hqs", [P, HEADS, S], F32, 16)
        ych = at_kb("ych", [P, 4, S], F32R, 16)
        hk = at_kb("hk", [P, HEADS, S], F32, 24)
        ycl = at_kb("ycl", [P, 4, S], F32R, 24)
        lnrow = at_kb("lnrow", [P, 2, 512], F32, 16)
        aqr = at_kb("aqr", [P, 4, S], F32, 32)
        ybh = at_kb("ybh", [P, 4, S], F32R, 32)
        itok = at_kb("itok", [P, NT, 512], F32, 40)
        ybl = at_kb("ybl", [P, 4, S], F32R, 40)
        bb = at_kb("bb", [P, HEADS, S], F32, 48)
        hgs = at_kb("hgs", [P, HEADS, S], F32, 56)
        mg = at_kb("mg", [P, KD, S], F32, 48)
        mgh = at_kb("mgh", [P, KD, S], F32R, 0)
        mgl = at_kb("mgl", [P, KD, S], F32R, 16)
        kd = at_kb("kd", [P, 2, S], F32, 64)
        vt = at_kb("vt", [P, NT, 128], F32, 68)
        khT = at_kb("khT", [P, NT, 128], F32, 70)
        states = at_kb("states", [P, NCH - 1, 128], F32, 72)
        asb = at_kb("asb", [P, S], F32, 75.5)
        gates = at_kb("gates", [P, 4, S], F32, 70)
        kt = at_kb("kt", [P, KTS, NCH, CH], F32, 78)
        odg = at_kb("odg", [P, 16, P], F32, 78)
        pm = at_kb("pm", [P, 4, 256], F32, 78)
        pts = at_kb("pts", [P, 2, 4, 128], F32, 82)
        tmp = [at_kb(f"tmp{i}", [P, S], F32, 88 + 2 * i) for i in range(5)]
        sq = [at_kb(f"sq{i}", [P, S], F32, 98 + 2 * i) for i in range(2)]
        ada_sum = place("ada_sum", [P, 8, P], F32)
        acth = at_kb("acth", [P, NPAIR, S], F32R, 0)
        actl = at_kb("actl", [P, NPAIR, S], F32R, 44)
        hgset = [(tmp[0], tmp[1], tmp[2]), (tmp[4], sq[0], sq[1])]
        sqring = [sq[0], sq[1], tmp[0], tmp[1]]
        sqsum = tmp[4]
        ada_ffn = at_kb("ada_ffn", [P, BLK], F32, 98)
        bcs = tmp[2]
        osq = [tmp[0], tmp[1], tmp[4], sq[0]]

        cosb = place("cosb", [P, S], F32)
        sinb = place("sinb", [P, S], F32)
        const = place("const", [P, NCONST], F32)
        cols = place("cols", [P, L, NCOL], F32)
        rows = place("rows", [P, NROW], F32)
        ws = place("ws", [P, 4, 128], F32)
        mod = place("mod", [P, 48], F32)
        ccol = place("ccol", [P, KD], F32)
        cact = place("cact", [P, KD], F32)
        cA = place("cA", [P, 2, KD], F32)
        cG = place("cG", [P, 2, KD], F32)
        lbs = place("lbs", [P, L, 2, HEADS], F32)
        lbt = place("lbt", [P, 4, HEADS], F32)
        spare = place("spare", [P, 1], F32)
        sscol = place("sscol", [P, NT], F32)
        std = place("std", [P, 16], F32)
        rstd = place("rstd", [P, 16], F32)
        mv = place("mv", [P, NT, 2], F32)
        vstd = place("vstd", [P, 2, NT], F32)
        amx = place("amx", [P, 3, 4], F32)
        ars = place("ars", [P, 3, 4], F32)
        elast = place("elast", [P, 2, NCH], F32)
        bn = place("bn", [P, NT, 6], F32)

        ident = const[:, K_ID:K_ID + P]
        ones = const[:, K_ONE:K_ONE + P]
        eps = const[:, K_EPS:K_EPS + 1]

        acc = [ctx.enter_context(nc.psum_tensor(f"acc{i}", [P, S], F32)) for i in range(4)]
        b4, b5, b6, b7 = [ctx.enter_context(nc.psum_tensor(f"bank{i}", [P, S], F32)) for i in range(4, 8)]
        small = [b4, b5, b6, b7]
        hbank = [b4, b5]
        rowbank = [b4, b6, acc[3]]

        const_in = sem("const_in")
        x_in = sem("x_in")
        pos_in = sem("pos_in")
        rows_in = sem("rows_in")
        ws_in = sem("ws_in")
        ada0_in = [sem(f"ada0_in{i}") for i in range(4)]
        stored = sem("stored")
        landed = [sem(f"landed{i}") for i in range(STAGES)]
        whi_ready = sem("whi_ready")
        wlo_ready = sem("wlo_ready")
        part_used = sem("part_used")
        ada_in = sem("ada_in")
        ada_used = sem("ada_used")
        ada_summed = sem("ada_summed")
        tile_done = sem("tile_done")
        acc_free = [sem(f"acc_free{i}") for i in range(4)]
        f_ready = sem("f_ready")
        hi_ready = sem("hi_ready")
        lo_ready = sem("lo_ready")
        x_ready = sem("x_ready")
        x_ready_pool = sem("x_ready_pool")
        y_scaled = sem("y_scaled")
        bcs_ready = sem("bcs_ready")
        sq_ready = sem("sq_ready")
        sq_added = sem("sq_added")
        ss_done = sem("ss_done")
        ss_cols = sem("ss_cols")
        std_ready = sem("std_ready")
        diag_ready = sem("diag_ready")
        bc_ready = sem("bc_ready")
        cact_ready = sem("cact_ready")
        ada0_rows = sem("ada0_rows")
        ada0_copied = sem("ada0_copied")
        ada0_summed = sem("ada0_summed")
        ada0_done = sem("ada0_done")
        ang_ready = sem("ang_ready")
        trig_ready = sem("trig_ready")
        lb_a = sem("lb_a")
        lb_b = sem("lb_b")
        dve_own = sem("dve_own")
        act_own = sem("act_own")
        pool_own = sem("pool_own")
        kd_ready = sem("kd_ready")
        ws_ready = sem("ws_ready")
        vvar = sem("vvar")
        vsd = sem("vsd")
        vn_ready = sem("vn_ready")
        sgu_done = sem("sgu_done")
        forget_ready = sem("forget_ready")
        log_ready = sem("log_ready")
        diff_ready = sem("diff_ready")
        exp_ready = sem("exp_ready")
        kdiff = sem("kdiff")
        kexp = sem("kexp")
        kt_ready = sem("kt_ready")
        qk_ready = sem("qk_ready")
        khT_done = sem("khT_done")
        khT_copied = sem("khT_copied")
        ds_done = sem("ds_done")
        state_ready = sem("state_ready")
        a_done = sem("a_done")
        masked = sem("masked")
        o_done = sem("o_done")
        o_copied = sem("o_copied")
        osq_ready = sem("osq_ready")
        odiag = sem("odiag")
        obc = sem("obc")
        qk_done = sem("qk_done")
        max_ready = sem("max_ready")
        p_exp = sem("p_exp")
        p_ready = sem("p_ready")
        pt_done = sem("pt_done")
        pt_copied_a = sem("pt_copied_a")
        pt_copied_v = sem("pt_copied_v")
        pv_done = sem("pv_done")
        ybh_ready = sem("ybh_ready")
        yb_ready = sem("yb_ready")
        conv0 = sem("conv0")
        silu_done = sem("silu_done")

        numbers = {}
        for l in range(L):
            for t in TILES:
                if t[0] != "ada" or t[1] < ada_tiles(l):
                    numbers[(l,) + t] = len(numbers)

        def tile(l, name, i):
            return numbers[(l, name, i)]

        def evacuated(eng, t):
            eng.wait_ge(acc_free[t % 4], t // 4 + 1)

        def block_is_used(eng, lb):
            l, b = lb
            if b in PART_AT:
                eng.wait_ge(part_used, len(PART_AT) * l + PART_AT[b] + 1)
            else:
                eng.wait_ge(tile_done, tile(l, *last_tile(b)) + 1)

        def x_updated(eng, n, k):
            if k in POOL_K:
                eng.wait_ge(x_ready_pool, len(POOL_K) * (n - 1) + POOL_K.index(k) + 1)
            else:
                own = [i for i in range(KD) if i not in POOL_K]
                eng.wait_ge(x_ready, len(own) * (n - 1) + own.index(k) + 1)

        block = ctx.enter_context(nc.Block())

        def block_src(item):
            if item[0] == "ada":
                return ada_d[item[1], item[2]], BLK
            l, (name, i) = item
            if name == "gate":
                return win_d[l, NFRONT + i], BLK
            if name == "proj":
                return proj_d[l, i], BLK
            if name == "wout":
                return wout_d[l, i], BLK
            if name == "w1":
                return w1_d[l, i], BLK
            if name == "w2":
                k0 = 8 * (i % 3)
                n = min(8, NPAIR - k0) * P
                return w2_d[l, i // 3, :, k0 * P:k0 * P + n], n
            return win_d[l, BLOCK_AT[(name, i)]], BLK

        def modcols(part):
            return mod[:, 8 * part:8 * part + 8]

        @block.sync
        def _(sp):
            sp.dma_start(ccol[:, :], c_d).then_inc(const_in, 16)
            sp.dma_start(const[:, :], const_d).then_inc(const_in, 16)
            sp.dma_start(cols[:, :, :], cols_d).then_inc(const_in, 16)
            for i in range(4):
                if i == 3:
                    sp.dma_start(x[:, :, :], xT_d).then_inc(x_in, 16)
                sp.dma_start(ada0[:, 4 * i:4 * i + 4, :], ada_d[0, 4 * i:4 * i + 4].rearrange("c p n -> p c n")).then_inc(ada0_in[i], 16)
            for i, b in enumerate(stream):
                if i >= STAGES:
                    old = stream[i - STAGES]
                    if old[0] == "ada":
                        sp.wait_ge(ada_used, ada_no[old] + 1)
                    else:
                        sp.wait_ge(wlo_ready, kinds.index(old) + 1)
                src, n = block_src(b)
                sp.dma_start(stage[:, i % STAGES, 0:n], src).then_inc(landed[i % STAGES], 16)
            for k in range(KD):
                x_updated(sp, 2 * L, k)
                sp.dma_start(out_d[:, k, :], x[:, k, :]).then_inc(stored, 16)
            sp.wait_ge(stored, 16 * KD)

        @block.gpsimd
        def _(pool):
            pool.dma_start(tmp[3][:, :].bitcast(I32), pos_d.partition_broadcast(P)).then_inc(pos_in, 16)

            def layer_rows(l):
                pool.wait_ge(tile_done, tile(l, "hf", 0) + 1)
                pool.dma_start(rows[:, :], rows_d[l].partition_broadcast(P)).then_inc(rows_in, 16)
                pool.dma_start(ws[:, :, :], ws_d[l]).then_inc(ws_in, 16)

            def norm_rows(l):
                pool.wait_ge(qk_ready, HEADS * l + 2)
                pool.dma_start(lnrow[:, :, :], ln_d[l].partition_broadcast(P)).then_inc(rows_in, 16)

            def causal_weights(l):
                pool.wait_ge(ws_in, 16 * (l + 1))
                nc.gpsimd.affine_select(out=ws[:, :, :], in_=ws[:, :, :], compare_op=ALU.is_ge, fill=0.0, base=0,
                                        pattern=[[0, 4], [1, 128]], channel_multiplier=-1).then_inc(ws_ready, 1)

            def load_conditioning(l, i):
                for x_l, c in ada_after(l, ("w1", i)):
                    item = ("ada", x_l, c)
                    if i == 0:
                        pool.wait_ge(ss_done, 8 * (2 * l + 2))
                    elif ada_no[item]:
                        pool.wait_ge(ada_used, ada_no[item])
                    pool.dma_start(ada_ffn[:, :], ada_d[x_l, c]).then_inc(ada_in, 16)

            def update_x(l, name, n):
                pool.wait_ge(bcs_ready, n)
                for i, k in enumerate(POOL_K):
                    if k == POOL_K[-1]:
                        pool.wait_ge(y_scaled, n)
                    else:
                        evacuated(pool, tile(l, name, k))
                        nc.gpsimd.tensor_tensor(y[:, k, :], y[:, k, :], bcs[:, :], ALU.mult).then_inc(pool_own, 1)
                        pool.wait_ge(pool_own, 2 * (n - 1) + i + 1)
                    nc.gpsimd.tensor_tensor(x[:, k, :], x[:, k, :], y[:, k, :], ALU.add).then_inc(x_ready_pool, 1)

            for i, item in enumerate(kinds):
                l, b = item
                n = block_src(item)[1]
                slot = at[item] % STAGES
                pool.wait_ge(whi_ready, i + 1)
                if i >= RING:
                    block_is_used(pool, kinds[i - RING])
                nc.gpsimd.tensor_tensor(wlo[:, i % RING, 0:n], stage[:, slot, 0:n], whi[:, i % RING, 0:n].bitcast(F32),
                                        ALU.subtract).then_inc(wlo_ready, 1)
                if b[0] == "w1" and b[1]:
                    load_conditioning(l, b[1] - 1)
                if b == ("wout", 7):
                    update_x(l, "wout", 2 * l + 1)
                if b == ("w2", 23):
                    update_x(l, "w2", 2 * l + 2)
                if b == ("hf", 3):
                    layer_rows(l)
                if b == ("hi", 0):
                    causal_weights(l)
                if b == ("kv", 0):
                    norm_rows(l)

        @block.scalar
        def _(act):
            A = nc.scalar.activation
            own = [0]
            done = [0]

            def chain(ins):
                ins.then_inc(act_own, 1)
                own[0] += 1

            def sync():
                act.wait_ge(act_own, own[0])

            def weights(l, b, ahead=0):
                upto = NBLOCK * l + BLOCK_AT[b] + ahead
                while done[0] <= min(upto, len(kinds) - 1):
                    i = done[0]
                    n = block_src(kinds[i])[1]
                    slot = at[kinds[i]] % STAGES
                    act.wait_ge(landed[slot], 16 * (at[kinds[i]] // STAGES + 1))
                    if i >= RING:
                        block_is_used(act, kinds[i - RING])
                    A(whi[:, i % RING, 0:n], stage[:, slot, 0:n], ACT.Copy).then_inc(whi_ready, 1)
                    done[0] += 1

            def squares(n, k, src):
                i = n // 2
                ring = sqring if n % 2 == 0 else sq
                if n % 2 == 0:
                    if k >= 4:
                        act.wait_ge(ss_done, 8 * i + k - 3)
                    elif n:
                        act.wait_ge(sq_added, (KD - 1) * i)
                    elif k == 2:
                        act.wait_ge(trig_ready, 2)
                elif k >= 2:
                    act.wait_ge(sq_added, (KD - 1) * i + max(k - 2, 1))
                else:
                    act.wait_ge(ss_done, 8 * i + 8)
                A(ring[k % len(ring)][:, :], src, ACT.Square).then_inc(sq_ready, 1)

            def deviation(n):
                act.wait_ge(ss_cols, n + 1)
                A(std[:, 0:NT], b6[:, 0:NT] if n % 2 else sscol[:, :], ACT.Sqrt, bias=eps, scale=1.0 / D).then_inc(std_ready, 1)

            def copy_broadcast(n):
                act.wait_ge(bc_ready, n + 1)
                A(bcs[:, :], b6[:, :], ACT.Copy).then_inc(bcs_ready, 1)

            def square_root_table():
                A(spare[:, :], eps, ACT.Sqrt)

            def pre_norm(l, which):
                n = 4 * l + 2 * which
                for k in range(KD):
                    if n:
                        x_updated(act, 2 * l + which, k)
                    elif k == 0:
                        act.wait_ge(x_in, 16)
                    squares(n, k, x[:, k, :])
                if n == 0:
                    copy_row(1)
                weights(l, ("w1", 1) if which else ("hf", 1))
                deviation(n)
                if n == 0:
                    copy_row(2)
                name = "h2" if which else "h1"
                shift = modcols(3 if which else 0)
                for k in range(KD):
                    act.wait_ge(f_ready, split(l, name, k) + 1)
                    A(hh[:, k, :], hf32[:, k, :], ACT.Identity, bias=shift[:, k:k + 1]).then_inc(hi_ready, 1)

            def take(l, name, i):
                if (name, i) in PART_AT or name == "aq" or (name, i) == ("kv", 0):
                    return
                if name in ("gv", "hi"):
                    for j in range(2):
                        t = tile(l, name, i - 1 + j)
                        act.wait_ge(tile_done, t + 1)
                        dst = gvt if name == "gv" else itok
                        half = 256 * (i // 2)
                        A(dst[:, 2 * j:2 * j + 2, half:half + 256], acc[t % 4][:, :].rearrange("p (t n) -> p t n", t=2),
                          ACT.Gelu_apprx_tanh if name == "gv" else ACT.Copy).then_inc(acc_free[t % 4], 1)
                    return
                t = tile(l, name, i)
                a = acc[t % 4][:, :]
                act.wait_ge(tile_done, t + 1)
                if name == "hf":
                    chain(A(bb[:, i, :], a, ACT.Sigmoid))
                    ins = A(hk[:, i, :], a, ACT.Sigmoid, scale=-1.0)
                elif name == "hq":
                    ins = A(hqs[:, i, :], a, ACT.Silu)
                elif name == "hg":
                    ins = A(hgs[:, i, :], a, ACT.Silu)
                elif name == "gu":
                    ins = A(gut[:, i, :], a, ACT.Gelu_apprx_tanh)
                else:
                    ins = A(vt[:, :, :], a.rearrange("p (t n) -> p t n", t=NT), ACT.Copy)
                ins.then_inc(acc_free[t % 4], 1)

            def hg_step(l, step):
                h, half = step // 2, step % 2
                q = HEADS * l + h
                t0, t1, t2 = hgset[h % 2]
                if half == 0:
                    act.wait_ge(forget_ready, q + 1)
                    A(t0[:, :], bb[:, h, :], ACT.Ln).then_inc(log_ready, 1)
                    act.wait_ge(diff_ready, q + 1)
                    chain(A(t0[:, :], t0[:, :], ACT.Exp))
                    chain(A(t1[:, :], bb[:, h, :], ACT.Exp))
                    chain(A(elast[:, h % 2, :], bb[:, h, :].rearrange("p (c t) -> p c t", t=CH)[:, :, CH - 1], ACT.Exp))
                    A(t2[:, :], t2[:, :], ACT.Exp).then_inc(exp_ready, 1)
                else:
                    act.wait_ge(khT_done, q + 1)
                    A(khT[:, :, :], b6[:, :].rearrange("p (t n) -> p t n", t=NT), ACT.Copy).then_inc(khT_copied, 1)
                for i in range(4 * half, 4 * half + 4):
                    act.wait_ge(kdiff, NSUB * q + i + 1)
                    v = kt[:, i % KTS, :, 0:SUB * (i + 1)]
                    A(v, v, ACT.Exp).then_inc(kexp, 1)

            def hg_output(l, h):
                q = HEADS * l + h
                act.wait_ge(o_done, q + 1)
                A(bb[:, h, :], hbank[h % 2][:, :], ACT.Copy).then_inc(o_copied, 1)

            def attention_exp(l, u):
                a = 8 * l + u
                w = 256 if u // 2 else 128
                act.wait_ge(max_ready, a + 1)
                for i in range(4):
                    chain(A(pm[:, i, 0:w], pm[:, i, 0:w], ACT.Exp, bias=amx[:, 1, i:i + 1], accum_out=ars[:, 0, i:i + 1]))
                A(ars[:, 1, :], amx[:, 2, :], ACT.Exp).then_inc(p_exp, 1)

            def convolve(l, p, j):
                t = tile(l, "w1", 2 * p + j)
                c0 = C_CONV + 8 * p + 4 * j
                act.wait_ge(tile_done, t + 1)
                A(tmp[2 * (p % 2) + j][:, :], acc[t % 4][:, :], ACT.Identity, bias=cols[:, l, c0 + 3:c0 + 4],
                  scale=cols[:, l, c0 + 2:c0 + 3]).then_inc(conv0, 1)

            act.wait_ge(const_in, 48)
            A(cact[:, :], ccol[:, :], ACT.Silu).then_inc(cact_ready, 1)
            act.wait_ge(lb_a, 1)
            A(lbt[:, 0:2, :], lbt[:, 0:2, :], ACT.Exp).then_inc(lb_b, 1)
            act.wait_ge(ang_ready, 1)
            A(cosb[:, :], tmp[0][:, :], ACT.Sin).then_inc(trig_ready, 1)
            A(sinb[:, :], tmp[1][:, :], ACT.Sin).then_inc(trig_ready, 1)

            def copy_row(g):
                act.wait_ge(ada0_rows, g + 1)
                w = P * (ROW_SPANS[g][1] - ROW_SPANS[g][0])
                A(ada0_row[0:1, g, 0:w], rowbank[g][0:1, 0:w], ACT.Copy).then_inc(ada0_copied, 1)

            copy_row(0)
            for l in range(L):
                pre_norm(l, 0)
                for b in BLOCKS[:NFRONT]:
                    weights(l, b, 2)
                    if b in HG_BLOCKS:
                        i = HG_BLOCKS.index(b)
                        if i % 2 == 0 and i // 2 < 2 * HEADS:
                            hg_step(l, i // 2)
                        if i % 4 == 1 and 9 <= i <= 17:
                            hg_output(l, (i - 9) // 4)
                    take(l, *b)
                    if b == ("gu", 1):
                        evacuated(act, tile(l, "kv", 0))
                        for j in range(2):
                            A(kd[64 - 64 * j:128 - 64 * j, j, :], kd[64 * j:64 * j + 64, j, :], ACT.Copy).then_inc(kd_ready, 1)
                    if b == ("gu", 0):
                        act.wait_ge(vvar, l + 1)
                        A(vstd[:, 0, :], mv[:, :, 1], ACT.Sqrt, bias=eps).then_inc(vsd, 1)
                hg_output(l, 3)
                for h in range(HEADS):
                    act.wait_ge(o_copied, HEADS * (l + 1))
                    A(osq[h][:, :], bb[:, h, :], ACT.Square).then_inc(osq_ready, 1)
                for g in range(4):
                    act.wait_ge(f_ready, split(l, "ya", g) + 1)
                    A(yah[:, g, :], tmp[2 + g % 2][:, :], ACT.Copy).then_inc(hi_ready, 1)
                t = tile(l, "oss", 0)
                act.wait_ge(tile_done, t + 1)
                A(std[:, :], acc[t % 4][:, 0:16], ACT.Sqrt, bias=eps, scale=1.0 / 128).then_inc(acc_free[t % 4], 1)
                for s in range(NSTEP):
                    br, mp = s // NMP, s % NMP
                    u = s - 1
                    if 0 <= u < 8:
                        attention_exp(l, u)
                    for j in range(2):
                        weights(l, ("gate", 2 * s + j), 2)
                        t = tile(l, "gate", 2 * s + j)
                        act.wait_ge(tile_done, t + 1)
                        if s >= 2:
                            evacuated(act, tile(l, "proj", 2 * s - 4 + j))
                        A(gates[:, (2 * s + j) % 4, :], acc[t % 4][:, :], ACT.Sigmoid).then_inc(acc_free[t % 4], 1)
                        if s == 0:
                            for h in (2 * j, 2 * j + 1):
                                act.wait_ge(f_ready, split(l, "yc", h) + 1)
                                A(ych[:, h, :], tmp[h % 2][:, :], ACT.Copy).then_inc(hi_ready, 1)
                        if 2 <= u < 8 and j == (0 if u == 7 else 1):
                            act.wait_ge(pt_done, 8 * l + u + 1)
                            A(pts[:, 0, :, :], b6[:, :].rearrange("p (t n) -> p t n", t=4), ACT.Copy).then_inc(pt_copied_a, 1)
                        if 0 <= u < 8 and j == 1:
                            act.wait_ge(pv_done, 8 * l + u + 1)
                            v = slice(P * (u // 2), P * (u // 2) + P)
                            A(ybh[:, 2 * (u % 2):2 * (u % 2) + 2, v],
                              b6[:, 0:256].rearrange("p (t n) -> p t n", t=2), ACT.Copy).then_inc(ybh_ready, 1)
                    weights(l, ("proj", s), 2)
                    if br == 2:
                        for m in (2 * mp, 2 * mp + 1):
                            act.wait_ge(f_ready, split(l, "mg", m) + 1)
                            A(mgh[:, m, :], tmp[m % 2][:, :], ACT.Copy).then_inc(hi_ready, 1)
                n = 4 * l + 1
                for m in range(KD):
                    weights(l, ("wout", m), 2)
                    t = tile(l, "wout", m)
                    act.wait_ge(tile_done, t + 1)
                    squares(n, m, acc[t % 4][:, :])
                    if m == 0:
                        square_root_table()
                deviation(n)
                copy_broadcast(n)
                pre_norm(l, 1)
                for p in range(NPAIR + 1):
                    last = tmp[2 * ((p - 1) % 2)][:, :]
                    if p < NPAIR:
                        weights(l, ("w1", 2 * p), 2)
                    if p:
                        evacuated(act, tile(l, "w1", 2 * p - 1))
                        A(last, last, ACT.Silu).then_inc(silu_done, 1)
                    if p < NPAIR:
                        if p >= 2:
                            act.wait_ge(lo_ready, split(l, "ff", p - 2) + 1)
                        convolve(l, p, 0)
                    if p:
                        act.wait_ge(f_ready, split(l, "ff", p - 1) + 1)
                        A(acth[:, p - 1, :], last, ACT.Copy).then_inc(hi_ready, 1)
                    if p < NPAIR:
                        weights(l, ("w1", 2 * p + 1), 2)
                        convolve(l, p, 1)
                n = 4 * l + 3
                for m in range(KD):
                    weights(l, ("w2", 3 * m))
                    weights(l, ("w2", 3 * m + 1))
                    weights(l, ("w2", 3 * m + 2), 2)
                    t = tile(l, "w2", m)
                    act.wait_ge(tile_done, t + 1)
                    squares(n, m, acc[t % 4][:, :])
                    if m == 0:
                        square_root_table()
                deviation(n)
                copy_broadcast(n)

        @block.vector
        def _(dve):
            V = nc.vector
            own = [0]

            def chain(ins):
                ins.then_inc(dve_own, 1)
                own[0] += 1

            def sync():
                dve.wait_ge(dve_own, own[0])

            def free(t, ins):
                ins.then_inc(acc_free[t % 4], 1)

            def lo(s, dst, src, hi, shift=None):
                dve.wait_ge(hi_ready, s + 1)
                if shift is None:
                    V.tensor_tensor(dst, src, hi.bitcast(F32), ALU.subtract).then_inc(lo_ready, 1)
                else:
                    V.scalar_tensor_tensor(out=dst, in0=src, scalar=shift, in1=hi.bitcast(F32), op0=ALU.add,
                                           op1=ALU.subtract).then_inc(lo_ready, 1)

            def ada_units(l, b):
                for x_l, c in ada_after(l, b):
                    item = ("ada", x_l, c)
                    if item in at:
                        i = at[item]
                        dve.wait_ge(landed[i % STAGES], 16 * (i // STAGES + 1))
                        w = stage[:, i % STAGES, :].rearrange("p (k n) -> p k n", k=KD)
                    else:
                        dve.wait_ge(ada_in, 16 * (ffn_adas.index(item) + 1))
                        w = ada_ffn[:, :].rearrange("p (k n) -> p k n", k=KD)
                    chain(V.tensor_tensor(w, w, cact[:, :].unsqueeze(2).broadcast_to([P, KD, P]), ALU.mult))
                    n = ada_no[item]
                    if n % 4 == 0 and n >= 8:
                        dve.wait_ge(tile_done, ada_tile_of(n // 4 - 2) + 1)
                    sync()
                    V.tensor_reduce(ada_sum[:, n % 8, :], w.rearrange("p k n -> p n k"), AX_X, ALU.add).then_inc(ada_used, 1)

            def ada_tile_of(i):
                return sorted(v for k, v in numbers.items() if k[1] == "ada")[i]

            def take_ada(l, i):
                t = tile(l, "ada", i)
                layer, c0 = (l, 16 + 4 * i) if i < 8 else (l + 1, 4 * (i - 8))
                dve.wait_ge(tile_done, t + 1)
                free(t, V.tensor_tensor(mod[:, c0:c0 + 4], acc[t % 4][:, 0:4], cols[:, layer, C_ADA + c0:C_ADA + c0 + 4], ALU.add))

            def broadcast_rstd(n):
                dve.wait_ge(std_ready, n + 1)
                chain(V.reciprocal(rstd[:, 0:NT], std[:, 0:NT]))
                sync()
                V.tensor_tensor(tmp[3][:, :].rearrange("p (t n) -> p t n", t=NT),
                                ident.unsqueeze(1).broadcast_to([P, NT, P]),
                                rstd[:, 0:NT].unsqueeze(2).broadcast_to([P, NT, P]), ALU.mult).then_inc(diag_ready, 1)

            def pre_norm(l, which):
                n = 4 * l + 2 * which
                g0 = C_NFPRE if which else C_NMPRE
                dve.wait_ge(ss_done, 8 * (n // 2) + 8)
                sync()
                T = tmp[3][:, :].rearrange("p (t n) -> p t n", t=NT)
                chain(V.tensor_tensor(T, b7[:, :].rearrange("p (t n) -> p t n", t=NT),
                                      ident.unsqueeze(1).broadcast_to([P, NT, P]), ALU.mult))
                sync()
                V.tensor_reduce(sscol[:, :], T, AX_X, ALU.add).then_inc(ss_cols, 1)
                if n == 0:
                    dve.wait_ge(ada0_done, 1)
                    chain(V.tensor_tensor(mod[:, 0:16], b5[:, 0:16], cols[:, 0, C_ADA:C_ADA + 16], ALU.add))
                    sync()
                if l or which:
                    last = tile(l, "ada", 5) if which else tile(l - 1, "ada", 11)
                    evacuated(dve, last)
                chain(V.scalar_tensor_tensor(out=cA[:, which, :], in0=modcols(4 if which else 1), scalar=1.0,
                                             in1=cols[:, l, g0:g0 + 8], op0=ALU.add, op1=ALU.mult))
                broadcast_rstd(n)
                name = "h2" if which else "h1"
                shift = modcols(3 if which else 0)
                dve.wait_ge(bc_ready, n + 1)
                sync()
                for k in range(KD):
                    V.scalar_tensor_tensor(out=hf32[:, k, :], in0=x[:, k, :], scalar=cA[:, which, k:k + 1],
                                           in1=b6[:, :], op0=ALU.mult, op1=ALU.mult).then_inc(f_ready, 1)
                for k in range(KD):
                    lo(split(l, name, k), hl[:, k, :], hf32[:, k, :], hh[:, k, :], shift[:, k:k + 1])

            def take_y(l, name, m):
                t = tile(l, name, m)
                n = 4 * l + (1 if name == "wout" else 3)
                dve.wait_ge(sq_ready, 8 * n + m + 1)
                if m == KD - 1:
                    add_squares(n, m)
                which = 0 if name == "wout" else 1
                if m == 0:
                    evacuated(dve, tile(l, "ada", 7 if which else 1))
                    g0 = C_NFPOST if which else C_NMPOST
                    chain(V.tensor_tensor(cG[:, which, :], modcols(5 if which else 2), cols[:, l, g0:g0 + 8], ALU.mult))
                    sync()
                free(t, V.tensor_scalar(y[:, m, :], acc[t % 4][:, :], cG[:, which, m:m + 1], None, ALU.mult))
                if 0 < m < KD - 1:
                    add_squares(n, m)

            def add_squares(n, m):
                if m > 1:
                    dve.wait_ge(sq_added, (KD - 1) * (n // 2) + m - 1)
                V.tensor_tensor(sqsum[:, :], sq[0][:, :] if m == 1 else sqsum[:, :], sq[m % 2][:, :], ALU.add).then_inc(sq_added, 1)

            def post_norm(l, which):
                n = 4 * l + 1 + 2 * which
                broadcast_rstd(n)
                dve.wait_ge(bcs_ready, 2 * l + which + 1)
                evacuated(dve, tile(l, "w2" if which else "wout", KD - 1))
                k = POOL_K[-1]
                V.tensor_tensor(y[:, k, :], y[:, k, :], bcs[:, :], ALU.mult).then_inc(y_scaled, 1)
                for k in range(KD):
                    if k not in POOL_K:
                        chain(V.tensor_tensor(y[:, k, :], y[:, k, :], bcs[:, :], ALU.mult))
                        sync()
                        V.tensor_tensor(x[:, k, :], x[:, k, :], y[:, k, :], ALU.add).then_inc(x_ready, 1)

            def rotate(t, parts, before=None):
                a = acc[t % 4]
                dve.wait_ge(tile_done, t + 1)
                for r, dst in parts:
                    chain(V.tensor_tensor(dst, a[r, :], cosb[r, :], ALU.mult))
                if before is not None:
                    evacuated(dve, before)
                for u in range(4):
                    w = u ^ 1
                    chain(V.tensor_tensor(tmp[3][32 * u:32 * u + 32, :], a[32 * w:32 * w + 32, :],
                                          sinb[32 * u:32 * u + 32, :], ALU.mult))
                sync()
                for i, (r, dst) in enumerate(parts):
                    ins = V.tensor_tensor(dst, dst, tmp[3][r, :], ALU.add)
                    if i < len(parts) - 1:
                        chain(ins)
                    else:
                        free(t, ins)

            def hg_step(l, step):
                h, half = step // 2, step % 2
                q = HEADS * l + h
                t0, t1, t2 = hgset[h % 2]
                b3 = bb[:, h, :].rearrange("p (g t) -> p g t", t=SUB)
                bc = bb[:, h, :].rearrange("p (c t) -> p c t", t=CH)
                kc = hk[:, h, :].rearrange("p (c t) -> p c t", t=CH)

                def key_diff(i):
                    n = SUB * (i + 1)
                    if i >= KTS:
                        dve.wait_ge(a_done, NSUB * q + i - KTS + 1)
                    elif h:
                        dve.wait_ge(a_done, NSUB * (q - 1) + (i + KTS if i + KTS < NSUB else i) + 1)
                    m = SUB * i + MID
                    V.tensor_tensor(kt[:, i % KTS, :, 0:n], bc[:, :, m:m + 1].broadcast_to([P, NCH, n]), bc[:, :, 0:n],
                                    ALU.subtract).then_inc(kdiff, 1)

                def key_tile(i):
                    n = SUB * (i + 1)
                    dve.wait_ge(kexp, NSUB * q + i + 1)
                    if i % 4 == 0:
                        sync()
                    v = kt[:, i % KTS, :, 0:n]
                    V.tensor_tensor(v, v, kc[:, :, 0:n], ALU.mult).then_inc(kt_ready, 1)

                if half == 0:
                    lb, lb1 = lbs[:, l, 0, h:h + 1], lbs[:, l, 1, h:h + 1]
                    chain(V.tensor_scalar(bb[:, h, :], bb[:, h, :], lb1, lb, ALU.mult, ALU.add))
                    chain(V.tensor_scalar(hk[:, h, :], hk[:, h, :], lb1, None, ALU.mult))
                    sync()
                    if h >= 2:
                        dve.wait_ge(o_done, q - 1)
                    V.tensor_scalar(bb[:, h, :], bb[:, h, :], MIN_FORGET, None, ALU.max).then_inc(forget_ready, 1)
                    dve.wait_ge(log_ready, q + 1)
                    for c in range(NCH):
                        v = slice(CH * c, CH * c + CH)
                        chain(V.tensor_tensor_scan(bb[:, h, v], t0[:, v], t0[:, v], 0.0, ALU.add, ALU.bypass))
                    sync()
                    chain(V.tensor_tensor(t0[:, :].rearrange("p (g t) -> p g t", t=SUB), b3,
                                          b3[:, :, MID:MID + 1].broadcast_to([P, S // SUB, SUB]), ALU.subtract))
                    V.tensor_tensor(t2[:, :].rearrange("p (c t) -> p c t", t=CH),
                                    bc[:, :, CH - 1:CH].broadcast_to([P, NCH, CH]), bc, ALU.subtract).then_inc(diff_ready, 1)
                    for i in range(4):
                        key_diff(i)
                    dve.wait_ge(exp_ready, q + 1)
                    V_ = V.scalar_tensor_tensor
                    chain(V_(out=t0[:, :], in0=hqs[:, h, :], scalar=HG_SCALE, in1=t0[:, :], op0=ALU.mult, op1=ALU.mult))
                    chain(V_(out=t1[:, :], in0=hqs[:, h, :], scalar=HG_SCALE, in1=t1[:, :], op0=ALU.mult, op1=ALU.mult))
                    sync()
                    V.tensor_tensor(t2[:, :], hk[:, h, :], t2[:, :], ALU.mult).then_inc(qk_ready, 1)
                    for i in range(4):
                        key_tile(i)
                else:
                    for i in range(4, NSUB):
                        key_diff(i)
                    for i in range(4, NSUB):
                        key_tile(i)

            def hg_states(l, h):
                q = HEADS * l + h
                dve.wait_ge(ds_done, q + 1)
                if h:
                    dve.wait_ge(o_done, q)
                for c in range(NCH - 1):
                    src = (b6 if c % 2 else b7)[:, P * (c // 2):P * (c // 2) + P]
                    if c == 0:
                        ins = V.tensor_copy(states[:, 0, :], src)
                    else:
                        ins = V.scalar_tensor_tensor(out=states[:, c, :], in0=states[:, c - 1, :],
                                                     scalar=elast[:, h % 2, c:c + 1], in1=src, op0=ALU.mult, op1=ALU.add)
                    if c < NCH - 2:
                        chain(ins)
                        sync()
                    else:
                        ins.then_inc(state_ready, 1)
                dve.wait_ge(a_done, NSUB * (q + 1))
                V.copy_predicated(asb[:, :].rearrange("p (c t) -> p c t", c=NT),
                                  const[:, K_HM:K_HM + P].bitcast(U32).unsqueeze(1).broadcast_to([P, NT, P]),
                                  hbank[h % 2][:, :].rearrange("p (c t) -> p c t", c=NT)).then_inc(masked, 1)

            def softmax_max(l, u):
                a, n, j = 8 * l + u, u // 2, u % 2
                w = 256 if n else 128
                mk = const[:, K_AM + 256 - w:K_AM + 256].unsqueeze(1).broadcast_to([P, 2, w])
                dve.wait_ge(qk_done, a + 1)
                if u:
                    dve.wait_ge(pt_done, a)
                for o in range(2):
                    chain(V.scalar_tensor_tensor(out=pm[:, o:4:2, 0:w], in0=small[o][:, 0:2 * w].rearrange("p (h k) -> p h k", h=2),
                                                 scalar=AT_SCALE, in1=mk, op0=ALU.mult, op1=ALU.add))
                sync()
                chain(V.tensor_reduce(amx[:, 0, :], pm[:, :, 0:w], AX_X, ALU.max))
                sync()
                sk = rows[:, R_SINK + 4 * j:R_SINK + 4 * j + 4]
                chain(V.tensor_tensor(amx[:, 0, :], amx[:, 0, :], sk, ALU.max))
                sync()
                chain(V.tensor_scalar(amx[:, 1, :], amx[:, 0, :], -1.0, None, ALU.mult))
                V.tensor_tensor(amx[:, 2, :], sk, amx[:, 0, :], ALU.subtract).then_inc(max_ready, 1)

            def softmax_norm(l, u):
                a = 8 * l + u
                w = 256 if u // 2 else 128
                dve.wait_ge(p_exp, a + 1)
                chain(V.tensor_tensor(ars[:, 2, :], ars[:, 0, :], ars[:, 1, :], ALU.add))
                sync()
                chain(V.reciprocal(ars[:, 2, :], ars[:, 2, :]))
                sync()
                V.tensor_tensor(pm[:, :, 0:w], pm[:, :, 0:w], ars[:, 2, :].unsqueeze(2).broadcast_to([P, 4, w]),
                                ALU.mult).then_inc(p_ready, 1)

            def convolve(l, p, j):
                t = tile(l, "w1", 2 * p + j)
                c0 = C_CONV + 8 * p + 4 * j
                a, T = acc[t % 4], tmp[2 * (p % 2) + j]
                dve.wait_ge(conv0, 2 * (NPAIR * l + p) + j + 1)
                chain(V.scalar_tensor_tensor(out=T[:, 1:S], in0=a[:, 0:S - 1], scalar=cols[:, l, c0 + 1:c0 + 2],
                                             in1=T[:, 1:S], op0=ALU.mult, op1=ALU.add))
                sync()
                free(t, V.scalar_tensor_tensor(out=T[:, 2:S], in0=a[:, 0:S - 2], scalar=cols[:, l, c0:c0 + 1],
                                               in1=T[:, 2:S], op0=ALU.mult, op1=ALU.add))

            def attended_low(l, u):
                dve.wait_ge(ybh_ready, 8 * l + u + 1)
                v = slice(P * (u // 2), P * (u // 2) + P)
                jj = slice(2 * (u % 2), 2 * (u % 2) + 2)
                V.tensor_tensor(ybl[:, jj, v], b6[:, 0:256].rearrange("p (t n) -> p t n", t=2),
                                ybh[:, jj, v].bitcast(F32), ALU.subtract).then_inc(yb_ready, 1)

            def merge(l, s, j):
                br, m = s // NMP, 2 * (s % NMP) + j
                t = tile(l, "proj", 2 * s + j)
                gate = gates[:, (2 * s + j) % 4, :]
                evacuated(dve, tile(l, "gate", 2 * s + j))
                dve.wait_ge(tile_done, t + 1)
                if br == 0:
                    free(t, V.tensor_tensor(mg[:, m, :], acc[t % 4][:, :], gate, ALU.mult))
                    return
                T = tmp[2 + j]
                sync()
                free(t, V.tensor_tensor(T[:, :], acc[t % 4][:, :], gate, ALU.mult))
                evacuated(dve, t)
                if br == 1:
                    chain(V.tensor_tensor(mg[:, m, :], mg[:, m, :], T[:, :], ALU.add))
                else:
                    if m >= 2:
                        dve.wait_ge(lo_ready, split(l, "mg", m - 2) + 1)
                    V.tensor_tensor(tmp[j][:, :], mg[:, m, :], T[:, :], ALU.add).then_inc(f_ready, 1)

            dve.wait_ge(const_in, 48)
            lg = [cols[:, l, C_LB:C_LB + HEADS] for l in range(L)]
            chain(V.tensor_tensor(lbt[:, 2, :], lg[0], lg[1], ALU.max))
            sync()
            chain(V.tensor_tensor(lbt[:, 0, :], lg[0], lbt[:, 2, :], ALU.subtract))
            V.tensor_tensor(lbt[:, 1, :], lg[1], lbt[:, 2, :], ALU.subtract).then_inc(lb_a, 1)
            dve.wait_ge(lb_b, 1)
            chain(V.tensor_tensor(lbt[:, 2, :], lbt[:, 0, :], lbt[:, 1, :], ALU.add))
            sync()
            chain(V.reciprocal(lbt[:, 3, :], lbt[:, 2, :]))
            sync()
            chain(V.tensor_tensor(lbt[:, 0, :], lbt[:, 0, :], lbt[:, 3, :], ALU.mult))
            chain(V.tensor_tensor(lbt[:, 1, :], lbt[:, 1, :], lbt[:, 3, :], ALU.mult))
            sync()
            chain(V.tensor_tensor(lbt[:, 2, :], lbt[:, 0, :], lbt[:, 1, :], ALU.add))
            chain(V.tensor_tensor(lbs[:, 0, 0, :], lbt[:, 0, :], lbt[:, 0, :], ALU.subtract))
            sync()
            chain(V.tensor_tensor(lbs[:, 1, 0, :], lbt[:, 2, :], lbt[:, 0, :], ALU.subtract))
            sync()
            chain(V.tensor_scalar(lbs[:, :, 1, :], lbs[:, :, 0, :], -1.0, 1.0, ALU.mult, ALU.add))
            dve.wait_ge(pos_in, 16)
            chain(V.tensor_copy(tmp[2][:, :], tmp[3][:, :].bitcast(I32)))
            sync()
            chain(V.tensor_scalar(tmp[2][:, :], tmp[2][:, :], const[:, K_INV:K_INV + 1], None, ALU.mult))
            sync()
            for dst, turn in ((0, 0.25), (1, 0.0)):
                r = tmp[dst][:, :]
                chain(V.tensor_scalar(tmp[3][:, :], tmp[2][:, :], 1.0 / TWO_PI, turn, ALU.mult, ALU.add))
                sync()
                chain(V.tensor_scalar(tmp[3][:, :], tmp[3][:, :], MAGIC, None, ALU.add))
                sync()
                chain(V.tensor_scalar(tmp[3][:, :], tmp[3][:, :], -MAGIC, None, ALU.add))
                sync()
                chain(V.scalar_tensor_tensor(out=r, in0=tmp[3][:, :], scalar=-TWO_PI_HI, in1=tmp[2][:, :], op0=ALU.mult, op1=ALU.add))
                sync()
                chain(V.scalar_tensor_tensor(out=r, in0=tmp[3][:, :], scalar=-TWO_PI_LO, in1=r, op0=ALU.mult, op1=ALU.add))
                sync()
                if turn:
                    chain(V.tensor_scalar(r, r, TWO_PI / 4, PI_SAFE, ALU.add, ALU.min))
                    sync()
                    chain(V.tensor_scalar(r, r, -PI_SAFE, None, ALU.max))
                else:
                    sync()
                    V.tensor_scalar(r, r, PI_SAFE, -PI_SAFE, ALU.min, ALU.max).then_inc(ang_ready, 1)
            dve.wait_ge(trig_ready, 2)
            chain(V.tensor_scalar(sinb[:, :], sinb[:, :], const[:, K_SGN:K_SGN + 1], None, ALU.mult))
            for i, c in enumerate(DVE_COLS):
                if i in (0, 4):
                    dve.wait_ge(ada0_in[c // 4], 16)
                w = ada0[:, c, :].rearrange("p (k n) -> p k n", k=KD)
                chain(V.tensor_tensor(w, w, cact[:, :].unsqueeze(2).broadcast_to([P, KD, P]), ALU.mult))
                sync()
                V.tensor_reduce(ada0_sum[:, i, :], w.rearrange("p k n -> p n k"), AX_X, ALU.add).then_inc(ada0_summed, 1)
            for l in range(L):
                pre_norm(l, 0)
                chain(V.memset(asb[:, :], 0.0))
                evacuated(dve, tile(l, "hf", 3))
                evacuated(dve, tile(l, "hq", 3))
                sync()
                for step in range(2 * HEADS):
                    hg_step(l, step)
                    if step >= 2 and step % 2 == 0:
                        hg_states(l, step // 2 - 1)
                    if step == 2 * HEADS - 2:
                        evacuated(dve, tile(l, "gv", 3))
                        for i in range(NT):
                            chain(V.bn_stats(bn[:, i, :], gvt[:, i, :]))
                        sync()
                        for i in range(NT):
                            ins = V.bn_aggr(mv[:, i, :], bn[:, i, :])
                            if i < NT - 1:
                                chain(ins)
                        ins.then_inc(vvar, 1)
                        rotate(tile(l, "kv", 0), [(slice(0, 64), kd[0:64, 0, :]), (slice(64, 128), kd[64:128, 1, :])])
                for i in range(4):
                    t = tile(l, "aq", i)
                    rotate(t, [(slice(0, 128), aqr[:, i, :])], t - 1 if i else tile(l, "kv", 0))
                    if i == 1:
                        hg_states(l, HEADS - 1)
                dve.wait_ge(vsd, l + 1)
                chain(V.reciprocal(vstd[:, 1, :], vstd[:, 0, :]))
                sync()
                for i in range(NT):
                    chain(V.tensor_scalar(gvt[:, i, :], gvt[:, i, :], mv[:, i, 0:1], vstd[:, 1, i:i + 1], ALU.subtract, ALU.mult))
                dve.wait_ge(rows_in, 32 * (l + 1))
                sync()
                for i in range(NT):
                    chain(V.tensor_tensor(gvt[:, i, :], gvt[:, i, :], lnrow[:, 0, :], ALU.mult))
                sync()
                for i in range(NT):
                    V.tensor_tensor(gvt[:, i, :], gvt[:, i, :], lnrow[:, 1, :], ALU.add).then_inc(vn_ready, 1)
                bs = rows[:, R_BS:R_BS + 512].rearrange("p (g t) -> p g t", g=4)
                evacuated(dve, tile(l, "gu", 3))
                dve.wait_ge(o_done, HEADS * (l + 1))
                for g in range(5):
                    if g < 4:
                        dve.wait_ge(sgu_done, 4 * l + g + 1)
                        if g >= 2:
                            dve.wait_ge(lo_ready, split(l, "ya", g - 2) + 1)
                        u = (tmp[2], tmp[3])[g % 2]
                        chain(V.tensor_tensor(u[:, :].rearrange("p (c t) -> p c t", c=NT),
                                              small[g][:, :].rearrange("p (c t) -> p c t", c=NT),
                                              bs[:, g:g + 1, :].broadcast_to([P, NT, P]), ALU.add))
                        sync()
                        V.tensor_tensor(u[:, :], u[:, :], gut[:, g, :], ALU.mult).then_inc(f_ready, 1)
                    if g:
                        if g == 1:
                            dve.wait_ge(sgu_done, 4 * l + 4)
                        lo(split(l, "ya", g - 1), yal[:, g - 1, :], tmp[2 + (g - 1) % 2][:, :], yah[:, g - 1, :])
                evacuated(dve, tile(l, "oss", 0))
                chain(V.reciprocal(rstd[:, :], std[:, :]))
                sync()
                V.tensor_tensor(odg[:, :, :], ident.unsqueeze(1).broadcast_to([P, 16, P]),
                                rstd[:, :].unsqueeze(2).broadcast_to([P, 16, P]), ALU.mult).then_inc(odiag, 1)
                ada_units(l, ("gate", 0))
                dve.wait_ge(lo_ready, split(l, "ya", 3) + 1)
                evacuated(dve, tile(l, "hg", 3))
                dve.wait_ge(obc, HEADS * (l + 1))
                for h in range(HEADS + 1):
                    if h < HEADS:
                        t2 = tmp[2 + h % 2]
                        chain(V.scalar_tensor_tensor(out=t2[:, :], in0=bb[:, h, :], scalar=cols[:, l, C_GN:C_GN + 1],
                                                     in1=small[h][:, :], op0=ALU.mult, op1=ALU.mult))
                        if h >= 2:
                            dve.wait_ge(lo_ready, split(l, "yc", h - 2) + 1)
                        sync()
                        V.tensor_tensor(tmp[h % 2][:, :], t2[:, :], hgs[:, h, :], ALU.mult).then_inc(f_ready, 1)
                    if h:
                        lo(split(l, "yc", h - 1), ycl[:, h - 1, :], tmp[(h - 1) % 2][:, :], ych[:, h - 1, :])
                dve.wait_ge(lo_ready, split(l, "yc", 3) + 1)
                for s in range(NSTEP):
                    br, mp = s // NMP, s % NMP
                    u = s - 1
                    if 0 <= u < 8:
                        softmax_max(l, u)
                    if s:
                        ada_units(l, ("gate", 2 * s))
                    if 0 <= u < 8:
                        softmax_norm(l, u)
                    if s >= 2 and s % 2 == 0:
                        take_ada(l, s // 2 - 1)
                    if u != 7:
                        ada_units(l, ("gate", 2 * s + 1))
                    if 0 <= u < 8:
                        dve.wait_ge(pt_done, 8 * l + u + 1)
                        V.tensor_copy(pts[:, 1, :, :], b7[:, :].rearrange("p (t n) -> p t n", t=4)).then_inc(pt_copied_v, 1)
                    if u == 7:
                        ada_units(l, ("gate", 2 * s + 1))
                        attended_low(l, u)
                    for j in range(2):
                        merge(l, s, j)
                    if 0 <= u < 7:
                        attended_low(l, u)
                    if br == 2:
                        for m in (2 * mp, 2 * mp + 1):
                            lo(split(l, "mg", m), mgl[:, m, :], tmp[m % 2][:, :], mgh[:, m, :])
                for m in range(KD):
                    take_y(l, "wout", m)
                    if m == 0:
                        take_ada(l, 5)
                post_norm(l, 0)
                pre_norm(l, 1)
                for p in range(NPAIR + 1):
                    T = tmp[2 * ((p - 1) % 2)]
                    if p:
                        dve.wait_ge(silu_done, NPAIR * l + p)
                        V.tensor_tensor(T[:, :], T[:, :], tmp[2 * ((p - 1) % 2) + 1][:, :], ALU.mult).then_inc(f_ready, 1)
                    if p < NPAIR:
                        ada_units(l, ("w1", 2 * p))
                        convolve(l, p, 0)
                    if p:
                        lo(split(l, "ff", p - 1), actl[:, p - 1, :], T[:, :], acth[:, p - 1, :])
                    if p < NPAIR:
                        ada_units(l, ("w1", 2 * p + 1))
                        convolve(l, p, 1)
                    if p in ADA_PAIR and ADA_PAIR[p] < ada_tiles(l):
                        take_ada(l, ADA_PAIR[p])
                for m in range(KD):
                    take_y(l, "w2", m)
                post_norm(l, 1)

        @block.tensor
        def _(pe):
            MM = nc.tensor.matmul

            def sums_of_squares(n, k):
                pe.wait_ge(sq_ready, 8 * n + k + 1)
                MM(b7[:, :], ones, sqring[k % 4][:, :], start=(k == 0), stop=(k == KD - 1)).then_inc(ss_done, 1)

            def column_sums(n):
                pe.wait_ge(lo_ready, split(n // 4, "h1" if n % 4 == 1 else "h2", 7) + 1)
                pe.wait_ge(sq_added, (KD - 1) * (n // 2 + 1))
                for c in range(NT):
                    ins = MM(b6[:, c:c + 1], sqsum[:, P * c:P * c + P], ones[:, 0:1], start=True, stop=True)
                ins.then_inc(ss_cols, 1)

            def broadcast(n):
                pe.wait_ge(diag_ready, n + 1)
                MM(b6[:, :], ones, tmp[3][:, :], start=True, stop=True).then_inc(bc_ready, 1)

            def keep_clock(n):
                for _ in range(n):
                    MM(b5[:, :], ones, const[:, 0:S], start=True, stop=True)

            def weights_of(l, b):
                s = NBLOCK * l + BLOCK_AT[b]
                pe.wait_ge(whi_ready, s + 1)
                return s % RING, s + 1

            def acquire(t):
                if t >= 4:
                    pe.wait_ge(acc_free[t % 4], t // 4)
                return acc[t % 4]

            def three(out, s, views, xh, xl, first=True, last=True, hi_wait=None, lo_wait=None):
                slot, ready = s
                n = len(xh)
                for k in range(n):
                    if hi_wait:
                        hi_wait(k)
                    MM(out, views(whi, slot, k), xh[k], start=(first and k == 0), stop=False, skip_group_check=True)
                pe.wait_ge(wlo_ready, ready)
                for k in range(n):
                    MM(out, views(wlo, slot, k), xh[k], start=False, stop=False, skip_group_check=True)
                for k in range(n):
                    if lo_wait:
                        lo_wait(k)
                    ins = MM(out, views(whi, slot, k), xl[k], start=False, stop=(last and k == n - 1), skip_group_check=True)
                return ins

            def whole(w, slot, k):
                return w[:, slot, P * k:P * k + P]

            def feature_tile(l, b, t, xh, xl, **kw):
                out = acquire(t)
                three(out[:, :], weights_of(l, b), whole, [xh[:, k, :] for k in range(KD)], [xl[:, k, :] for k in range(KD)],
                      **kw).then_inc(tile_done, 1)

            def first_tiles(l, names, norm):
                outs, slots = [], []
                for b in names:
                    outs.append(acquire(tile(l, *b))[:, :])
                    slots.append(weights_of(l, b))
                for k in range(KD):
                    pe.wait_ge(hi_ready, split(l, norm, k) + 1)
                    for out, (slot, ready) in zip(outs, slots):
                        MM(out, whole(whi, slot, k), hh[:, k, :], start=(k == 0), stop=False, skip_group_check=True)
                        if k == 0:
                            pe.wait_ge(wlo_ready, ready)
                        MM(out, whole(wlo, slot, k), hh[:, k, :], start=False, stop=False, skip_group_check=True)
                for k in range(KD):
                    pe.wait_ge(lo_ready, split(l, norm, k) + 1)
                    for out, (slot, _) in zip(outs, slots):
                        ins = MM(out, whole(whi, slot, k), hl[:, k, :], start=False, stop=(k == KD - 1), skip_group_check=True)
                        if k == KD - 1:
                            ins.then_inc(tile_done, 1)

            def token_half(l, name, i):
                slot, ready = weights_of(l, (name, i))
                pe.wait_ge(wlo_ready, ready)
                k0 = 4 * (i % 2)
                for j in range(2):
                    t = tile(l, name, 2 * (i // 2) + j)
                    out = acquire(t) if i % 2 == 0 else acc[t % 4]
                    for u in range(2):
                        v = slice(P * (2 * j + u), P * (2 * j + u) + P)
                        o = out[:, 256 * u:256 * u + 256]
                        for k in range(4):
                            wh = whi[:, slot, 256 * k:256 * k + 256]
                            wl = wlo[:, slot, 256 * k:256 * k + 256]
                            MM(o, hh[:, k0 + k, v], wh, start=(i % 2 == 0 and u == 0 and k == 0), stop=False, skip_group_check=True)
                            MM(o, hh[:, k0 + k, v], wl, start=False, stop=False, skip_group_check=True)
                            ins = MM(o, hl[:, k0 + k, v], wh, start=False, stop=(i % 2 == 1 and k == 3), skip_group_check=True)
                    if i % 2:
                        ins.then_inc(tile_done, 1)
                if i % 2 == 0:
                    ins.then_inc(part_used, 1)

            def values(l):
                t = tile(l, "kv", 1)
                out = acquire(t)
                slot, ready = weights_of(l, ("kv", 1))
                pe.wait_ge(wlo_ready, ready)
                for u in range(NT):
                    v = slice(P * u, P * u + P)
                    for k in range(KD):
                        wh, wl = whole(whi, slot, k), whole(wlo, slot, k)
                        MM(out[:, v], hh[:, k, v], wh, start=(k == 0), stop=False, skip_group_check=True)
                        MM(out[:, v], hh[:, k, v], wl, start=False, stop=False, skip_group_check=True)
                        ins = MM(out[:, v], hl[:, k, v], wh, start=False, stop=(k == KD - 1), skip_group_check=True)
                ins.then_inc(tile_done, 1)

            def hg_step(l, step):
                h, half = step // 2, step % 2
                q = HEADS * l + h
                hv = slice(P * h, P * h + P)
                t0, t1, t2 = hgset[h % 2]
                if half == 0:
                    pe.wait_ge(qk_ready, q + 1)
                    if h:
                        pe.wait_ge(state_ready, q)
                    for c in range(NT):
                        ins = nc.tensor.transpose(b6[:, P * c:P * c + P], t2[:, P * c:P * c + P], ident)
                    ins.then_inc(khT_done, 1)
                    if h >= 2:
                        pe.wait_ge(o_copied, q - 1)
                    zero = const[0:CH, K_HM + CH:K_HM + CH + 1].broadcast_to([CH, S])
                    MM(hbank[h % 2][:, :], ones[0:CH, :], zero, start=True, stop=True, skip_group_check=True)
                else:
                    if h:
                        hg_out(l, h - 1)
                    else:
                        evacuated(pe, tile(l, "hi", 2))
                        evacuated(pe, tile(l, "hi", 3))
                    pe.wait_ge(khT_copied, q + 1)
                    for c in range(NCH - 1):
                        r = slice(CH * (c % 2), CH * (c % 2) + CH)
                        o = (b6 if c % 2 else b7)[:, P * (c // 2):P * (c // 2) + P]
                        ins = MM(o, khT[r, c // 2, :], itok[r, c // 2, hv], start=True, stop=True)
                    ins.then_inc(ds_done, 1)
                for i in range(4 * half, 4 * half + 4):
                    pe.wait_ge(kt_ready, NSUB * q + i + 1)
                    n = SUB * (i + 1)
                    for c in range(NCH):
                        v = slice(CH * c + SUB * i, CH * c + SUB * i + SUB)
                        r = CH * (c % 2)
                        ins = MM(hbank[h % 2][r:r + n, v], kt[:, i % KTS, c, 0:n], t0[:, v], start=False, stop=True,
                                 skip_group_check=True)
                    ins.then_inc(a_done, 1)

            def hg_out(l, h):
                q = HEADS * l + h
                hv = slice(P * h, P * h + P)
                pe.wait_ge(state_ready, q + 1)
                pe.wait_ge(masked, q + 1)
                o = hbank[h % 2]
                for r in range(NT):
                    MM(o[:, P * r:P * r + P], itok[:, r, hv], asb[:, P * r:P * r + P], start=True, stop=False,
                       skip_group_check=True)
                    for c in (2 * r, 2 * r + 1):
                        if c:
                            ins = MM(o[:, CH * c:CH * c + CH], states[:, c - 1, :], hgset[h % 2][1][:, CH * c:CH * c + CH],
                                     start=False, stop=True, skip_group_check=True)
                ins.then_inc(o_done, 1)

            def scores(l, u):
                a, n, j = 8 * l + u, u // 2, u % 2
                w = 256 if n else 128
                if u:
                    pe.wait_ge(max_ready, a)
                for i in range(4):
                    h = 4 * j + i
                    r = slice(64 * (h % 2), 64 * (h % 2) + 64)
                    ins = MM(small[i % 2][:, w * (i // 2):w * (i // 2) + w], aqr[r, h // 2, P * n:P * n + P],
                             kd[r, j, P * (n + 1) - w:P * (n + 1)], start=True, stop=True)
                ins.then_inc(qk_done, 1)

            def turn(l, u):
                a, n = 8 * l + u, u // 2
                pe.wait_ge(p_ready, a + 1)
                if u:
                    pe.wait_ge(yb_ready, a)
                for half in range(0 if n else 1, 2):
                    o = 128 * half if n else 0
                    for i in range(4):
                        ins = nc.tensor.transpose((b7 if half else b6)[:, P * i:P * i + P], pm[:, i, o:o + P], ident)
                ins.then_inc(pt_done, 1)

            def attend(l, u):
                a, n, j = 8 * l + u, u // 2, u % 2
                if n:
                    pe.wait_ge(pt_copied_a, 6 * l + u - 1)
                pe.wait_ge(pt_copied_v, a + 1)
                for i in range(4):
                    o = b6[64 * (i % 2):64 * (i % 2) + 64, P * (i // 2):P * (i // 2) + P]
                    for half in range(0 if n else 1, 2):
                        ins = MM(o, vt[:, n - 1 + half, 64 * j:64 * j + 64], pts[:, half, i, :],
                                 start=(half == 0 or not n), stop=(half == 1), skip_group_check=True)
                ins.then_inc(pv_done, 1)

            done_adas = [0]

            def ada_tile(l, i):
                t = tile(l, "ada", i)
                out = acquire(t)
                done_adas[0] += 4
                pe.wait_ge(ada_used, done_adas[0])
                for c in range(4):
                    ins = MM(out[:, c:c + 1], ada_sum[:, (done_adas[0] - 4 + c) % 8, :], ones[:, 0:1], start=True, stop=True)
                ins.then_inc(tile_done, 1)

            pe.wait_ge(const_in, 48)
            pe.wait_ge(cact_ready, 1)
            def first_rows(g):
                a, b = ROW_SPANS[g]
                pe.wait_ge(ada0_in[a // 4], 16)
                for k in range(KD):
                    ins = MM(rowbank[g][0:1, 0:P * (b - a)], cact[:, k:k + 1], ada0[:, a:b, P * k:P * k + P],
                             start=(k == 0), stop=(k == KD - 1))
                ins.then_inc(ada0_rows, 1)

            def first_columns(g):
                pe.wait_ge(ada0_copied, g + 1)
                a, b = ROW_SPANS[g]
                for c in range(a, b):
                    MM(b5[:, c:c + 1], ada0_row[0:1, g, P * (c - a):P * (c - a) + P], ones[0:1, 0:1], start=True, stop=True)

            first_rows(0)
            first_rows(1)
            first_columns(0)
            for k in range(KD):
                sums_of_squares(0, k)
            first_rows(2)
            first_columns(1)
            for i, c in enumerate(DVE_COLS):
                if i == 4:
                    first_columns(2)
                pe.wait_ge(ada0_summed, i + 1)
                ins = MM(b5[:, c:c + 1], ada0_sum[:, i, :], ones[:, 0:1], start=True, stop=True)
            ins.then_inc(ada0_done, 1)

            for l in range(L):
                if l:
                    keep_clock(3)
                    for k in range(KD):
                        sums_of_squares(4 * l, k)
                    keep_clock(3)
                broadcast(4 * l)
                keep_clock(2)
                first_tiles(l, [("hf", 0), ("hf", 1)], "h1")
                for b in BLOCKS[2:NFRONT]:
                    name, i = b
                    if name in ("hi", "gv"):
                        token_half(l, name, i)
                    elif b == ("kv", 1):
                        values(l)
                    else:
                        feature_tile(l, b, tile(l, name, i), hh, hl)
                    if b in HG_BLOCKS:
                        i = HG_BLOCKS.index(b)
                        if i >= 2 and i % 2 == 0 and i // 2 - 1 < 2 * HEADS:
                            hg_step(l, i // 2 - 1)
                hg_out(l, HEADS - 1)
                pe.wait_ge(vn_ready, NT * (l + 1))
                pe.wait_ge(ws_ready, l + 1)
                for g in range(4):
                    if g < 2:
                        pe.wait_ge(o_copied, HEADS * (l + 1) - (g == 0))
                    for c in range(NT):
                        ins = MM(small[g][:, P * c:P * c + P], gvt[:, c, P * g:P * g + P], ws[:, g, :], start=True, stop=True)
                    ins.then_inc(sgu_done, 1)
                t = tile(l, "oss", 0)
                out = acquire(t)
                for h in range(HEADS):
                    pe.wait_ge(osq_ready, HEADS * l + h + 1)
                    for c in range(NT):
                        ins = MM(out[:, 4 * h + c:4 * h + c + 1], osq[h][:, P * c:P * c + P], ones[:, 0:1],
                                 start=True, stop=True)
                ins.then_inc(tile_done, 1)
                for s in range(NSTEP):
                    br, mp = s // NMP, s % NMP
                    u = s - 1
                    feature_tile(l, ("gate", 2 * s), tile(l, "gate", 2 * s), hh, hl)
                    if s == 0:
                        pe.wait_ge(odiag, l + 1)
                        for h in range(HEADS):
                            MM(small[h][:, :], ones, odg[:, 4 * h:4 * h + 4, :], start=True, stop=True).then_inc(obc, 1)
                    if s >= 2 and s % 2 == 0:
                        ada_tile(l, s // 2 - 1)
                    if u == 7:
                        turn(l, u)
                    feature_tile(l, ("gate", 2 * s + 1), tile(l, "gate", 2 * s + 1), hh, hl)
                    if u == 7:
                        attend(l, u)
                    elif 0 <= u < 7:
                        turn(l, u)
                    if mp == 0:
                        if br == 0:
                            pe.wait_ge(lo_ready, split(l, "ya", 3) + 1)
                        elif br == 1:
                            pe.wait_ge(lo_ready, split(l, "yc", 3) + 1)
                        else:
                            pe.wait_ge(yb_ready, 8 * (l + 1))
                    yh, yl = ((yah, yal), (ych, ycl), (ybh, ybl))[br]
                    w = weights_of(l, ("proj", s))
                    for j in range(2):
                        t = tile(l, "proj", 2 * s + j)
                        out = acquire(t)
                        three(out[:, :], w, lambda wt, slot, k: wt[:, slot, 256 * k + P * j:256 * k + P * j + P],
                              [yh[:, k, :] for k in range(4)], [yl[:, k, :] for k in range(4)]).then_inc(tile_done, 1)
                        if j == 0 and 0 <= u < 7:
                            attend(l, u)
                    if s == 0:
                        evacuated(pe, tile(l, "aq", 3))
                        pe.wait_ge(kd_ready, 2 * (l + 1))
                        evacuated(pe, tile(l, "kv", 1))
                        pe.wait_ge(f_ready, split(l, "yc", 3) + 1)
                    if s < 8:
                        scores(l, s)
                for m in range(KD):
                    kw = {} if m else {"hi_wait": lambda k: pe.wait_ge(hi_ready, split(l, "mg", k) + 1),
                                       "lo_wait": lambda k: pe.wait_ge(lo_ready, split(l, "mg", k) + 1)}
                    feature_tile(l, ("wout", m), tile(l, "wout", m), mgh, mgl, **kw)
                    if m == 0:
                        ada_tile(l, 5)
                column_sums(4 * l + 1)
                keep_clock(1)
                broadcast(4 * l + 1)
                keep_clock(3)
                for k in range(KD):
                    sums_of_squares(4 * l + 2, k)
                keep_clock(3)
                broadcast(4 * l + 2)
                keep_clock(2)
                first_tiles(l, [("w1", 0), ("w1", 1)], "h2")
                for p in range(NPAIR):
                    for j in range(2):
                        if p:
                            feature_tile(l, ("w1", 2 * p + j), tile(l, "w1", 2 * p + j), hh, hl)
                    if p in ADA_PAIR and ADA_PAIR[p] < ada_tiles(l):
                        ada_tile(l, ADA_PAIR[p])
                for m in range(KD):
                    t = tile(l, "w2", m)
                    out = acquire(t)
                    for third in range(3):
                        k0 = 8 * third
                        nk = min(8, NPAIR - k0)
                        if m == 0:
                            pe.wait_ge(lo_ready, split(l, "ff", k0 + nk - 1) + 1)
                        ins = three(out[:, :], weights_of(l, ("w2", 3 * m + third)), whole,
                                    [acth[:, k0 + k, :] for k in range(nk)], [actl[:, k0 + k, :] for k in range(nk)],
                                    first=third == 0, last=third == 2)
                        ins.then_inc(tile_done if third == 2 else part_used, 1)
                column_sums(4 * l + 3)
                broadcast(4 * l + 3)


def kernel(**inputs):
    import numpy as np
    import concourse.bacc as bacc
    from concourse.bass_utils import run_bass_kernel_spmd

    a = {k: np.asarray(v) for k, v in inputs.items()}

    def blocks(w, width):
        l, k, n = w.shape
        w = w.reshape(l, k // P, P, n // width, width).transpose(0, 3, 2, 1, 4)
        return np.ascontiguousarray(w).reshape(l, n // width, P, k // P * width)

    def columns(v):
        v = v.reshape(v.shape[:-1] + (v.shape[-1] // P, P))
        return np.moveaxis(v, -1, 0)

    w_in = a["w_in"]
    gu, gv, aq, kv, hq, hf, hi, hg = (w_in[:, :, s:e] for s, e in (
        (0, 512), (512, 1024), (1024, 1536), (1536, 1792), (1792, 2304), (2304, 2816), (2816, 3328), (3328, 3840)))
    g = w_in[:, :, 3840:].reshape(L, D, 3, D)[:, :, (0, 2, 1)].reshape(L, D, 3 * D)
    def token_blocks(w):
        w = w.reshape(L, 2, 4, P, 2, 256).transpose(0, 4, 1, 3, 2, 5)
        return np.ascontiguousarray(w).reshape(L, 4, P, BLK)

    parts = [blocks(hf, P), blocks(hq, P), token_blocks(hi), blocks(hg, P), token_blocks(gv), blocks(kv, P),
             blocks(aq, P), blocks(gu, P), blocks(g, P)]
    win = np.concatenate(parts, axis=1)
    proj = np.concatenate([blocks(a[n], 256) for n in ("proj_a", "proj_c", "proj_b")], axis=1)
    w1 = a["ffn_w1"].reshape(L, D, 2, NPAIR, P).transpose(0, 1, 3, 2, 4).reshape(L, D, 2 * FF)

    conv = np.concatenate([a["ffn_conv_w"], a["ffn_conv_b"][:, None, :]], axis=1)
    conv = conv.reshape(L, 4, 2, NPAIR, P).transpose(4, 0, 3, 2, 1).reshape(P, L, NPAIR * 8)
    cols = np.concatenate([columns(a[n]) for n in ("ada_b", "norm_mix_pre", "norm_mix_post", "norm_ffn_pre",
                                                   "norm_ffn_post", "hg_lb_logits", "hg_gnorm")] + [conv], axis=2)
    rows = np.concatenate([a["gm_bs"].reshape(L, 512), a["attn_sinks"]], axis=1)
    ln_rows = np.concatenate([a["gm_ln_g"], a["gm_ln_b"]], axis=1)

    const = np.zeros((P, NCONST), np.float32)
    i = np.arange(P)
    const[:, K_ID:K_ID + P] = np.eye(P)
    const[:, K_ONE:K_ONE + P] = 1.0
    delta = i[:, None] + P - np.arange(256)[None, :]
    const[:, K_AM:K_AM + 256] = np.where((delta >= 0) & (delta < 128), 0.0, -1e30)
    const[:, K_HM:K_HM + P] = (i[:, None] // CH == i[None, :] // CH) & (i[:, None] <= i[None, :])
    const[:, K_INV] = np.float32(10000.0) ** (-(i % 32).astype(np.float32) / np.float32(32))
    const[:, K_SGN] = np.where(i // 32 % 2 == 0, -1.0, 1.0)
    const[:, K_EPS] = EPS

    arrays = {
        "xT": np.ascontiguousarray(a["x"][0].reshape(S, KD, P).transpose(2, 1, 0)),
        "c": np.ascontiguousarray(a["c"][0].reshape(KD, P).T),
        "pos": np.ascontiguousarray(a["positions"][0]),
        "cols": np.ascontiguousarray(cols),
        "rows": np.ascontiguousarray(rows),
        "ln_rows": np.ascontiguousarray(ln_rows),
        "const": const,
        "ws": np.ascontiguousarray(a["gm_ws"].transpose(0, 3, 1, 2)),
        "ada": blocks(a["ada_w"], P),
        "win": win,
        "proj": proj,
        "wout": blocks(a["w_out"], P),
        "w1": blocks(w1, P),
        "w2": blocks(a["ffn_w2"], P),
    }
    nc = bacc.Bacc("TRN2", target_bir_lowering=False, num_devices=1)
    args = [nc.dram_tensor(n, v.shape, mybir.dt.from_np(v.dtype), kind="ExternalInput").ap() for n, v in arrays.items()]
    out = nc.dram_tensor("out", (P, KD, S), F32, kind="ExternalOutput").ap()
    trunk(nc, *args, out)
    r = run_bass_kernel_spmd(nc, [arrays], core_ids=[0])
    got = r.results[0]["out"]
    return np.ascontiguousarray(got.transpose(2, 1, 0)).reshape(1, S, D)
```
